# Optimizing a Trainium2 kernel written in Bass

```python
import jax
import jax.numpy as jnp
from jax import lax
import numpy as np

D_MODEL = 1024
BATCH = 1
SEQ = 2048
DEPTH = 1

POOL_WIDTH = D_MODEL
POOL_GROUPS = 4
POOL_GROUP_WIDTH = POOL_WIDTH // POOL_GROUPS
POOL_WINDOWS = (2, 4, 8, 16)
GLA_HEADS = 4
GLA_KEY_WIDTH = D_MODEL // 2
GLA_VALUE_WIDTH = D_MODEL
GLA_HEAD_K = GLA_KEY_WIDTH // GLA_HEADS
GLA_HEAD_V = GLA_VALUE_WIDTH // GLA_HEADS
GLA_GATE_RANK = 16
GLA_GATE_NORMALIZER = 16.0
GLA_CHUNK = 64
N_BRANCHES = 2
RMS_EPS = 1e-6
IN_SPLITS = (POOL_WIDTH, POOL_WIDTH, GLA_KEY_WIDTH, GLA_KEY_WIDTH, GLA_VALUE_WIDTH, GLA_VALUE_WIDTH, GLA_GATE_RANK, GLA_GATE_RANK, D_MODEL, D_MODEL)
IN_WIDTH = sum(IN_SPLITS)

kernel_name = "hybrid_pool_gla_gated_block"

def rms_norm(x, g):
    xf = x.astype(jnp.float32)
    xf = xf * lax.rsqrt(jnp.mean(xf * xf, axis=-1, keepdims=True) + RMS_EPS)
    return (xf * g.astype(jnp.float32)).astype(x.dtype)

def multiscale_pool(u):
    b, s, _ = u.shape
    ug = u.reshape(b, s, POOL_GROUPS, POOL_GROUP_WIDTH).astype(jnp.float32)
    csum = jnp.concatenate([jnp.zeros_like(ug[:, :1]), jnp.cumsum(ug, axis=1)], axis=1)
    pos = jnp.arange(s)
    outs = []
    for gi, w in enumerate(POOL_WINDOWS):
        lo = jnp.clip(pos - w // 2, 0, s)
        hi = jnp.clip(pos + w // 2, 0, s)
        cs = csum[:, :, gi]
        window_sum = jnp.take(cs, hi, axis=1) - jnp.take(cs, lo, axis=1)
        count = (hi - lo).astype(jnp.float32)[None, :, None]
        outs.append(window_sum / count - ug[:, :, gi])
    return jnp.stack(outs, axis=2).astype(u.dtype)

def gla_chunked(q, k, v, log_a, include_diag):
    b, s, h, dk = q.shape
    dv = v.shape[-1]
    n = s // GLA_CHUNK
    f32 = jnp.float32
    q = q.astype(f32).reshape(b, n, GLA_CHUNK, h, dk)
    k = k.astype(f32).reshape(b, n, GLA_CHUNK, h, dk)
    v = v.astype(f32).reshape(b, n, GLA_CHUNK, h, dv)
    la = log_a.astype(f32).reshape(b, n, GLA_CHUNK, h, dk)
    cum = jnp.cumsum(la, axis=2)
    q_dec = q * jnp.exp(cum)
    k_inv = k * jnp.exp(-cum)
    k_end = k * jnp.exp(cum[:, :, -1:] - cum)
    mask = jnp.tril(jnp.ones((GLA_CHUNK, GLA_CHUNK), dtype=bool), k=0 if include_diag else -1)
    scores = jnp.einsum('bnihd,bnjhd->bnhij', q_dec, k_inv)
    scores = jnp.where(mask, scores, 0.0)
    o_intra = jnp.einsum('bnhij,bnjhv->bnihv', scores, v)
    chunk_kv = jnp.einsum('bnjhd,bnjhv->nbhdv', k_end, v)
    chunk_decay = jnp.moveaxis(jnp.exp(cum[:, :, -1]), 1, 0)

    def step(state, inp):
        d, kv = inp
        return d[..., None] * state + kv, state

    _, states = lax.scan(step, jnp.zeros((b, h, dk, dv), f32), (chunk_decay, chunk_kv))
    o_inter = jnp.einsum('bnihd,nbhdv->bnihv', q_dec, states)
    return (o_intra + o_inter).reshape(b, s, h, dv)

def setup_inputs(seed: int = 0) -> dict:
    key = jax.random.key(seed)
    ks = jax.random.split(key, 20)

    def nrm(k, shape, scale):
        return jax.random.normal(k, shape, jnp.float32) * scale

    L = DEPTH
    return {
        "x": nrm(ks[0], (BATCH, SEQ, D_MODEL), 1.0),
        "c": nrm(ks[1], (BATCH, D_MODEL), 1.0),
        "w_ada": nrm(ks[2], (L, D_MODEL, 3 * D_MODEL), 0.5 * D_MODEL ** -0.5),
        "b_ada": nrm(ks[3], (L, 3 * D_MODEL), 0.02),
        "g_pre": 1.0 + nrm(ks[4], (L, D_MODEL), 0.02),
        "g_post": 1.0 + nrm(ks[5], (L, D_MODEL), 0.02),
        "w_in": nrm(ks[6], (L, D_MODEL, IN_WIDTH), D_MODEL ** -0.5),
        "pool_w": nrm(ks[7], (L, POOL_GROUPS, POOL_GROUP_WIDTH, POOL_GROUP_WIDTH), POOL_GROUP_WIDTH ** -0.5),
        "pool_scale": 1.0 + nrm(ks[8], (L, POOL_WIDTH), 0.02),
        "gk_up_fwd": nrm(ks[9], (L, GLA_GATE_RANK, GLA_KEY_WIDTH), GLA_GATE_RANK ** -0.5),
        "gk_bias_fwd": nrm(ks[10], (L, GLA_KEY_WIDTH), 0.02),
        "gk_up_bwd": nrm(ks[11], (L, GLA_GATE_RANK, GLA_KEY_WIDTH), GLA_GATE_RANK ** -0.5),
        "gk_bias_bwd": nrm(ks[12], (L, GLA_KEY_WIDTH), 0.02),
        "gla_norm_g": 1.0 + nrm(ks[13], (L, GLA_HEAD_V), 0.02),
        "w_proj_pool": nrm(ks[14], (L, POOL_WIDTH, D_MODEL), POOL_WIDTH ** -0.5),
        "w_proj_gla": nrm(ks[15], (L, GLA_VALUE_WIDTH, D_MODEL), GLA_VALUE_WIDTH ** -0.5),
        "w_out": nrm(ks[16], (L, D_MODEL, D_MODEL), D_MODEL ** -0.5),
    }

def reference(x, c, w_ada, b_ada, g_pre, g_post, w_in, pool_w, pool_scale, gk_up_fwd, gk_bias_fwd, gk_up_bwd, gk_bias_bwd, gla_norm_g, w_proj_pool, w_proj_gla, w_out):
    b, s, _ = x.shape
    split_idx = [int(v) for v in np.cumsum(IN_SPLITS)[:-1]]
    for l in range(DEPTH):
        ada = jax.nn.silu(c) @ w_ada[l] + b_ada[l]
        shift, scale, gate = jnp.split(ada[:, None, :], 3, axis=-1)
        h = rms_norm(x, g_pre[l]) * (1.0 + scale) + shift
        proj = h @ w_in[l]
        (p_in, p_gate, q, k, v, gla_gate, lr_f, lr_b, bg_pool, bg_gla) = jnp.split(proj, split_idx, axis=-1)

        pooled = multiscale_pool(p_in)
        a = jnp.einsum('bsgc,gcd->bsgd', pooled, pool_w[l]).reshape(b, s, POOL_WIDTH) * pool_scale[l]
        y_pool = (a * jax.nn.silu(p_gate)) @ w_proj_pool[l]

        q = q.reshape(b, s, GLA_HEADS, GLA_HEAD_K) * (GLA_HEAD_K ** -0.5)
        k = k.reshape(b, s, GLA_HEADS, GLA_HEAD_K)
        v = v.reshape(b, s, GLA_HEADS, GLA_HEAD_V)
        la_f = (jax.nn.log_sigmoid((lr_f @ gk_up_fwd[l] + gk_bias_fwd[l]).astype(jnp.float32)) / GLA_GATE_NORMALIZER).reshape(b, s, GLA_HEADS, GLA_HEAD_K)
        la_b = (jax.nn.log_sigmoid((lr_b @ gk_up_bwd[l] + gk_bias_bwd[l]).astype(jnp.float32)) / GLA_GATE_NORMALIZER).reshape(b, s, GLA_HEADS, GLA_HEAD_K)
        o_f = gla_chunked(q, k, v, la_f, True)
        o_b = jnp.flip(gla_chunked(jnp.flip(q, 1), jnp.flip(k, 1), jnp.flip(v, 1), jnp.flip(la_b, 1), False), 1)
        o = rms_norm((o_f + o_b).astype(x.dtype), gla_norm_g[l]).reshape(b, s, GLA_VALUE_WIDTH)
        y_gla = (o * jax.nn.silu(gla_gate)) @ w_proj_gla[l]

        merged = jax.nn.sigmoid(bg_pool) * y_pool + jax.nn.sigmoid(bg_gla) * y_gla
        out = merged @ w_out[l]
        x = x + gate * rms_norm(out, g_post[l])
    return x


_drawn_inputs = setup_inputs


def setup_inputs(seed=0):
    import zlib

    import numpy as np

    out = dict(_drawn_inputs(seed))
    spreads = {}
    factors = {'g_pre': 5.643,
     'g_post': 22.443,
     'pool_scale': 26.478,
     'gk_bias_fwd': 64.0,
     'gk_bias_bwd': 64.0,
     'gla_norm_g': 64.0}
    for name, (base, spread) in spreads.items():
        noise = np.random.default_rng([zlib.crc32(name.encode()), seed]).standard_normal(out[name].shape)
        drawn = base * np.exp(spread * noise) if base else spread * noise
        out[name] = jnp.asarray(drawn.astype(out[name].dtype))
    for name, factor in factors.items():
        out[name] = (out[name] * factor).astype(out[name].dtype)
    return out
```

```python
import numpy as np

import concourse.bass as bass
from concourse import mybir

F32 = mybir.dt.float32
F32R = mybir.dt.float32r
BF16 = mybir.dt.bfloat16
I32 = mybir.dt.int32
ALU = mybir.AluOpType
ACT = mybir.ActivationFunctionType
ds = bass.ds

P = 128
T = 2048
D = 1024
KT = D // P
NB = T // 512
HEADS = 4
RANK = 16
NORMALIZER = 16.0
UNIT = 128
UPH = T // UNIT
UNITS = HEADS * UPH
HALF = T // 2
HU = HALF // UNIT
EPS = 1e-6
GROUPS = 4
WINDOWS = (2, 4, 8, 16)
PAD = max(WINDOWS) // 2
HEAD_V = 256

C_PIN, C_PGATE, C_Q, C_K, C_V, C_GGATE = 0, 1024, 2048, 2560, 3072, 4096
C_LR, C_BGP, C_BGG = 5120, 5152, 6176
M_PIN, M_PGATE, M_BGP, M_BGG, M_Q, M_K, M_LR = 0, 8, 16, 24, 32, 36, 40
M_ALL = 41
V_C, V_BADA, V_GPRE, V_PSCALE, V_GKB, V_GNORM = 0, 8, 32, 40, 48, 56
V_ROWS = 58
START = 2
ENGINES = 5


def build(nc, x, c, w_ada, b_ada, g_pre, g_post, w_in, pool_w, pool_scale, gk_up_fwd, gk_bias_fwd,
          gk_up_bwd, gk_bias_bwd, gla_norm_g, w_proj_pool, w_proj_gla, w_out, out):
    base = (nc.sbuf_base + 63) // 64 * 64
    limit = nc.sbuf_usable_end

    class Region:

        def __init__(self, at):
            self.at = at

        def __call__(self, name, shape, dtype=F32):
            size = 2 if dtype == BF16 else 4
            n = size * int(np.prod(shape[1:]))
            t = nc.alloc_sbuf_tensor_at(name, shape, dtype, offset=self.at)
            self.at += (n + 31) // 32 * 32
            assert self.at <= limit, (name, self.at, limit)
            return t.ap()

    def sem(name):
        return nc.alloc_semaphore(name)

    proj = nc.dram_tensor("proj", (M_ALL, P, T), F32).ap()
    decayed = nc.dram_tensor("decayed", (UNITS, P, 4, UNIT), F32).ap()
    v_tok = nc.dram_tensor("v_tok", (UNITS, P, HEAD_V), F32).ap()
    state_b = nc.dram_tensor("state_b", (UNITS, P, HEAD_V), F32).ap()
    v_ch = nc.dram_tensor("v_ch", (HEADS * NB, 2, P, 512), F32).ap()
    gate_ch = nc.dram_tensor("gate_ch", (UNITS, 2, P, UNIT), F32).ap()
    gla_out = nc.dram_tensor("gla_out", (UNITS, 2, P, UNIT), F32).ap()
    pool_out = nc.dram_tensor("pool_out", (2 * GROUPS, P, T), F32).ap()
    y_pool = nc.dram_tensor("y_pool", (KT, P, T), F32).ap()
    merged = nc.dram_tensor("merged", (KT, P, T), F32).ap()

    keep = Region(base)
    ident = keep("ident", [P, P])
    ones = keep("ones", [P, P])
    later = keep("later", [P, P], I32)
    vecs = keep("vecs", [P, P])
    gnorm8 = keep("gnorm8", [P, KT])
    c_act = keep("c_act", [P, KT])
    h_scale = keep("h_scale", [P, KT])
    h_shift = keep("h_shift", [P, KT])
    eps_col = keep("eps_col", [P, 1])
    one_col = keep("one_col", [P, 1])
    mid = keep("mid", [P, 2, UNITS + 2])
    tot = keep("tot", [P, 2, UNITS + 2])
    edge = keep("edge", [P, GROUPS, 2 * PAD])
    stage = keep("stage", [P, 2, KT, P])
    w_hi = [keep(f"w_hi{s}", [P, KT, P], F32R) for s in range(2)]
    w_lo = [keep(f"w_lo{s}", [P, KT, P], F32R) for s in range(2)]
    low = keep.at

    big = Region(low)
    h_hi = big("h_hi", [P, KT, T], F32R)
    h_lo = big("h_lo", [P, KT, T], F32R)
    above = big.at

    r0 = Region(above)
    rows = Region(low + 4 * KT * T)("rows", [P, P])
    ada_w = r0("ada_w", [P, 2, KT, 256])
    xin = r0("xin", [P, 2, 4, D])
    h_full = r0("h_full", [P, 2, 512])
    sumsq = r0("sumsq", [P, T // P])
    rstd = r0("rstd", [P, T // P])

    r1 = Region(above)
    tile_out = r1("tile_out", [P, 2, T])
    lr_half = r1("lr_half", [2 * RANK, HALF])
    gk_up = r1("gk_up", [2 * RANK, 2, P])
    q_half = r1("q_half", [P, HALF])
    k_half = r1("k_half", [P, HALF])
    dec_a = r1("dec_a", [P, HALF])
    dec_in = r1("dec_in", [P, HU, UNIT + 1])
    dec_sum = r1("dec_sum", [P, HU, UNIT + 1])
    run_on = r1("run_on", [P, HU, UNIT + 1], BF16)
    q_dec = r1("q_dec", [P, HALF])
    k_dec = r1("k_dec", [P, HALF])

    into = Region(limit // 64 * 64 - 4 * D - 512)("into", [P, 2, UNITS])

    r2 = Region(low)
    kb_in = [r2(f"kb_in{s}", [P, 4, UNIT]) for s in range(2)]
    vt_in = [r2(f"vt_in{s}", [P, 2, 512]) for s in range(2)]
    kv_tok = [r2(f"kv_tok{s}", [P, 3, P]) for s in range(2)]
    sb_out = [r2(f"sb_out{s}", [P, HEAD_V]) for s in range(2)]
    zb = [r2(f"zb{s}", [P, HEAD_V]) for s in range(2)]
    into_tmp = r2("into_tmp", [P, 2, UNITS])

    r3 = Region(low)
    dec_u = [r3(f"dec_u{s}", [P, 4, UNIT]) for s in range(2)]
    v_u = [r3(f"v_u{s}", [P, HEAD_V]) for s in range(2)]
    sb_u = [r3(f"sb_u{s}", [P, HEAD_V]) for s in range(2)]
    gate_u = [r3(f"gate_u{s}", [P, 2, UNIT]) for s in range(2)]
    kf_tok = [r3(f"kf_tok{s}", [P, P]) for s in range(2)]
    score = [r3(f"score{s}", [P, UNIT]) for s in range(2)]
    sf = [r3(f"sf{s}", [P, HEAD_V]) for s in range(2)]
    zf = [r3(f"zf{s}", [P, HEAD_V]) for s in range(2)]
    o_sq = [r3(f"o_sq{s}", [P, 2, UNIT]) for s in range(2)]
    o_ss = [r3(f"o_ss{s}", [P, UNIT]) for s in range(2)]
    o_sd = [r3(f"o_sd{s}", [P, UNIT]) for s in range(2)]
    o_rs = [r3(f"o_rs{s}", [P, UNIT]) for s in range(2)]
    o_n = [r3(f"o_n{s}", [P, 2, UNIT]) for s in range(2)]
    o_g = [r3(f"o_g{s}", [P, 2, UNIT]) for s in range(2)]

    r4 = Region(low)
    u_pad = [r4(f"u_pad{s}", [P, 2, T + 2 * PAD]) for s in range(2)]
    sums = [r4(f"sums{s}", [P, 2, T + 2 * PAD]) for s in range(2)]
    pooled_hi = r4("pooled_hi", [P, 2, T], F32R)
    pooled_lo = r4("pooled_lo", [P, 2, T], F32R)
    pw_in = r4("pw_in", [P, 2, 256])
    pw_hi = r4("pw_hi", [P, 2, 256], F32R)
    pw_lo = r4("pw_lo", [P, 2, 256], F32R)
    pg_in = r4("pg_in", [P, 2, T])
    pa_out = r4("pa_out", [P, 2, T])

    c_wide = r4("c_wide", [P, KT, P])
    gate_w = r4("gate_w", [P, 2, 2, D])
    brow = r4("brow", [1, D])
    prow = r4("prow", [1, D])
    gate_row = Region(limit // 64 * 64 - 4 * D)("gate_row", [P, D])
    assert r4.at <= limit // 64 * 64 - 4 * D

    r5 = Region(above)
    src_in = r5("src_in", [P, 2, T])
    y_out = r5("y_out", [P, 2, T])
    sig_in = r5("sig_in", [P, 2, T])

    r7 = Region(low)
    wo_hi = r7("wo_hi", [P, KT, D], F32R)
    wo_lo = r7("wo_lo", [P, KT, D], F32R)
    wo_in = r7("wo_in", [P, 2, D])
    m_in = [r7(f"m_in{s}", [P, KT, P]) for s in range(2)]
    m_hi = [r7(f"m_hi{s}", [P, KT, P], F32R) for s in range(2)]
    m_lo = [r7(f"m_lo{s}", [P, KT, P], F32R) for s in range(2)]
    x_in = [r7(f"x_in{s}", [P, D]) for s in range(2)]
    fin = [r7(f"fin{s}", [P, D]) for s in range(2)]
    fin_sq = [r7(f"fin_sq{s}", [P, D]) for s in range(2)]
    fin_s = [r7(f"fin_s{s}", [P, 4]) for s in range(2)]

    ps = nc.alloc_psum_tensor("ps", [P, 8, 512], F32).ap()

    step_done, cleared, passed = sem("step_done"), sem("cleared"), sem("passed")
    early = []

    def sem01(name):
        early.append(nc.alloc_semaphore(name))
        return early[-1]

    unused = iter(early)

    def again(name):
        return next(unused)

    consts_ready = sem01("consts_ready")
    rows_loaded = sem01("rows_loaded")
    rows_cleared = sem01("rows_cleared")
    vecs_turned, vecs_ready, c_ready = sem01("vecs_turned"), sem01("vecs_ready"), sem01("c_ready")
    ada_loaded = [sem01(f"ada_loaded{s}") for s in range(2)]
    ada_used, ada_ready, mod_part, mod_ready = sem01("ada_used"), sem01("ada_ready"), sem01("mod_part"), sem01("mod_ready")
    x_loaded = [sem01(f"x_loaded{s}") for s in range(2)]
    sumsq_ready, var_ready, std_ready, rstd_ready = sem01("sumsq_ready"), sem01("var_ready"), sem01("std_ready"), sem01("rstd_ready")
    xn_ready, x_turned, x_used = sem01("xn_ready"), sem01("x_turned"), sem01("x_used")
    hi_ready, full_ready, lo_ready = sem01("hi_ready"), sem01("full_ready"), sem01("lo_ready")

    w_loaded = [sem01(f"w_loaded{s}") for s in range(2)]
    w_hi_ready = sem01("w_hi_ready")
    w_ready = sem01("w_ready")
    product_done = sem01("product_done")
    ps_free = [sem01(f"ps_free{s}") for s in range(2)]
    tile_ready, tile_scaled = sem01("tile_ready"), sem01("tile_scaled")
    tile_stored = [sem(f"tile_stored{s}") for s in range(2)]
    tile_free = [sem01(f"tile_free{s}") for s in range(2)]
    decay_free = sem01("decay_free")
    lr_loaded, gk_loaded, q_loaded, k_loaded = sem01("lr_loaded"), sem01("gk_loaded"), sem01("q_loaded"), sem01("k_loaded")
    gk_cleared = sem01("gk_cleared")
    abs_done, expneg_done, logsig_ready = sem01("abs_done"), sem01("expneg_done"), sem01("logsig_ready")
    min_done, la_done, scan_done, centred = sem01("min_done"), sem01("la_done"), sem01("scan_done"), sem01("centred")
    exps_ready, decayed_ready = sem01("exps_ready"), sem01("decayed_ready")
    qd_stored, kd_stored = sem("qd_stored"), sem("kd_stored")

    def barrier(eng, step):
        eng.drain().then_inc(step_done, 1)
        eng.wait_ge(step_done, ENGINES * step)
        if step == 4:
            if eng.engine == nc.sync.engine:
                for s in early:
                    eng.sem_clear(s).then_inc(cleared, 1)
            eng.wait_ge(cleared, len(early))
            eng.sem_inc(passed, 1)

    def wait_apart(eng, *waits):
        for s, v in waits:
            eng.wait_ge(s, v)
        eng.sem_inc(passed, 1)

    def split_product(pe, banks, lhs_hi, lhs_lo, rhs_hi, rhs_lo, k, first_k, last_k):
        for b in range(NB):
            pe.matmul(banks[:, b], lhs_hi, rhs_hi[:, k, ds(512 * b, 512)], start=first_k, stop=False)
        for b in range(NB):
            pe.matmul(banks[:, b], lhs_hi, rhs_lo[:, k, ds(512 * b, 512)], start=False, stop=False)
        for b in range(NB):
            last = pe.matmul(banks[:, b], lhs_lo, rhs_hi[:, k, ds(512 * b, 512)], start=False, stop=last_k)
        return last

    kb_loaded = [sem01(f"kb_loaded{s}") for s in range(2)]
    into_sum, into_ready = sem01("into_sum"), sem01("into_ready")
    kv_turned, kv_copied, kv_product = sem01("kv_turned"), sem01("kv_copied"), sem01("kv_product")
    zb_ready, sb_ready = sem01("zb_ready"), sem01("sb_ready")
    zb_cleared, zf_cleared, pool_consts = sem01("zb_cleared"), sem01("zf_cleared"), sem01("pool_consts")
    v_stored = [sem01(f"v_stored{s}") for s in range(2)]
    sb_stored = [sem01(f"sb_stored{s}") for s in range(2)]
    unit_loaded = [sem(f"unit_loaded{s}") for s in range(2)]
    scores_done, attn_done, norm_summed = sem("scores_done"), sem("attn_done"), sem("norm_summed")
    states_product = sem("states_product")
    kf_copied, score_copied, score_ready = sem("kf_copied"), sem("score_copied"), sem("score_ready")
    sf_ready, zf_ready = sem("sf_ready"), sem("zf_ready")
    sq_ready, ss_ready, sd_ready, rs_ready, on_ready, og_ready = (sem(n) for n in (
        "sq_ready", "ss_ready", "sd_ready", "rs_ready", "on_ready", "og_ready"))
    og_stored = [sem(f"og_stored{s}") for s in range(2)]
    pads_cleared = again("pads_cleared")
    wide_ready, brow_loaded, gate_used, gate_product, gate_half, gate_ready = (again(n) for n in (
        "wide_ready", "brow_loaded", "gate_used", "gate_product", "gate_half", "gate_ready"))
    gate_loaded = [again(f"gate_loaded{s}") for s in range(2)]
    u_loaded = [again(f"u_loaded{s}") for s in range(2)]
    pg_loaded, pw_loaded = again("pg_loaded"), again("pw_loaded")
    sum_step = [again("sum_step_dve"), again("sum_step_pool")]
    pooled_full = [again("pooled_full_dve"), again("pooled_full_pool")]
    pooled_hi_ready = again("pooled_hi_ready")
    pooled_lo_q = [again("pooled_lo_dve"), again("pooled_lo_pool")]
    pw_hi_ready, pw_ready = again("pw_hi_ready"), again("pw_ready")
    pool_product, pa_ready = again("pool_product"), again("pa_ready")
    pa_stored = [sem(f"pa_stored{s}") for s in range(2)]

    src_loaded = [again(f"src_loaded{e}") for e in range(2)]
    src_hi, src_ready = again("src_hi"), again("src_ready")
    pj_loaded = [again(f"pj_loaded{e}") for e in range(2)]
    pj_hi_ready, pj_ready, pj_product = again("pj_hi_ready"), again("pj_ready"), again("pj_product")
    sig_loaded = [again(f"sig_loaded{e}") for e in range(2)]
    y_loaded = [again(f"y_loaded{e}") for e in range(2)]
    gated, summed = again("gated"), again("summed")
    y_stored = [sem(f"y_stored{e}") for e in range(2)]
    y_free = [again(f"y_free{e}") for e in range(2)]
    wo_loaded = [again(f"wo_loaded{s}") for s in range(2)]
    wo_hi_ready, wo_ready = again("wo_hi_ready"), again("wo_ready")
    m_loaded = [again(f"m_loaded{s}") for s in range(2)]
    x7_loaded = [again(f"x7_loaded{s}") for s in range(2)]
    m_hi_ready, m_ready, out_product = again("m_hi_ready"), again("m_ready"), again("out_product")
    ss7_ready, var7_ready, sd7_ready, rs7_ready, normed7, fin_ready = (again(n) for n in (
        "ss7_ready", "var7_ready", "sd7_ready", "rs7_ready", "normed7", "fin_ready"))
    out_stored = [sem(f"out_stored{s}") for s in range(2)]
    fin_free = [again(f"fin_free{s}") for s in range(2)]

    QK_USES = 1 + 2 * HEADS
    CLASSES = ("p_in", "p_gate", "decay_fwd", "v", "gla_gate", "decay_bwd", "bg_pool", "bg_gla")
    TILES = [n for n in CLASSES if not n.startswith("decay")]
    COLUMN = {"p_in": C_PIN, "p_gate": C_PGATE, "v": C_V, "gla_gate": C_GGATE, "bg_pool": C_BGP, "bg_gla": C_BGG}
    TILE_AT = {"p_in": M_PIN, "p_gate": M_PGATE, "bg_pool": M_BGP, "bg_gla": M_BGG}
    FUNC = {"p_in": ACT.Copy, "p_gate": ACT.Silu, "v": ACT.Copy, "gla_gate": ACT.Silu,
            "bg_pool": ACT.Sigmoid, "bg_gla": ACT.Sigmoid}
    USES, WTILES = len(CLASSES), len(TILES)
    IN_SLOT = [(QK_USES + 1) // 2, QK_USES // 2]
    w_in_v = w_in[0].rearrange("(k p) n -> p k n", p=P)

    def slot(p):
        return (QK_USES + p) % 2

    def in_slot(p, j, each):
        return IN_SLOT[slot(p)] + (each // 2) * j + sum(slot(q) == slot(p) for q in range(p))

    def use_of(t):
        return CLASSES.index(TILES[t])

    def banks(s):
        return ps[:, 4 * s:4 * s + 4]

    def flat(a):
        return a.rearrange("p b n -> p (b n)")

    def pooled_at(g):
        return sums[(len(bin(WINDOWS[g])) - 3) % 2]

    def pool_half(eng, g, q):
        w, mine = WINDOWS[g], sum_step[q]
        steps = len(bin(w)) - 3
        done = sum(len(bin(v)) - 3 for v in WINDOWS[:g]) + 2 * g
        u, length = u_pad[g % 2], T + 2 * PAD
        eng.wait_ge(u_loaded[g % 2], 16 * (g // 2 + 1))
        if g:
            eng.wait_ge(pooled_hi_ready, 2 * g)
            eng.wait_ge(pooled_lo_q[q], g)
        eng.tensor_tensor(sums[0][:, q, 1:length], u[:, q, 0:length - 1], u[:, q, 1:length], ALU.add).then_inc(mine, 1)
        lo, hi = 1, length
        for k in range(1, steps):
            eng.wait_ge(mine, done + k)
            r = 2 ** (k - 1)
            lo, hi = lo + r, hi - r
            a, b = sums[(k - 1) % 2], sums[k % 2]
            eng.tensor_tensor(b[:, q, lo:hi], a[:, q, lo - r:hi - r], a[:, q, lo + r:hi + r], ALU.add).then_inc(mine, 1)
        total, full = sums[(steps - 1) % 2], sums[steps % 2]
        eng.wait_ge(mine, done + steps)
        eng.tensor_tensor(total[:, q, PAD:2 * PAD], total[:, q, PAD:2 * PAD], edge[:, g, 0:PAD], ALU.mult)
        eng.tensor_tensor(total[:, q, T:T + PAD], total[:, q, T:T + PAD], edge[:, g, PAD:2 * PAD], ALU.mult).then_inc(mine, 1)
        eng.wait_ge(mine, done + steps + 1)
        inner = slice(PAD, PAD + T)
        eng.tensor_scalar(full[:, q, inner], total[:, q, inner], 1.0 / w, None, ALU.mult).then_inc(mine, 1)
        eng.wait_ge(mine, done + steps + 2)
        eng.tensor_tensor(full[:, q, inner], full[:, q, inner], u[:, q, inner], ALU.subtract).then_inc(pooled_full[q], 1)
        if g:
            eng.wait_ge(pool_product, 2 * g)
        eng.wait_ge(pooled_full[q], g + 1)
        eng.wait_ge(pooled_hi_ready, 2 * g + q + 1)
        eng.tensor_tensor(pooled_lo[:, q, :], full[:, q, inner], pooled_hi[:, q, :].bitcast(F32), ALU.subtract)\
           .then_inc(pooled_lo_q[q], 1)

    block = nc.Block()
    with block:

        @block.sync
        def _(sp):
            sp.wait_ge(rows_cleared, 1)
            for at, n, src in ((V_C, 8, c), (V_BADA, 24, b_ada), (V_GPRE, 8, g_pre), (V_PSCALE, 8, pool_scale),
                               (V_GKB, 4, gk_bias_fwd), (V_GKB + 4, 4, gk_bias_bwd), (V_GNORM, 2, gla_norm_g)):
                sp.dma_start(rows[at:at + n, :], src.rearrange("o (r p) -> (o r) p", p=P)).then_inc(rows_loaded, 16)
            ada_v = w_ada[0].rearrange("(k p) n -> p k n", p=P)
            x_v = x[0].rearrange("(g t p) n -> g p t n", t=4, p=P)
            for n in range(8):
                if n >= 2:
                    sp.wait_ge(ada_used, n - 1)
                sp.dma_start(ada_w[:, n % 2], ada_v[:, :, 256 * n:256 * n + 256]).then_inc(ada_loaded[n % 2], 16)
                if n in (3, 5):
                    g = n // 2 - 1
                    sp.dma_start(xin[:, g], x_v[g]).then_inc(x_loaded[g], 16)
            sp.dma_start(stage[:, 0], w_in_v[:, :, C_LR:C_LR + P]).then_inc(w_loaded[0], 16)
            for g in range(2, 4):
                sp.wait_ge(x_turned, KT * (g - 1))
                sp.dma_start(xin[:, g % 2], x_v[g]).then_inc(x_loaded[g % 2], 16)
            barrier(sp, 1)

            with sp.Fori(0, HEADS) as h:
                sp.wait_ge(w_ready, START + 2 * h)
                sp.dma_start(stage[:, 1], w_in_v[:, :, ds(C_Q + P * h, P)]).then_inc(w_loaded[1], 16)
                sp.wait_ge(w_ready, START + 2 * h + 1)
                sp.dma_start(stage[:, 0], w_in_v[:, :, ds(C_K + P * h, P)]).then_inc(w_loaded[0], 16)
            def load_tile(t, j):
                sp.wait_ge(w_ready, START + QK_USES + WTILES * j + t - 1)
                sp.dma_start(stage[:, slot(t)], w_in_v[:, :, ds(COLUMN[TILES[t]] + P * j, P)]).then_inc(w_loaded[slot(t)], 16)

            with sp.Fori(0, HEADS) as h:
                with sp.Fori(0, 2) as s:
                    j = 2 * h + s
                    load_tile(0, j)
                    load_tile(1, j)
                    sp.wait_ge(tile_stored[0], 16 * IN_SLOT[0])
                    sp.wait_ge(tile_stored[1], 16 * IN_SLOT[1])
                    sp.wait_ge(product_done, START + QK_USES + USES * j - USES + CLASSES.index("decay_bwd") + 1)
                    sp.dma_start(lr_half[:, :], proj[M_LR, 0:2 * RANK, ds(HALF * s, HALF)]).then_inc(lr_loaded, 16)
                    sp.wait_ge(gk_cleared, 1)
                    sp.dma_start(gk_up[0:RANK, 0, :], gk_up_fwd[0, :, ds(P * h, P)]).then_inc(gk_loaded, 16)
                    sp.dma_start(gk_up[RANK:2 * RANK, 1, :], gk_up_bwd[0, :, ds(P * h, P)]).then_inc(gk_loaded, 16)
                    sp.wait_ge(decayed_ready, START + 2 * j)
                    sp.dma_start(q_half[:, :], proj[M_Q + h, :, ds(HALF * s, HALF)]).then_inc(q_loaded, 16)
                    sp.dma_start(k_half[:, :], proj[M_K + h, :, ds(HALF * s, HALF)]).then_inc(k_loaded, 16)
                    for t in range(2, WTILES):
                        load_tile(t, j)
            barrier(sp, 2)

            def load_group(b, g, back):
                if back is not None:
                    wait_apart(sp, (kv_turned, back))
                n = 2 * HEADS * 2 - 1 - g - 2 * b
                sp.dma_start(kb_in[g][:, :, :], decayed[ds(4 * n, 4), :, 3, :].rearrange("n p t -> p n t")).then_inc(kb_loaded[g], 16)
                sp.dma_start(vt_in[g][:, :, :], v_ch[n].rearrange("a p t -> p a t")).then_inc(kb_loaded[g], 16)

            def store_units(b, g):
                for e in range(4 * g, 4 * g + 4):
                    wait_apart(sp, (kv_copied, START + 8 * b + e + 1))
                    sp.dma_start(v_tok[UNITS - 1 - 8 * b - e], flat(kv_tok[e % 2][:, 1:3])).then_inc(v_stored[e % 2], 16)
                    wait_apart(sp, (sb_ready, 8 * b + e + 2))
                    sp.dma_start(state_b[UNITS - 1 - 8 * b - e], sb_out[e % 2][:, :]).then_inc(sb_stored[e % 2], 16)

            load_group(0, 0, None)
            load_group(0, 1, None)
            with sp.Fori(0, UNITS // 8 - 1) as b:
                for g in range(2):
                    store_units(b, g)
                    load_group(b + 1, g, 8 * b + 4 * g + 4)
            for g in range(2):
                store_units(UNITS // 8 - 1, g)
            for e in range(2):
                sp.wait_ge(v_stored[e], 16 * (1 + UNITS // 2))
                sp.wait_ge(sb_stored[e], 16 * (1 + UNITS // 2))
            barrier(sp, 3)

            def load_unit(n, e):
                sp.wait_ge(attn_done, START + n - 1)
                sp.wait_ge(og_ready, START + n - 1)
                sp.dma_start(dec_u[e][:, :, :], decayed[n]).then_inc(unit_loaded[e], 16)
                sp.dma_start(v_u[e][:, :], v_tok[n]).then_inc(unit_loaded[e], 16)
                sp.dma_start(sb_u[e][:, :], state_b[n]).then_inc(unit_loaded[e], 16)
                sp.dma_start(gate_u[e][:, :, :], gate_ch[n].rearrange("a p t -> p a t")).then_inc(unit_loaded[e], 16)

            def store_unit(n, e):
                wait_apart(sp, (og_ready, START + n + 1))
                sp.dma_start(gla_out[n].rearrange("a p t -> p a t"), o_g[e][:, :, :]).then_inc(og_stored[e], 16)

            load_unit(0, 0)
            load_unit(1, 1)
            with sp.Fori(1, UNITS // 2) as i:
                for e in range(2):
                    load_unit(2 * i + e, e)
                for e in range(2):
                    store_unit(2 * i - 2 + e, e)
            for e in range(2):
                store_unit(UNITS - 2 + e, e)
            for e in range(2):
                sp.wait_ge(og_stored[e], 16 * (1 + UNITS // 2))
            barrier(sp, 4)

            sp.dma_start(brow[:, :], b_ada[:, 2 * D:3 * D]).then_inc(brow_loaded, 16)
            sp.dma_start(prow[:, :], g_post[:, :]).then_inc(brow_loaded, 16)
            sp.wait_ge(pads_cleared, 2)
            for g in range(GROUPS):
                if g >= 2:
                    sp.wait_ge(gate_used, 2 * (g - 1))
                sp.dma_start(gate_w[:, g % 2], ada_v[:, 2 * g:2 * g + 2, 2 * D:3 * D]).then_inc(gate_loaded[g % 2], 16)
            for g in range(GROUPS):
                if g >= 2:
                    for q in range(2):
                        sp.wait_ge(pooled_full[q], g - 1)
                sp.dma_start(u_pad[g % 2][:, :, PAD:PAD + T], proj[M_PIN + 2 * g:M_PIN + 2 * g + 2]
                             .rearrange("a p t -> p a t")).then_inc(u_loaded[g % 2], 16)
                if g:
                    sp.wait_ge(pw_ready, g)
                sp.dma_start(pw_in[:, :, :], pool_w[0, g].rearrange("(a p) n -> p a n", p=P)).then_inc(pw_loaded, 16)
                if g:
                    sp.wait_ge(pa_ready, 2 * g)
                sp.dma_start(pg_in[:, :, :], proj[M_PGATE + 2 * g:M_PGATE + 2 * g + 2]
                             .rearrange("a p t -> p a t")).then_inc(pg_loaded, 16)
            barrier(sp, 5)

            for r, (wt, sig_at) in enumerate(((w_proj_pool, M_BGP), (w_proj_gla, M_BGG))):
                wt_v = wt[0].rearrange("(k p) n -> p k n", p=P)
                with sp.Fori(0, KT // 2) as i:
                    for e in range(2):
                        m = 2 * i + e
                        sp.wait_ge(pj_ready, START + KT * r + m - 1)
                        sp.dma_start(stage[:, e], wt_v[:, :, ds(P * m, P)]).then_inc(pj_loaded[e], 16)
                        sp.wait_ge(gated, START + KT * r + m - 1)
                        sp.dma_start(sig_in[:, e], proj[sig_at + m]).then_inc(sig_loaded[e], 16)
                        if r == 1:
                            sp.wait_ge(src_ready, 2 * KT)
                            sp.wait_ge(summed, START + m - 1)
                            sp.dma_start(src_in[:, e], y_pool[m]).then_inc(y_loaded[e], 16)
                barrier(sp, 6 + r)

            wo_v = w_out[0].rearrange("(k p) n -> k p n", p=P)
            for k in range(KT):
                if k >= 2:
                    sp.wait_ge(wo_ready, k - 1)
                sp.dma_start(wo_in[:, k % 2], wo_v[k]).then_inc(wo_loaded[k % 2], 16)
            with sp.Fori(0, T // P // 2) as i:
                for e in range(2):
                    n = 2 * i + e
                    sp.wait_ge(m_ready, START + n - 1)
                    sp.dma_start(m_in[e][:, :, :], merged[:, :, ds(P * n, P)].rearrange("k p t -> p k t")).then_inc(m_loaded[e], 16)
                    sp.wait_ge(fin_ready, START + n - 1)
                    sp.dma_start(x_in[e][:, :], x[0, ds(P * n, P), :]).then_inc(x7_loaded[e], 16)
            barrier(sp, 8)

        @block.tensor
        def _(pe):
            pe.sem_inc(product_done, START)
            pe.wait_ge(consts_ready, 1)
            pe.wait_ge(rows_loaded, 16 * 7)
            pe.transpose(ps[:, 7, 0:P], rows[:, :], ident[:, :]).then_inc(vecs_turned, 1)
            pe.wait_ge(c_ready, 1)
            for n in range(8):
                pe.wait_ge(ada_loaded[n % 2], 16 * (n // 2 + 1))
                for m in range(2):
                    for k in range(KT):
                        last = pe.matmul(ps[:, 6, 2 * n + m:2 * n + m + 1], ada_w[:, n % 2, k, P * m:P * m + P],
                                         c_act[:, k:k + 1], start=(k == 0), stop=(k == KT - 1))
                last.then_inc(ada_used, 1)
            for g in range(4):
                pe.wait_ge(xn_ready, g + 1)
                for k in range(KT):
                    n = KT * g + k
                    if n >= 4:
                        pe.wait_ge(full_ready, n - 3)
                    for t in range(4):
                        last = pe.transpose(ps[:, n % 4, P * t:P * t + P], xin[:, g % 2, t, P * k:P * k + P], ident[:, :])
                    last.then_inc(x_turned, 1)
            barrier(pe, 1)

            def tile_product(s):
                for k in range(KT):
                    last = split_product(pe, banks(s), w_hi[s][:, k], w_lo[s][:, k], h_hi, h_lo, k, k == 0, k == KT - 1)
                last.then_inc(product_done, 1)

            pe.wait_ge(w_ready, START + 1)
            tile_product(0)
            with pe.Fori(0, HEADS) as h:
                for e in range(2):
                    s = 1 - e
                    pe.wait_ge(w_ready, START + 2 * h + e + 2)
                    pe.wait_ge(ps_free[s], h + e + 1)
                    tile_product(s)
            with pe.Fori(0, 2 * HEADS) as j:
                for p, name in enumerate(CLASSES):
                    s = slot(p)
                    pe.wait_ge(ps_free[s], in_slot(p, j, USES) + 1)
                    if name in TILES:
                        t = TILES.index(name)
                        pe.wait_ge(w_ready, START + QK_USES + WTILES * j + t + 1)
                        for k in range(KT):
                            last = split_product(pe, banks(s), w_hi[slot(t)][:, k], w_lo[slot(t)][:, k],
                                                 h_hi, h_lo, k, k == 0, k == KT - 1)
                    else:
                        d = int(name == "decay_bwd")
                        if d == 0:
                            pe.wait_ge(lr_loaded, 16 * j + 16)
                            pe.wait_ge(gk_loaded, 32 * j + 32)
                        for b in range(2):
                            last = pe.matmul(banks(s)[:, b], gk_up[:, d, :], lr_half[:, 512 * b:512 * b + 512],
                                             start=True, stop=True)
                    last.then_inc(product_done, 1)
            barrier(pe, 2)

            def kv_turn(n, g, q, s):
                pe.wait_ge(kv_copied, START + n - 1)
                pe.transpose(ps[:, s, 0:P], kb_in[g][:, q, :], ident[:, :])
                for half in range(2):
                    last = pe.transpose(ps[:, s, P + P * half:2 * P + P * half],
                                        vt_in[g][:, half, UNIT * q:UNIT * q + UNIT], ident[:, :])
                last.then_inc(kv_turned, 1)

            def kv_multiply(n, s):
                pe.wait_ge(kv_copied, START + n + 1)
                pe.wait_ge(zb_ready, START + n - 1)
                pe.matmul(ps[:, 2 + s, 0:HEAD_V], kv_tok[s][:, 0, :], flat(kv_tok[s][:, 1:3]),
                          start=True, stop=True).then_inc(kv_product, 1)

            with pe.Fori(0, 2 * HEADS) as b:
                for e in range(8):
                    if e in (0, 4):
                        pe.wait_ge(kb_loaded[e // 4], 32 * b + 32)
                    kv_turn(8 * b + e, e // 4, 3 - e % 4, e % 2)
                    if e:
                        kv_multiply(8 * b + e - 1, (e - 1) % 2)
                kv_multiply(8 * b + 7, 1)
            barrier(pe, 3)

            def scores(n, e):
                pe.wait_ge(unit_loaded[e], 64 * i_of(n) + 64)
                pe.wait_ge(score_ready, START + n - 1)
                pe.transpose(ps[:, e, 0:P], dec_u[e][:, 2, :], ident[:, :])
                for d in range(2):
                    last = pe.matmul(ps[:, e, P + P * d:2 * P + P * d], dec_u[e][:, 2 + d, :], dec_u[e][:, d, :],
                                     start=True, stop=True)
                last.then_inc(scores_done, 1)

            def attend(n, e):
                pe.wait_ge(kf_copied, START + n + 1)
                pe.wait_ge(zf_ready, START + n - 1)
                pe.matmul(ps[:, 2 + e, 0:HEAD_V], kf_tok[e][:, :], v_u[e][:, :], start=True, stop=True).then_inc(states_product, 1)
                pe.wait_ge(score_ready, START + n + 1)
                pe.wait_ge(on_ready, START + n - 1)
                for half in range(2):
                    cols = slice(P * half, P * half + P)
                    pe.matmul(ps[:, 4 + e, cols], v_u[e][:, cols], score[e][:, :], start=True, stop=False)
                    pe.matmul(ps[:, 4 + e, cols], sb_u[e][:, cols], dec_u[e][:, 1, :], start=False, stop=False)
                    if half == 0:
                        pe.wait_ge(sf_ready, START + n + 1)
                    last = pe.matmul(ps[:, 4 + e, cols], sf[e][:, cols], dec_u[e][:, 0, :], start=False, stop=True)
                last.then_inc(attn_done, 1)

            def norm_sum(n, e):
                pe.wait_ge(ss_ready, START + n + 1)
                pe.wait_ge(sd_ready, START + n - 1)
                pe.matmul(ps[:, 6 + e, 0:UNIT], ones[:, :], o_ss[e][:, :], start=True, stop=True).then_inc(norm_summed, 1)

            def i_of(n):
                return turn[0]

            turn = [0]
            scores(0, 0)
            scores(1, 1)
            attend(0, 0)
            attend(1, 1)
            norm_sum(0, 0)
            with pe.Fori(1, UNITS // 2) as i:
                turn[0] = i
                scores(2 * i, 0)
                norm_sum(2 * i - 1, 1)
                scores(2 * i + 1, 1)
                attend(2 * i, 0)
                attend(2 * i + 1, 1)
                norm_sum(2 * i, 0)
            norm_sum(UNITS - 1, 1)
            barrier(pe, 4)

            pe.wait_ge(brow_loaded, 32)
            pe.wait_ge(wide_ready, 1)
            for b in range(2):
                pe.matmul(ps[:, 2 + b], ones[0:1, :], prow[:, 512 * b:512 * b + 512], start=True, stop=True)
                pe.matmul(ps[:, b], ones[0:1, :], brow[:, 512 * b:512 * b + 512], start=True, stop=False)
            for g in range(GROUPS):
                pe.wait_ge(gate_loaded[g % 2], 16 * (g // 2 + 1))
                for r in range(2):
                    for b in range(2):
                        last = pe.matmul(ps[:, b], c_wide[:, 2 * g + r, :], gate_w[:, g % 2, r, 512 * b:512 * b + 512],
                                         start=False, stop=(g == GROUPS - 1 and r == 1))
                    last.then_inc(gate_used, 1)
            for g in range(GROUPS):
                pe.wait_ge(pw_ready, g + 1)
                pe.wait_ge(pooled_hi_ready, 2 * g + 2)
                for q in range(2):
                    pe.wait_ge(pooled_lo_q[q], g + 1)
                for dh in range(2):
                    if g == 0:
                        pe.wait_ge(gate_ready, 1)
                    else:
                        pe.wait_ge(pa_ready, 2 * g + dh - 1)
                    for a in range(2):
                        cols = slice(P * dh, P * dh + P)
                        last = split_product(pe, banks(dh), pw_hi[:, a, cols], pw_lo[:, a, cols], pooled_hi, pooled_lo,
                                             a, a == 0, a == 1)
                    last.then_inc(pool_product, 1)
            barrier(pe, 5)

            for r in range(2):
                with pe.Fori(0, KT // 2) as i:
                    for e in range(2):
                        m = 2 * i + e
                        pe.wait_ge(pj_ready, START + KT * r + m + 1)
                        pe.wait_ge(gated, START + KT * r + m - 1)
                        for k in range(KT):
                            pe.wait_ge(src_ready, KT * r + k + 1)
                            last = split_product(pe, banks(e), w_hi[e][:, k], w_lo[e][:, k], h_hi, h_lo, k, k == 0, k == KT - 1)
                        last.then_inc(pj_product, 1)
                barrier(pe, 6 + r)

            with pe.Fori(0, T // P // 2) as i:
                for e in range(2):
                    n = 2 * i + e
                    pe.wait_ge(m_ready, START + n + 1)
                    pe.wait_ge(normed7, START + n - 1)
                    for k in range(KT):
                        pe.wait_ge(wo_ready, k + 1)
                        for lhs, rhs in ((m_hi, wo_hi), (m_hi, wo_lo), (m_lo, wo_hi)):
                            for b in range(2):
                                last = pe.matmul(ps[:, 2 * e + b], lhs[e][:, k, :], rhs[:, k, 512 * b:512 * b + 512],
                                                 start=(k == 0 and lhs is m_hi and rhs is wo_hi),
                                                 stop=(k == KT - 1 and lhs is m_lo))
                    last.then_inc(out_product, 1)
            barrier(pe, 8)

        @block.scalar
        def _(act):
            act.wait_ge(vecs_ready, 1)
            act.activation(c_act[:, :], vecs[:, V_C:V_C + KT], ACT.Silu).then_inc(c_ready, 1)
            for g in range(4):
                act.wait_ge(x_loaded[g % 2], 16 * (g // 2 + 1))
                for t in range(4):
                    if g or t:
                        act.wait_ge(sumsq_ready, 4 * g + t)
                    act.activation(flat(ps[:, 4:6]), xin[:, g % 2, t], ACT.Square,
                                   accum_out=sumsq[:, 4 * g + t:4 * g + t + 1]).then_inc(sumsq_ready, 1)
                act.wait_ge(var_ready, g + 1)
                act.activation(rstd[:, 4 * g:4 * g + 4], rstd[:, 4 * g:4 * g + 4], ACT.Sqrt).then_inc(std_ready, 1)
                for k in range(KT):
                    n = KT * g + k
                    act.wait_ge(full_ready, n + 1)
                    act.activation(h_hi[:, k, 512 * g:512 * g + 512], h_full[:, n % 2], ACT.Copy).then_inc(hi_ready, 1)
            barrier(act, 1)

            def evacuate(n_use, ps_slot, out_slot, stored, func, scale=1.0):
                act.wait_ge(product_done, START + n_use + 1)
                act.wait_ge(tile_free[out_slot], stored)
                act.activation(tile_out[:, out_slot], flat(banks(ps_slot)), func, scale=scale).then_inc(tile_ready, 1)

            evacuate(0, 0, 0, 1, ACT.Copy)
            act.wait_ge(tile_ready, 1)
            act.sem_inc(ps_free[0], 1)
            with act.Fori(0, HEADS) as h:
                for e in range(2):
                    evacuate(2 * h + e + 1, 1 - e, 1 - e, h + e + 1, ACT.Copy,
                             scale=float(P) ** -0.5 if e == 0 else 1.0)
                    act.wait_ge(tile_ready, 2 * h + e + 2)
                    act.sem_inc(ps_free[1 - e], 1)
            with act.Fori(0, HEADS) as h:
                with act.Fori(0, 2) as s2:
                    j = 2 * h + s2
                    for p, name in enumerate(CLASSES):
                        use = QK_USES + USES * j + p
                        if name in TILES:
                            t = TILES.index(name)
                            evacuate(use, slot(p), slot(t), in_slot(t, j, WTILES) + 1, FUNC[name])
                            act.wait_ge(tile_ready, QK_USES + WTILES * j + t + 1)
                            act.sem_inc(ps_free[slot(p)], 1)
                        else:
                            d = int(name == "decay_bwd")
                            z = flat(banks(slot(p))[:, 0:2])
                            act.wait_ge(product_done, START + use + 1)
                            act.activation(dec_a[:, :], z, ACT.Abs, bias=vecs[:, ds(V_GKB + HEADS * d + h, 1)]).then_inc(abs_done, 1)
                            act.wait_ge(abs_done, 2 * j + d + 1)
                            act.activation(dec_a[:, :], dec_a[:, :], ACT.Exp, scale=-1.0).then_inc(expneg_done, 1)
                            act.wait_ge(expneg_done, 2 * j + d + 1)
                            act.activation(dec_a[:, :], dec_a[:, :], ACT.Ln, bias=one_col[:, :]).then_inc(logsig_ready, 1)
                            act.wait_ge(centred, 2 * j + d + 1)
                            sign = (1.0 if d == 0 else -1.0) / NORMALIZER
                            act.wait_ge(decay_free, 2 * j + d + 1)
                            act.activation(q_dec[:, :], dec_a[:, :], ACT.Exp, scale=sign)
                            act.activation(k_dec[:, :], dec_a[:, :], ACT.Exp, scale=-sign).then_inc(exps_ready, 1)
            barrier(act, 2)

            for d in range(2):
                act.wait_ge(into_sum, 2 * d + 2)
                act.activation(into[:, d], into_tmp[:, d], ACT.Exp, scale=1.0 / NORMALIZER).then_inc(into_ready, 1)
            with act.Fori(0, HEADS) as hh:
                with act.Fori(0, UPH // 2) as i:
                    for e in range(2):
                        n = UPH * hh + 2 * i + e
                        act.wait_ge(kv_turned, n + 1)
                        act.wait_ge(kv_product, START + n - 1)
                        act.wait_ge(v_stored[e], 16 * (UPH // 2 * hh + i) + 16)
                        act.activation(flat(kv_tok[e][:, :, :]), ps[:, e, 0:3 * P], ACT.Copy).then_inc(kv_copied, 1)
                        act.wait_ge(zb_ready, START + n)
                        if e == 0:
                            act.wait_ge(zb_cleared, hh + 1)
                        act.wait_ge(sb_stored[e], 16 * (UPH // 2 * hh + i) + 16)
                        act.activation(sb_out[e][:, :], zb[1 - e][:, :], ACT.Copy,
                                       scale=into[:, 1, ds(UNITS - 1 - n, 1)]).then_inc(sb_ready, 1)
            barrier(act, 3)

            def copies(n, e):
                act.wait_ge(scores_done, n + 1)
                act.wait_ge(states_product, START + n - 1)
                act.activation(kf_tok[e][:, :], ps[:, e, 0:P], ACT.Copy).then_inc(kf_copied, 1)
                act.wait_ge(attn_done, START + n - 1)
                act.activation(score[e][:, :], ps[:, e, P:2 * P], ACT.Copy).then_inc(score_copied, 1)

            def carry(n, e):
                act.wait_ge(zf_ready, START + n)
                act.activation(sf[e][:, :], zf[1 - e][:, :], ACT.Copy, scale=into[:, 0, ds(n, 1)]).then_inc(sf_ready, 1)

            def squares(n, e):
                act.wait_ge(attn_done, START + n + 1)
                act.wait_ge(ss_ready, START + n - 1)
                act.activation(flat(o_sq[e][:, :, :]), ps[:, 4 + e, 0:HEAD_V], ACT.Square).then_inc(sq_ready, 1)

            def root(n, e):
                act.wait_ge(norm_summed, START + n + 1)
                act.wait_ge(rs_ready, START + n - 1)
                act.activation(o_sd[e][:, :], ps[:, 6 + e, 0:UNIT], ACT.Sqrt, scale=1.0 / HEAD_V,
                               bias=eps_col[:, :]).then_inc(sd_ready, 1)

            act.wait_ge(zf_cleared, 1)
            copies(0, 0)
            carry(0, 0)
            copies(1, 1)
            carry(1, 1)
            squares(0, 0)
            squares(1, 1)
            root(0, 0)
            with act.Fori(1, UNITS // 2) as i:
                copies(2 * i, 0)
                root(2 * i - 1, 1)
                carry(2 * i, 0)
                copies(2 * i + 1, 1)
                carry(2 * i + 1, 1)
                squares(2 * i, 0)
                squares(2 * i + 1, 1)
                root(2 * i, 0)
            root(UNITS - 1, 1)
            barrier(act, 4)

            for g in range(GROUPS):
                act.wait_ge(pw_loaded, 16 * (g + 1))
                if g:
                    act.wait_ge(pool_product, 2 * g)
                act.activation(pw_hi[:, :, :], pw_in[:, :, :], ACT.Copy).then_inc(pw_hi_ready, 1)
                for q in range(2):
                    act.wait_ge(pooled_full[q], g + 1)
                    act.activation(pooled_hi[:, q, :], pooled_at(g)[:, q, PAD:PAD + T], ACT.Copy).then_inc(pooled_hi_ready, 1)
            barrier(act, 5)

            def load_source(r, k):
                if r == 0:
                    act.dma_start(src_in[:, k % 2], pool_out[k]).then_inc(src_loaded[k % 2], 16)
                else:
                    u = k // 2 * UPH
                    act.dma_start(src_in[:, k % 2].rearrange("p (u t) -> p u t", t=UNIT),
                                  gla_out[u:u + UPH, k % 2].rearrange("u p t -> p u t")).then_inc(src_loaded[k % 2], 16)

            for r in range(2):
                for k in range(2):
                    load_source(r, k)
                for k in range(KT):
                    act.wait_ge(src_loaded[k % 2], 16 * (KT // 2 * r + k // 2 + 1))
                    act.activation(h_hi[:, k, :], src_in[:, k % 2], ACT.Copy).then_inc(src_hi, 1)
                    if k + 2 < KT:
                        act.wait_ge(src_ready, KT * r + k + 1)
                        load_source(r, k + 2)
                barrier(act, 6 + r)

            for k in range(KT):
                act.wait_ge(wo_loaded[k % 2], 16 * (k // 2 + 1))
                act.activation(wo_hi[:, k, :], wo_in[:, k % 2], ACT.Copy).then_inc(wo_hi_ready, 1)
            with act.Fori(0, T // P // 2) as i:
                for e in range(2):
                    n = 2 * i + e
                    act.wait_ge(m_loaded[e], 16 * i + 16)
                    act.wait_ge(out_product, START + n - 1)
                    act.activation(m_hi[e][:, :, :], m_in[e][:, :, :], ACT.Copy).then_inc(m_hi_ready, 1)
                    act.wait_ge(out_product, START + n + 1)
                    act.activation(fin_sq[e][:, :], flat(ps[:, 2 * e:2 * e + 2]), ACT.Square,
                                   accum_out=fin_s[e][:, 0:1]).then_inc(ss7_ready, 1)
                    act.wait_ge(ss7_ready, n + 1)
                    act.activation(fin_s[e][:, 1:2], fin_s[e][:, 0:1], ACT.Sqrt, scale=1.0 / D,
                                   bias=eps_col[:, :]).then_inc(sd7_ready, 1)
            barrier(act, 8)

        @block.vector
        def _(dve):
            for s in (w_ready, decayed_ready, zb_ready, kv_copied, score_ready, kf_copied, zf_ready, on_ready,
                      ss_ready, sd_ready, rs_ready, sf_ready, og_ready, attn_done, states_product, kv_product, norm_summed):
                dve.sem_inc(s, START)
            for s in (*ps_free, *tile_free, decay_free, sb_ready):
                dve.sem_inc(s, 1)
            for s in (*v_stored, *sb_stored, *og_stored):
                dve.sem_inc(s, 16)
            dve.wait_ge(vecs_turned, 1)
            dve.tensor_copy(vecs[:, :], ps[:, 7, 0:P]).then_inc(vecs_ready, 1)
            dve.wait_ge(vecs_ready, 1)
            for r in range(KT // 2):
                dve.tensor_copy(gnorm8[:, 2 * r:2 * r + 2], vecs[:, V_GNORM:V_GNORM + 2])

            def inverse_rms(g):
                dve.wait_ge(sumsq_ready, 4 * g + 4)
                cols = slice(4 * g, 4 * g + 4)
                dve.tensor_scalar(rstd[:, cols], sumsq[:, cols], 1.0 / D, EPS, ALU.mult, ALU.add).then_inc(var_ready, 1)
                dve.wait_ge(std_ready, g + 1)
                dve.reciprocal(rstd[:, cols], rstd[:, cols]).then_inc(rstd_ready, 1)
                dve.wait_ge(rstd_ready, g + 1)
                for t in range(4):
                    last = dve.tensor_scalar(xin[:, g % 2, t], xin[:, g % 2, t], rstd[:, 4 * g + t:4 * g + t + 1], None, ALU.mult)
                last.then_inc(xn_ready, 1)

            inverse_rms(0)
            dve.wait_ge(ada_used, 8)
            dve.tensor_tensor(h_shift[:, :], ps[:, 6, 0:KT], vecs[:, V_BADA:V_BADA + KT], ALU.add).then_inc(mod_ready, 1)
            dve.scalar_tensor_tensor(h_scale[:, :], ps[:, 6, KT:2 * KT], 1.0, vecs[:, V_BADA + KT:V_BADA + 2 * KT],
                                     ALU.add, ALU.add).then_inc(mod_part, 1)
            dve.wait_ge(mod_part, 1)
            dve.tensor_tensor(h_scale[:, :], h_scale[:, :], vecs[:, V_GPRE:V_GPRE + KT], ALU.mult).then_inc(mod_ready, 1)
            dve.wait_ge(mod_ready, 2)
            for g in range(4):
                if g:
                    inverse_rms(g)
                for k in range(KT):
                    n = KT * g + k
                    dve.wait_ge(x_turned, n + 1)
                    if n >= 2:
                        dve.wait_ge(lo_ready, n - 1)
                    dve.tensor_scalar(h_full[:, n % 2], ps[:, n % 4], h_scale[:, k:k + 1], h_shift[:, k:k + 1],
                                      ALU.mult, ALU.add).then_inc(full_ready, 1)
            barrier(dve, 1)

            def split_weights(s, hi_sem, ready_sem, count):
                dve.tensor_copy(w_hi[s][:, :, :], stage[:, s]).then_inc(hi_sem, 1)
                dve.wait_ge(hi_sem, count + 1)
                dve.tensor_tensor(w_lo[s][:, :, :], stage[:, s], w_hi[s][:, :, :].bitcast(F32), ALU.subtract).then_inc(ready_sem, 1)

            dve.wait_ge(pool_consts, 3)
            dve.wait_ge(w_loaded[0], 16)
            split_weights(0, w_hi_ready, w_ready, 0)
            with dve.Fori(0, HEADS) as h:
                for e in range(2):
                    s = 1 - e
                    dve.wait_ge(product_done, START + 2 * h + e)
                    dve.wait_ge(w_loaded[s], 16 * h + 16 * e + 16)
                    split_weights(s, w_hi_ready, w_ready, 2 * h + e + 1)
            with dve.Fori(0, HEADS) as h:
                with dve.Fori(0, 2) as s2:
                    j = 2 * h + s2

                    def split_tile(t):
                        back = use_of(t - 2) + USES if t >= 2 else use_of(t + WTILES - 2)
                        dve.wait_ge(product_done, START + QK_USES + USES * j - USES + back + 1)
                        dve.wait_ge(w_loaded[slot(t)], 16 * in_slot(t, j, WTILES) + 16)
                        split_weights(slot(t), w_hi_ready, w_ready, QK_USES + WTILES * j + t)

                    def scale_tile(t, col):
                        dve.wait_ge(tile_ready, QK_USES + WTILES * j + t + 1)
                        dve.tensor_scalar(tile_out[:, slot(t)], tile_out[:, slot(t)], col, None, ALU.mult).then_inc(tile_scaled, 1)

                    def decay(d):
                        p = CLASSES.index(("decay_fwd", "decay_bwd")[d])
                        n = 2 * j + d
                        z = flat(banks(slot(p))[:, 0:2]).rearrange("p (u t) -> p u t", t=UNIT)
                        a = dec_a[:, :].rearrange("p (u t) -> p u t", t=UNIT)
                        dve.wait_ge(abs_done, n + 1)
                        dve.tensor_scalar(dec_in[:, :, 1:UNIT + 1], z, vecs[:, ds(V_GKB + HEADS * d + h, 1)], 0.0,
                                          ALU.add, ALU.min).then_inc(min_done, 1)
                        dve.wait_ge(min_done, n + 1)
                        dve.wait_ge(logsig_ready, n + 1)
                        dve.sem_inc(ps_free[slot(p)], 1)
                        dve.tensor_tensor(dec_in[:, :, 1:UNIT + 1], dec_in[:, :, 1:UNIT + 1], a, ALU.subtract).then_inc(la_done, 1)
                        dve.wait_ge(la_done, n + 1)
                        dve.tensor_tensor_scan(flat(dec_sum[:, :, :]), flat(run_on[:, :, :]), flat(dec_in[:, :, :]), 0.0,
                                               ALU.mult, ALU.add).then_inc(scan_done, 1)
                        dve.wait_ge(scan_done, n + 1)
                        dve.tensor_copy(mid[:, d, ds(HU * j + 1, HU)], dec_sum[:, :, UNIT // 2])
                        dve.tensor_copy(tot[:, d, ds(HU * j + 1, HU)], dec_sum[:, :, UNIT])
                        own = dec_sum[:, :, 1 - d:1 - d + UNIT]
                        dve.tensor_tensor(a, own, dec_sum[:, :, UNIT // 2:UNIT // 2 + 1].to_broadcast([P, HU, UNIT]),
                                          ALU.subtract).then_inc(centred, 1)

                    split_tile(0)
                    split_tile(1)
                    split_tile(2)
                    split_tile(3)
                    scale_tile(1, vecs[:, ds(V_PSCALE + j, 1)])
                    decay(0)
                    split_tile(4)
                    split_tile(5)
                    scale_tile(3, gnorm8[:, ds(j, 1)])
                    decay(1)
            barrier(dve, 2)

            for d in range(2):
                dve.tensor_tensor(into_tmp[:, d], tot[:, d, d:d + UNITS], mid[:, d, d:d + UNITS], ALU.subtract).then_inc(into_sum, 1)
                dve.wait_ge(into_sum, 2 * d + 1)
                dve.tensor_tensor(into_tmp[:, d], into_tmp[:, d], mid[:, d, d + 1:d + 1 + UNITS], ALU.add).then_inc(into_sum, 1)
            dve.wait_ge(into_ready, 2)
            dve.memset(into[:, 0, 0:UNITS:UPH], 0.0)
            with dve.Fori(0, HEADS) as hh:
                dve.wait_ge(zb_ready, START + UPH * hh)
                dve.memset(zb[1][:, :], 0.0).then_inc(zb_cleared, 1)
                wait_apart(dve, (zb_cleared, hh + 1))
                with dve.Fori(0, UPH // 2) as i:
                    for e in range(2):
                        n = UPH * hh + 2 * i + e
                        wait_apart(dve, (kv_product, START + n + 1), (sb_ready, n + 1), (zb_ready, START + n))
                        dve.scalar_tensor_tensor(zb[e][:, :], zb[1 - e][:, :], into[:, 1, ds(UNITS - 1 - n, 1)],
                                                 ps[:, 2 + e, 0:HEAD_V], ALU.mult, ALU.add).then_inc(zb_ready, 1)
            barrier(dve, 3)

            def choose(n, e):
                wait_apart(dve, (scores_done, n + 1), (score_copied, n + 1))
                dve.copy_predicated(score[e][:, :], later[:, :], ps[:, e, 2 * P:3 * P]).then_inc(score_ready, 1)

            def add_state(n, e):
                dve.wait_ge(states_product, START + n + 1)
                dve.wait_ge(sf_ready, START + n)
                dve.wait_ge(zf_ready, START + n)
                dve.scalar_tensor_tensor(zf[e][:, :], zf[1 - e][:, :], into[:, 0, ds(n, 1)],
                                         ps[:, 2 + e, 0:HEAD_V], ALU.mult, ALU.add).then_inc(zf_ready, 1)

            def normalize(n, e):
                dve.wait_ge(sd_ready, START + n + 1)
                dve.reciprocal(o_rs[e][:, :], o_sd[e][:, :]).then_inc(rs_ready, 1)
                dve.wait_ge(rs_ready, START + n + 1)
                dve.wait_ge(og_ready, START + n - 1)
                o = ps[:, 4 + e, 0:HEAD_V].rearrange("p (a t) -> p a t", a=2)
                dve.tensor_tensor(o_n[e][:, :, :], o, o_rs[e][:, :].unsqueeze(1).to_broadcast([P, 2, UNIT]), ALU.mult)\
                   .then_inc(on_ready, 1)

            dve.memset(zf[1][:, :], 0.0).then_inc(zf_cleared, 1)
            dve.wait_ge(zf_cleared, 1)
            choose(0, 0)
            choose(1, 1)
            add_state(0, 0)
            add_state(1, 1)
            normalize(0, 0)
            with dve.Fori(1, UNITS // 2) as i:
                choose(2 * i, 0)
                normalize(2 * i - 1, 1)
                choose(2 * i + 1, 1)
                add_state(2 * i, 0)
                add_state(2 * i + 1, 1)
                normalize(2 * i, 0)
            normalize(UNITS - 1, 1)
            barrier(dve, 4)

            for s in (pj_ready, gated, summed, m_ready, fin_ready, out_product, normed7):
                dve.sem_inc(s, START)
            for s in (*y_free, *fin_free):
                dve.sem_inc(s, 1)
            dve.tensor_copy(c_wide[:, :, :], c_act[:, :].unsqueeze(2).to_broadcast([P, KT, P])).then_inc(wide_ready, 1)
            dve.wait_ge(gate_used, 8)
            dve.tensor_copy(gate_row[:, :], flat(ps[:, 0:2])).then_inc(gate_half, 1)
            dve.wait_ge(gate_half, 1)
            dve.tensor_tensor(gate_row[:, :], gate_row[:, :], flat(ps[:, 2:4]), ALU.mult).then_inc(gate_ready, 1)
            for g in range(GROUPS):
                dve.wait_ge(pw_loaded, 16 * (g + 1))
                dve.wait_ge(pw_hi_ready, g + 1)
                dve.tensor_tensor(pw_lo[:, :, :], pw_in[:, :, :], pw_hi[:, :, :].bitcast(F32), ALU.subtract).then_inc(pw_ready, 1)
                pool_half(dve, g, 0)
                for dh in range(2):
                    dve.wait_ge(pool_product, 2 * g + dh + 1)
                    dve.wait_ge(pg_loaded, 16 * (g + 1))
                    if g:
                        dve.wait_ge(pa_stored[dh], 16 * g)
                    dve.tensor_tensor(pa_out[:, dh], flat(banks(dh)), pg_in[:, dh], ALU.mult).then_inc(pa_ready, 1)
            barrier(dve, 5)

            for r in range(2):
                def split_next(m, e, i):
                    dve.wait_ge(pj_loaded[e], 16 * (KT // 2) * r + 16 * i + 16)
                    split_weights(e, pj_hi_ready, pj_ready, KT * r + m)

                split_next(0, 0, 0)
                for k in range(KT):
                    dve.wait_ge(src_hi, KT * r + k + 1)
                    dve.tensor_tensor(h_lo[:, k, :], src_in[:, k % 2], h_hi[:, k, :].bitcast(F32), ALU.subtract).then_inc(src_ready, 1)
                split_next(1, 1, 0)

                def gate_tile(m, e, i):
                    dve.wait_ge(pj_product, KT * r + m + 1)
                    dve.wait_ge(sig_loaded[e], 16 * (KT // 2) * r + 16 * i + 16)
                    dve.wait_ge(y_free[e], KT // 2 * r + i + 1)
                    dve.tensor_tensor(y_out[:, e], flat(banks(e)), sig_in[:, e], ALU.mult).then_inc(gated, 1)

                with dve.Fori(0, KT // 2 - 1) as i:
                    for e in range(2):
                        gate_tile(2 * i + e, e, i)
                        split_next(2 * i + e + 2, e, i + 1)
                for e in range(2):
                    gate_tile(KT - 2 + e, e, KT // 2 - 1)
                barrier(dve, 6 + r)

            for k in range(KT):
                dve.wait_ge(wo_hi_ready, k + 1)
                dve.tensor_tensor(wo_lo[:, k, :], wo_in[:, k % 2], wo_hi[:, k, :].bitcast(F32), ALU.subtract).then_inc(wo_ready, 1)

            def split_tokens(n, e):
                dve.wait_ge(m_hi_ready, n + 1)
                dve.tensor_tensor(m_lo[e][:, :, :], m_in[e][:, :, :], m_hi[e][:, :, :].bitcast(F32), ALU.subtract).then_inc(m_ready, 1)

            with dve.Fori(0, T // P // 2) as i:
                for e in range(2):
                    n = 2 * i + e
                    split_tokens(n, e)
                    dve.wait_ge(sd7_ready, n + 1)
                    dve.reciprocal(fin_s[e][:, 2:3], fin_s[e][:, 1:2]).then_inc(rs7_ready, 1)
                    dve.wait_ge(rs7_ready, n + 1)
                    dve.wait_ge(fin_free[e], i + 1)
                    dve.scalar_tensor_tensor(fin[e][:, :], flat(ps[:, 2 * e:2 * e + 2]), fin_s[e][:, 2:3], gate_row[:, :],
                                             ALU.mult, ALU.mult).then_inc(normed7, 1)
            barrier(dve, 8)

        @block.gpsimd
        def _(pool):
            pool.memset(rows[:, :], 0.0).then_inc(rows_cleared, 1)
            pool.memset(ones[:, :], 1.0)
            pool.memset(eps_col[:, :], EPS)
            pool.memset(one_col[:, :], 1.0)
            pool.memset(mid[:, :, :], 0.0)
            pool.memset(tot[:, :, :], 0.0)
            pool.memset(edge[:, :, :], 1.0).then_inc(pool_consts, 1)
            pool.wait_ge(pool_consts, 1)
            pool.affine_select(out=ident[:, :], in_=ones[:, :], compare_op=ALU.is_equal, fill=0.0, base=0,
                               pattern=[[-1, P]], channel_multiplier=1).then_inc(consts_ready, 1)
            pool.affine_select(out=later[:, :], in_=ones[:, :], compare_op=ALU.is_gt, fill=0.0, base=0,
                               pattern=[[-1, P]], channel_multiplier=1)
            for g, w in enumerate(WINDOWS):
                for t in range(w // 2):
                    pool.memset(edge[:, g, t:t + 1], w / (t + w // 2))
                for r in range(1, w // 2):
                    pool.memset(edge[:, g, 2 * PAD - r:2 * PAD - r + 1], w / (r + w // 2))
            for g in range(4):
                for k in range(KT):
                    n = KT * g + k
                    pool.wait_ge(hi_ready, n + 1)
                    pool.wait_ge(full_ready, n + 1)
                    cols = slice(512 * g, 512 * g + 512)
                    pool.tensor_tensor(h_lo[:, k, cols], h_full[:, n % 2], h_hi[:, k, cols].bitcast(F32),
                                       ALU.subtract).then_inc(lo_ready, 1)
            barrier(pool, 1)

            pool.memset(gk_up[:, :, :], 0.0).then_inc(gk_cleared, 1)
            pool.memset(dec_in[:, :, 0:1], 0.0)
            pool.memset(run_on[:, :, :], 1.0).then_inc(pool_consts, 1)
            pool.wait_ge(pool_consts, 2)
            pool.memset(run_on[:, :, 0:1], 0.0).then_inc(pool_consts, 1)
            def store(dst, t_slot, count):
                pool.dma_start(dst, tile_out[:, t_slot]).then_inc(tile_stored[t_slot], 16)
                pool.wait_ge(tile_stored[t_slot], 16 * count)
                pool.sem_inc(tile_free[t_slot], 1)

            pool.wait_ge(tile_ready, 1)
            store(proj[M_LR], 0, 1)
            with pool.Fori(0, HEADS) as h:
                for e in range(2):
                    pool.wait_ge(tile_ready, 2 * h + e + 2)
                    store(proj[(M_Q, M_K)[e] + h], 1 - e, h + e + 1)
            with pool.Fori(0, HEADS) as h:
                with pool.Fori(0, 2) as s2:
                    j = 2 * h + s2

                    def store_tile(t):
                        name = TILES[t]
                        if name in ("p_gate", "gla_gate"):
                            pool.wait_ge(tile_scaled, 2 * j + t // 2 + 1)
                        else:
                            pool.wait_ge(tile_ready, QK_USES + WTILES * j + t + 1)
                        a = tile_out[:, slot(t)]
                        if name == "v":
                            dst = v_ch[ds(NB * h, NB), s2].rearrange("b p t -> p b t")
                            a = a.rearrange("p (b t) -> p b t", t=512)
                        elif name == "gla_gate":
                            dst = gate_ch[ds(UPH * h, UPH), s2].rearrange("b p t -> p b t")
                            a = a.rearrange("p (b t) -> p b t", t=UNIT)
                        else:
                            dst = proj[TILE_AT[name] + j]
                        pool.dma_start(dst, a).then_inc(tile_stored[slot(t)], 16)
                        pool.wait_ge(tile_stored[slot(t)], 16 * in_slot(t, j, WTILES) + 16)
                        pool.sem_inc(tile_free[slot(t)], 1)

                    def apply_decay(d):
                        n = 2 * j + d
                        pool.wait_ge(exps_ready, n + 1)
                        pool.wait_ge(q_loaded, 16 * j + 16)
                        pool.wait_ge(k_loaded, 16 * j + 16)
                        pool.tensor_tensor(q_dec[:, :], q_dec[:, :], q_half[:, :], ALU.mult)
                        pool.tensor_tensor(k_dec[:, :], k_dec[:, :], k_half[:, :], ALU.mult).then_inc(decayed_ready, 1)
                        pool.wait_ge(decayed_ready, START + n + 1)
                        for a, src, stored in ((d, q_dec, qd_stored), (2 + d, k_dec, kd_stored)):
                            pool.dma_start(decayed[ds(HU * j, HU), :, a, :].rearrange("u p t -> p u t"),
                                           src[:, :].rearrange("p (u t) -> p u t", t=UNIT)).then_inc(stored, 16)
                        pool.wait_ge(qd_stored, 16 * n + 16)
                        pool.wait_ge(kd_stored, 16 * n + 16)
                        pool.sem_inc(decay_free, 1)

                    store_tile(0)
                    store_tile(1)
                    apply_decay(0)
                    store_tile(2)
                    store_tile(3)
                    apply_decay(1)
                    store_tile(4)
                    store_tile(5)
            barrier(pool, 2)

            barrier(pool, 3)

            with pool.Fori(0, UNITS // 2) as i:
                for e in range(2):
                    n = 2 * i + e
                    pool.wait_ge(sq_ready, n + 1)
                    pool.wait_ge(norm_summed, START + n - 1)
                    pool.tensor_tensor(o_ss[e][:, :], o_sq[e][:, 0, :], o_sq[e][:, 1, :], ALU.add).then_inc(ss_ready, 1)
                for e in range(2):
                    n = 2 * i + e
                    pool.wait_ge(on_ready, START + n + 1)
                    pool.wait_ge(unit_loaded[e], 64 * i + 64)
                    pool.wait_ge(og_stored[e], 16 * i + 16)
                    pool.tensor_tensor(o_g[e][:, :, :], o_n[e][:, :, :], gate_u[e][:, :, :], ALU.mult).then_inc(og_ready, 1)
            barrier(pool, 4)

            for s in range(2):
                pool.memset(u_pad[s][:, :, 0:PAD], 0.0)
                pool.memset(u_pad[s][:, :, PAD + T:], 0.0).then_inc(pads_cleared, 1)
            for g in range(GROUPS):
                pool_half(pool, g, 1)
                for dh in range(2):
                    pool.wait_ge(pa_ready, 2 * g + dh + 1)
                    pool.dma_start(pool_out[2 * g + dh], pa_out[:, dh]).then_inc(pa_stored[dh], 16)
            for dh in range(2):
                pool.wait_ge(pa_stored[dh], 16 * GROUPS)
            barrier(pool, 5)

            for r, dst in enumerate((y_pool, merged)):
                with pool.Fori(0, KT // 2) as i:
                    for e in range(2):
                        m = 2 * i + e
                        pool.wait_ge(gated, START + KT * r + m + 1)
                        if r == 1:
                            pool.wait_ge(y_loaded[e], 16 * i + 16)
                            pool.tensor_tensor(y_out[:, e], y_out[:, e], src_in[:, e], ALU.add).then_inc(summed, 1)
                            pool.wait_ge(summed, START + m + 1)
                        pool.dma_start(dst[m], y_out[:, e]).then_inc(y_stored[e], 16)
                        pool.wait_ge(y_stored[e], 16 * (KT // 2) * r + 16 * i + 16)
                        pool.sem_inc(y_free[e], 1)
                barrier(pool, 6 + r)

            with pool.Fori(0, T // P // 2) as i:
                for e in range(2):
                    n = 2 * i + e
                    pool.wait_ge(normed7, START + n + 1)
                    pool.wait_ge(x7_loaded[e], 16 * i + 16)
                    pool.tensor_tensor(fin[e][:, :], fin[e][:, :], x_in[e][:, :], ALU.add).then_inc(fin_ready, 1)
                    pool.wait_ge(fin_ready, START + n + 1)
                    pool.dma_start(out[0, ds(P * n, P), :], fin[e][:, :]).then_inc(out_stored[e], 16)
                    pool.wait_ge(out_stored[e], 16 * i + 16)
                    pool.sem_inc(fin_free[e], 1)
            barrier(pool, 8)

_INS = ["x", "c", "w_ada", "b_ada", "g_pre", "g_post", "w_in", "pool_w", "pool_scale", "gk_up_fwd", "gk_bias_fwd",
        "gk_up_bwd", "gk_bias_bwd", "gla_norm_g", "w_proj_pool", "w_proj_gla", "w_out"]


def kernel(**inputs):
    import numpy as _np
    import concourse.bacc as _bacc
    from concourse import mybir as _mybir
    from concourse.bass_utils import run_bass_kernel_spmd as _run

    nc = _bacc.Bacc("TRN2", target_bir_lowering=False, num_devices=1)
    arrays, args = {}, []
    for name in _INS:
        a = _np.ascontiguousarray(inputs[name])
        arrays[f"in_{name}"] = a
        args.append(nc.dram_tensor(f"in_{name}", a.shape, _mybir.dt.from_np(a.dtype), kind="ExternalInput").ap())
    out = nc.dram_tensor("out_0", (1, T, D), F32, kind="ExternalOutput").ap()
    build(nc, *args, out)
    r = _run(nc, [arrays], core_ids=[0])
    return r.results[0]["out_0"]
```

```python
import numpy as np

import concourse.bass as bass
from concourse import mybir

F32 = mybir.dt.float32
F32R = mybir.dt.float32r
BF16 = mybir.dt.bfloat16
I32 = mybir.dt.int32
ALU = mybir.AluOpType
ACT = mybir.ActivationFunctionType
ds = bass.ds

P = 128
T = 2048
D = 1024
KT = D // P
NB = T // 512
HEADS = 4
RANK = 16
NORMALIZER = 16.0
UNIT = 128
UPH = T // UNIT
UNITS = HEADS * UPH
HALF = T // 2
HU = HALF // UNIT
EPS = 1e-6
GROUPS = 4
WINDOWS = (2, 4, 8, 16)
PAD = max(WINDOWS) // 2
HEAD_V = 256

C_PIN, C_PGATE, C_Q, C_K, C_V, C_GGATE = 0, 1024, 2048, 2560, 3072, 4096
C_LR, C_BGP, C_BGG = 5120, 5152, 6176
M_PIN, M_PGATE, M_BGP, M_BGG, M_Q, M_K, M_LR = 0, 8, 16, 24, 32, 36, 40
M_ALL = 41
V_C, V_BADA, V_GPRE, V_PSCALE, V_GKB, V_GNORM, V_GPOST = 0, 8, 32, 40, 48, 56, 58
V_ROWS = 66
START = 2
ENGINES = 5


def build(nc, x, c, w_ada, b_ada, g_pre, g_post, w_in, pool_w, pool_scale, gk_up_fwd, gk_bias_fwd,
          gk_up_bwd, gk_bias_bwd, gla_norm_g, w_proj_pool, w_proj_gla, w_out, out):
    base = (nc.sbuf_base + 63) // 64 * 64
    limit = nc.sbuf_usable_end

    class Region:

        def __init__(self, at):
            self.at = at

        def __call__(self, name, shape, dtype=F32):
            size = 2 if dtype == BF16 else 4
            n = size * int(np.prod(shape[1:]))
            t = nc.alloc_sbuf_tensor_at(name, shape, dtype, offset=self.at)
            self.at += (n + 31) // 32 * 32
            assert self.at <= limit, (name, self.at, limit)
            return t.ap()

    def sem(name):
        return nc.alloc_semaphore(name)

    proj = nc.dram_tensor("proj", (M_ALL, P, T), F32).ap()
    decayed = nc.dram_tensor("decayed", (UNITS, P, 4, UNIT), F32).ap()
    v_ch = nc.dram_tensor("v_ch", (HEADS * NB, 2, P, 512), F32).ap()
    gate_ch = nc.dram_tensor("gate_ch", (HEADS * NB, 2, P, 512), F32).ap()
    gla_out = nc.dram_tensor("gla_out", (HEADS * NB, 2, P, 512), F32).ap()
    pooled_ch = nc.dram_tensor("pooled_ch", (KT, P, T), F32).ap()
    y_pool = nc.dram_tensor("y_pool", (KT, P, T), F32).ap()
    merged = nc.dram_tensor("merged", (KT, P, T), F32).ap()

    keep = Region(base)
    ident = keep("ident", [P, P])
    ones = keep("ones", [P, P])
    later = keep("later", [P, P], I32)
    vecs = keep("vecs", [P, P])
    gnorm8 = keep("gnorm8", [P, KT])
    c_act = keep("c_act", [P, KT])
    h_scale = keep("h_scale", [P, KT])
    h_shift = keep("h_shift", [P, KT])
    eps_col = keep("eps_col", [P, 1])
    one_col = keep("one_col", [P, 1])
    mid = keep("mid", [P, 2, UNITS + 2])
    tot = keep("tot", [P, 2, UNITS + 2])
    edge = keep("edge", [P, GROUPS, 2 * PAD])
    weights_at = keep.at
    stage = keep("stage", [P, 2, KT, P])
    w_hi = [keep(f"w_hi{s}", [P, KT, P], F32R) for s in range(2)]
    w_lo = [keep(f"w_lo{s}", [P, KT, P], F32R) for s in range(2)]
    low = keep.at

    big = Region(low)
    h_hi = big("h_hi", [P, KT, T], F32R)
    h_lo = big("h_lo", [P, KT, T], F32R)
    above = big.at

    r0 = Region(above)
    rows = Region(low + 4 * KT * T)("rows", [P, P])
    ada_w = r0("ada_w", [P, 2, KT, 256])
    xin = r0("xin", [P, 2, 4, D])
    h_full = r0("h_full", [P, 2, 512])
    sumsq = r0("sumsq", [P, T // P])
    rstd = r0("rstd", [P, T // P])

    r1 = Region(above)
    tile_out = r1("tile_out", [P, 2, T])
    lr_half = r1("lr_half", [2 * RANK, HALF])
    gk_up = r1("gk_up", [2 * RANK, 2, P])
    q_half = r1("q_half", [P, HALF])
    k_half = r1("k_half", [P, HALF])
    dec_a = r1("dec_a", [P, HALF])
    dec_in = r1("dec_in", [P, HU, UNIT + 1])
    dec_sum = r1("dec_sum", [P, HU, UNIT + 1])
    run_on = r1("run_on", [P, HU, UNIT + 1], BF16)
    q_dec = r1("q_dec", [P, HALF])
    k_dec = r1("k_dec", [P, HALF])

    into = Region(limit // 64 * 64 - 4 * D - 512)("into", [P, 2, UNITS])

    h_size = 2 * 4 * KT * T
    held = Region(low)
    v_all = held("v_all", [P, UNITS, HEAD_V])
    sb_all = held("sb_all", [P, UNITS, HEAD_V])
    assert held.at == low + h_size
    inputs3 = Region(held.at)
    dec_u = [inputs3(f"dec_u{s}", [P, 4, 4, UNIT]) for s in range(2)]
    gate_u = [inputs3(f"gate_u{s}", [P, 2, 512]) for s in range(2)]

    r2 = Region(inputs3.at)
    kb_in = [r2(f"kb_in{s}", [P, 4, UNIT]) for s in range(2)]
    vt_in = [r2(f"vt_in{s}", [P, 2, 512]) for s in range(2)]
    kb_tok = [r2(f"kb_tok{s}", [P, P]) for s in range(2)]
    zb = [r2(f"zb{s}", [P, HEAD_V]) for s in range(2)]
    into_tmp = r2("into_tmp", [P, 2, UNITS])
    gate_w = r2("gate_w", [P, 2, KT, P])
    gate_wide = gate_w[:, 0]
    gate_col = r2("gate_col", [P, KT])

    r3 = Region(inputs3.at)
    o_g = [r3(f"o_g{s}", [P, 2, 512]) for s in range(2)]
    kf_tok = [r3(f"kf_tok{s}", [P, P]) for s in range(2)]
    score = [r3(f"score{s}", [P, UNIT]) for s in range(2)]
    sf = [r3(f"sf{s}", [P, HEAD_V]) for s in range(2)]
    zf = [r3(f"zf{s}", [P, HEAD_V]) for s in range(2)]
    o_sq = [r3(f"o_sq{s}", [P, HEAD_V]) for s in range(2)]
    o_n = [r3(f"o_n{s}", [P, HEAD_V]) for s in range(2)]
    o_ss = [r3(f"o_ss{s}", [P, 8]) for s in range(2)]
    assert max(r2.at, r3.at) <= limit // 64 * 64 - 4 * D - 512

    WIDE = HALF + 2 * PAD
    rp = Region(weights_at)
    pu = [rp(f"pu{s}", [P, WIDE]) for s in range(3)]
    psum2 = [rp(f"psum2_{s}", [P, WIDE]) for s in range(2)]
    assert rp.at <= low

    gate_row = Region(limit // 64 * 64 - 4 * D)("gate_row", [P, D])

    r4 = Region(above)
    pooled_in = [r4(f"pooled_in{s}", [P, 2, 512]) for s in range(2)]
    pooled_hi = [r4(f"pooled_hi{s}", [P, 2, 512], F32R) for s in range(2)]
    pooled_lo = [r4(f"pooled_lo{s}", [P, 2, 512], F32R) for s in range(2)]
    pg_in = [r4(f"pg_in{s}", [P, 2, 512]) for s in range(2)]
    pa = [r4(f"pa{s}", [P, 2, 512]) for s in range(2)]
    pw_in = r4("pw_in", [P, 2, 256])
    pw_hi = r4("pw_hi", [P, 2, 256], F32R)
    pw_lo = r4("pw_lo", [P, 2, 256], F32R)
    assert r4.at <= limit // 64 * 64 - 4 * D

    r5 = Region(above)
    src_in = r5("src_in", [P, 2, T])
    y_out = r5("y_out", [P, 2, T])
    sig_in = r5("sig_in", [P, 2, T])

    r7 = Region(low)
    wo_hi = r7("wo_hi", [P, KT, D], F32R)
    wo_lo = r7("wo_lo", [P, KT, D], F32R)
    wo_in = r7("wo_in", [P, 2, D])
    m_in = [r7(f"m_in{s}", [P, KT, P]) for s in range(2)]
    m_hi = [r7(f"m_hi{s}", [P, KT, P], F32R) for s in range(2)]
    m_lo = [r7(f"m_lo{s}", [P, KT, P], F32R) for s in range(2)]
    x_in = [r7(f"x_in{s}", [P, D]) for s in range(2)]
    fin = [r7(f"fin{s}", [P, D]) for s in range(2)]
    fin_sq = [r7(f"fin_sq{s}", [P, D]) for s in range(2)]
    fin_s = [r7(f"fin_s{s}", [P, 4]) for s in range(2)]

    ps = nc.alloc_psum_tensor("ps", [P, 8, 512], F32).ap()

    step_done, cleared, passed = sem("step_done"), sem("cleared"), sem("passed")
    swept, credits_given = sem("swept"), sem("credits_given")
    early = []

    def sem01(name):
        early.append(nc.alloc_semaphore(name))
        return early[-1]

    unused = iter(early)

    def again(name):
        return next(unused)

    consts_ready = sem01("consts_ready")
    rows_loaded = sem01("rows_loaded")
    rows_cleared = sem01("rows_cleared")
    vecs_turned, vecs_ready, c_ready = sem01("vecs_turned"), sem01("vecs_ready"), sem01("c_ready")
    ada_loaded = [sem01(f"ada_loaded{s}") for s in range(2)]
    ada_used, ada_ready, mod_part, mod_ready = sem01("ada_used"), sem01("ada_ready"), sem01("mod_part"), sem01("mod_ready")
    x_loaded = [sem01(f"x_loaded{s}") for s in range(2)]
    sumsq_ready, var_ready, std_ready, rstd_ready = sem01("sumsq_ready"), sem01("var_ready"), sem01("std_ready"), sem01("rstd_ready")
    xn_ready, x_turned, x_used = sem01("xn_ready"), sem01("x_turned"), sem01("x_used")
    hi_ready, full_ready, lo_ready = sem01("hi_ready"), sem01("full_ready"), sem01("lo_ready")

    w_loaded = [sem01(f"w_loaded{s}") for s in range(2)]
    w_hi_ready = sem01("w_hi_ready")
    w_ready = sem01("w_ready")
    product_done = sem01("product_done")
    ps_free = [sem01(f"ps_free{s}") for s in range(2)]
    tile_ready, tile_scaled = sem01("tile_ready"), sem01("tile_scaled")
    tile_stored = [sem(f"tile_stored{s}") for s in range(2)]
    tile_free = [sem01(f"tile_free{s}") for s in range(2)]
    decay_free = sem01("decay_free")
    lr_loaded, gk_loaded, q_loaded, k_loaded = sem01("lr_loaded"), sem01("gk_loaded"), sem01("q_loaded"), sem01("k_loaded")
    gk_cleared = sem01("gk_cleared")
    abs_done, expneg_done, logsig_ready = sem01("abs_done"), sem01("expneg_done"), sem01("logsig_ready")
    min_done, la_done, scan_done, centred = sem01("min_done"), sem01("la_done"), sem01("scan_done"), sem01("centred")
    exps_ready, decayed_ready = sem01("exps_ready"), sem01("decayed_ready")
    qd_stored, kd_stored = sem("qd_stored"), sem("kd_stored")

    def barrier(eng, step):
        eng.drain().then_inc(step_done, 1)
        eng.wait_ge(step_done, ENGINES * (step if step < 3 else step - 1))
        if step == 4:
            if eng.engine == nc.sync.engine:
                for s in early:
                    eng.sem_clear(s).then_inc(cleared, 1)
            eng.wait_ge(cleared, len(early))
            eng.sem_inc(passed, 1)

    def sweep_barrier(eng):
        eng.drain().then_inc(swept, 1)
        eng.wait_ge(swept, ENGINES - 1)

    def wait_apart(eng, *waits):
        for s, v in waits:
            eng.wait_ge(s, v)
        eng.sem_inc(passed, 1)

    def split_product(pe, banks, lhs_hi, lhs_lo, rhs_hi, rhs_lo, k, first_k, last_k):
        for b in range(NB):
            pe.matmul(banks[:, b], lhs_hi, rhs_hi[:, k, ds(512 * b, 512)], start=first_k, stop=False)
        for b in range(NB):
            pe.matmul(banks[:, b], lhs_hi, rhs_lo[:, k, ds(512 * b, 512)], start=False, stop=False)
        for b in range(NB):
            last = pe.matmul(banks[:, b], lhs_lo, rhs_hi[:, k, ds(512 * b, 512)], start=False, stop=last_k)
        return last

    kb_loaded = [sem01(f"kb_loaded{s}") for s in range(2)]
    gate_loaded = [sem01(f"gate_loaded{s}") for s in range(2)]
    gate_product, gate_sum, gate_wide_ready, gate_spread = (sem01(n) for n in (
        "gate_product", "gate_sum", "gate_wide_ready", "gate_spread"))
    into_sum, into_ready = sem01("into_sum"), sem01("into_ready")
    kv_turned, kv_copied, kv_product = sem01("kv_turned"), sem01("kv_copied"), sem01("kv_product")
    zb_ready = sem01("zb_ready")
    zb_cleared, zf_cleared, pool_consts = sem01("zb_cleared"), sem01("zf_cleared"), sem01("pool_consts")
    pu_loaded = [sem(f"pu_loaded{s}") for s in range(3)]
    pu_stored = [sem(f"pu_stored{s}") for s in range(3)]
    pool_step = sem("pool_step")
    group_loaded = [sem(f"group_loaded{s}") for s in range(2)]
    scores_done, attn_done = sem("scores_done"), sem("attn_done")
    states_product = sem("states_product")
    kf_copied, score_copied, score_ready = sem("kf_copied"), sem("score_copied"), sem("score_ready")
    sf_ready, zf_ready = sem("sf_ready"), sem("zf_ready")
    ss_ready, sd_ready, rs_ready, normed, o_turned, og_ready = (sem(n) for n in (
        "ss_ready", "sd_ready", "rs_ready", "normed", "o_turned", "og_ready"))
    og_stored = [sem(f"og_stored{s}") for s in range(2)]
    pooled_loaded = [again(f"pooled_loaded{s}") for s in range(2)]
    pg_loaded = [again(f"pg_loaded{s}") for s in range(2)]
    pw_loaded, pw_hi_ready, pw_ready = again("pw_loaded"), again("pw_hi_ready"), again("pw_ready")
    pooled_hi_ready, pooled_ready, pool_product = again("pooled_hi_ready"), again("pooled_ready"), again("pool_product")
    pa_ready, pa_hi_ready, pa_split = again("pa_ready"), again("pa_hi_ready"), again("pa_split")

    src_loaded = [again(f"src_loaded{e}") for e in range(2)]
    src_hi, src_ready = again("src_hi"), again("src_ready")
    pj_loaded = [again(f"pj_loaded{e}") for e in range(2)]
    pj_hi_ready, pj_ready, pj_product = again("pj_hi_ready"), again("pj_ready"), again("pj_product")
    sig_loaded = [again(f"sig_loaded{e}") for e in range(2)]
    y_loaded = [again(f"y_loaded{e}") for e in range(2)]
    gated, summed = again("gated"), again("summed")
    y_stored = [sem(f"y_stored{e}") for e in range(2)]
    y_free = [again(f"y_free{e}") for e in range(2)]
    wo_loaded = [again(f"wo_loaded{s}") for s in range(2)]
    wo_hi_ready, wo_ready = again("wo_hi_ready"), again("wo_ready")
    m_loaded = [again(f"m_loaded{s}") for s in range(2)]
    x7_loaded = [again(f"x7_loaded{s}") for s in range(2)]
    m_hi_ready, m_ready, out_product = again("m_hi_ready"), again("m_ready"), again("out_product")
    ss7_ready, var7_ready, sd7_ready, rs7_ready, normed7, fin_ready = (again(n) for n in (
        "ss7_ready", "var7_ready", "sd7_ready", "rs7_ready", "normed7", "fin_ready"))
    out_stored = [sem(f"out_stored{s}") for s in range(2)]
    fin_free = [again(f"fin_free{s}") for s in range(2)]

    QK_USES = 1 + 2 * HEADS
    CLASSES = ("p_in", "p_gate", "decay_fwd", "v", "gla_gate", "decay_bwd", "bg_pool", "bg_gla")
    TILES = [n for n in CLASSES if not n.startswith("decay")]
    COLUMN = {"p_in": C_PIN, "p_gate": C_PGATE, "v": C_V, "gla_gate": C_GGATE, "bg_pool": C_BGP, "bg_gla": C_BGG}
    TILE_AT = {"p_in": M_PIN, "p_gate": M_PGATE, "bg_pool": M_BGP, "bg_gla": M_BGG}
    FUNC = {"p_in": ACT.Copy, "p_gate": ACT.Silu, "v": ACT.Copy, "gla_gate": ACT.Silu,
            "bg_pool": ACT.Sigmoid, "bg_gla": ACT.Sigmoid}
    USES, WTILES = len(CLASSES), len(TILES)
    IN_SLOT = [(QK_USES + 1) // 2, QK_USES // 2]
    w_in_v = w_in[0].rearrange("(k p) n -> p k n", p=P)

    def slot(p):
        return (QK_USES + p) % 2

    def in_slot(p, j, each):
        return IN_SLOT[slot(p)] + (each // 2) * j + sum(slot(q) == slot(p) for q in range(p))

    def use_of(t):
        return CLASSES.index(TILES[t])

    def banks(s):
        return ps[:, 4 * s:4 * s + 4]

    def flat(a):
        return a.rearrange("p b n -> p (b n)")

    block = nc.Block()
    with block:

        @block.sync
        def _(sp):
            sp.wait_ge(rows_cleared, 1)
            for at, n, src in ((V_C, 8, c), (V_BADA, 24, b_ada), (V_GPRE, 8, g_pre), (V_PSCALE, 8, pool_scale),
                               (V_GKB, 4, gk_bias_fwd), (V_GKB + 4, 4, gk_bias_bwd), (V_GNORM, 2, gla_norm_g), (V_GPOST, 8, g_post)):
                sp.dma_start(rows[at:at + n, :], src.rearrange("o (r p) -> (o r) p", p=P)).then_inc(rows_loaded, 16)
            ada_v = w_ada[0].rearrange("(k p) n -> p k n", p=P)
            x_v = x[0].rearrange("(g t p) n -> g p t n", t=4, p=P)
            for n in range(8):
                if n >= 2:
                    sp.wait_ge(ada_used, n - 1)
                sp.dma_start(ada_w[:, n % 2], ada_v[:, :, 256 * n:256 * n + 256]).then_inc(ada_loaded[n % 2], 16)
                if n in (3, 5):
                    g = n // 2 - 1
                    sp.dma_start(xin[:, g], x_v[g]).then_inc(x_loaded[g], 16)
            sp.dma_start(stage[:, 0], w_in_v[:, :, C_LR:C_LR + P]).then_inc(w_loaded[0], 16)
            for g in range(2, 4):
                sp.wait_ge(x_turned, KT * (g - 1))
                sp.dma_start(xin[:, g % 2], x_v[g]).then_inc(x_loaded[g % 2], 16)
            barrier(sp, 1)

            with sp.Fori(0, HEADS) as h:
                sp.wait_ge(w_ready, START + 2 * h)
                sp.dma_start(stage[:, 1], w_in_v[:, :, ds(C_Q + P * h, P)]).then_inc(w_loaded[1], 16)
                sp.wait_ge(w_ready, START + 2 * h + 1)
                sp.dma_start(stage[:, 0], w_in_v[:, :, ds(C_K + P * h, P)]).then_inc(w_loaded[0], 16)
            def load_tile(t, j):
                sp.wait_ge(w_ready, START + QK_USES + WTILES * j + t - 1)
                sp.dma_start(stage[:, slot(t)], w_in_v[:, :, ds(COLUMN[TILES[t]] + P * j, P)]).then_inc(w_loaded[slot(t)], 16)

            with sp.Fori(0, HEADS) as h:
                with sp.Fori(0, 2) as s:
                    j = 2 * h + s
                    load_tile(0, j)
                    load_tile(1, j)
                    sp.wait_ge(tile_stored[0], 16 * IN_SLOT[0])
                    sp.wait_ge(tile_stored[1], 16 * IN_SLOT[1])
                    sp.wait_ge(product_done, START + QK_USES + USES * j - USES + CLASSES.index("decay_bwd") + 1)
                    sp.dma_start(lr_half[:, :], proj[M_LR, 0:2 * RANK, ds(HALF * s, HALF)]).then_inc(lr_loaded, 16)
                    sp.wait_ge(gk_cleared, 1)
                    sp.dma_start(gk_up[0:RANK, 0, :], gk_up_fwd[0, :, ds(P * h, P)]).then_inc(gk_loaded, 16)
                    sp.dma_start(gk_up[RANK:2 * RANK, 1, :], gk_up_bwd[0, :, ds(P * h, P)]).then_inc(gk_loaded, 16)
                    sp.wait_ge(decayed_ready, START + 2 * j)
                    sp.dma_start(q_half[:, :], proj[M_Q + h, :, ds(HALF * s, HALF)]).then_inc(q_loaded, 16)
                    sp.dma_start(k_half[:, :], proj[M_K + h, :, ds(HALF * s, HALF)]).then_inc(k_loaded, 16)
                    for t in range(2, WTILES):
                        load_tile(t, j)
            barrier(sp, 2)

            def load_group(b, g, back):
                if back is not None:
                    wait_apart(sp, (kv_turned, back))
                n = 2 * HEADS * 2 - 1 - g - 2 * b
                sp.dma_start(kb_in[g][:, :, :], decayed[ds(4 * n, 4), :, 3, :].rearrange("n p t -> p n t")).then_inc(kb_loaded[g], 16)
                sp.dma_start(vt_in[g][:, :, :], v_ch[n].rearrange("a p t -> p a t")).then_inc(kb_loaded[g], 16)

            load_group(0, 0, None)
            load_group(0, 1, None)
            for m in range(2):
                sp.dma_start(gate_w[:, m], ada_v[:, :, 2 * D + P * m:2 * D + P * m + P]).then_inc(gate_loaded[m], 16)
            with sp.Fori(0, UNITS // 8 - 1) as b:
                for g in range(2):
                    load_group(b + 1, g, 8 * b + 4 * g + 4)

            def load_units(n, g):
                sp.dma_start(dec_u[g][:, :, :, :], decayed[ds(4 * n, 4)].rearrange("n p a t -> p n a t")).then_inc(group_loaded[g], 16)
                sp.dma_start(gate_u[g][:, :, :], gate_ch[n].rearrange("a p t -> p a t")).then_inc(group_loaded[g], 16)

            def store_units(n, g):
                wait_apart(sp, (og_ready, START + 4 * n + 4))
                sp.dma_start(gla_out[n].rearrange("a p t -> p a t"), o_g[g][:, :, :]).then_inc(og_stored[g], 16)

            load_units(0, 0)
            load_units(1, 1)
            for m in range(2, KT):
                sp.wait_ge(gate_product, m - 1)
                sp.dma_start(gate_w[:, m % 2], ada_v[:, :, 2 * D + P * m:2 * D + P * m + P]).then_inc(gate_loaded[m % 2], 16)
            sweep_barrier(sp)

            with sp.Fori(0, UNITS // 8 - 1) as b:
                for g in range(2):
                    store_units(2 * b + g, g)
                    load_units(2 * b + g + 2, g)
            for g in range(2):
                store_units(UNITS // 4 - 2 + g, g)
            for g in range(2):
                sp.wait_ge(og_stored[g], 16 * (1 + UNITS // 8))
            barrier(sp, 4)

            def load_weights(r, m, e):
                wt_v = (w_proj_pool, w_proj_gla)[r][0].rearrange("(k p) n -> p k n", p=P)
                sp.dma_start(stage[:, e], wt_v[:, :, ds(P * m, P)]).then_inc(pj_loaded[e], 16)

            def load_pooled(g, b, s):
                sp.wait_ge(pooled_ready, START + NB * g + b - 1)
                sp.dma_start(pooled_in[s][:, :, :], pooled_ch[ds(2 * g, 2), :, 512 * b:512 * b + 512]
                             .rearrange("a p t -> p a t")).then_inc(pooled_loaded[s], 16)
                sp.wait_ge(pa_ready, START + NB * g + b - 1)
                sp.dma_start(pg_in[s][:, :, :], proj[ds(M_PGATE + 2 * g, 2), :, 512 * b:512 * b + 512]
                             .rearrange("a p t -> p a t")).then_inc(pg_loaded[s], 16)

            sp.wait_ge(credits_given, 1)
            with sp.Fori(0, GROUPS) as g:
                sp.wait_ge(pw_ready, g + 1)
                sp.dma_start(pw_in[:, :, :], pool_w[0, g].rearrange("(a p) n -> p a n", p=P)).then_inc(pw_loaded, 16)
                for b in range(NB):
                    load_pooled(g, b, b % 2)
            for e in range(2):
                load_weights(0, e, e)
            barrier(sp, 5)

            def load_gate(r, m, e):
                sp.wait_ge(gated, START + KT * r + m - 1)
                sp.dma_start(sig_in[:, e], proj[(M_BGP, M_BGG)[r] + m]).then_inc(sig_loaded[e], 16)
                if r == 1:
                    sp.wait_ge(summed, START + m - 1)
                    sp.dma_start(src_in[:, e], y_pool[m]).then_inc(y_loaded[e], 16)

            for r in range(2):
                if r == 1:
                    sp.wait_ge(src_ready, KT)
                    for e in range(2):
                        sp.wait_ge(y_stored[e], 16 * (KT // 2))
                for e in range(2):
                    load_gate(r, e, e)
                with sp.Fori(1, KT // 2) as i:
                    for e in range(2):
                        m = 2 * i + e
                        sp.wait_ge(pj_ready, KT * r + m - 1)
                        load_weights(r, m, e)
                        load_gate(r, m, e)
                if r == 0:
                    for e in range(2):
                        sp.wait_ge(pj_ready, KT + e - 1)
                        load_weights(1, e, e)
            barrier(sp, 6)

            wo_v = w_out[0].rearrange("(k p) n -> k p n", p=P)
            for k in range(KT):
                if k >= 2:
                    sp.wait_ge(wo_ready, k - 1)
                sp.dma_start(wo_in[:, k % 2], wo_v[k]).then_inc(wo_loaded[k % 2], 16)
            with sp.Fori(0, T // P // 2) as i:
                for e in range(2):
                    n = 2 * i + e
                    sp.wait_ge(m_ready, START + n - 1)
                    sp.dma_start(m_in[e][:, :, :], merged[:, :, ds(P * n, P)].rearrange("k p t -> p k t")).then_inc(m_loaded[e], 16)
                    sp.wait_ge(fin_ready, START + n - 1)
                    sp.dma_start(x_in[e][:, :], x[0, ds(P * n, P), :]).then_inc(x7_loaded[e], 16)
            barrier(sp, 7)

        @block.tensor
        def _(pe):
            pe.sem_inc(product_done, START)
            pe.wait_ge(consts_ready, 1)
            pe.wait_ge(rows_loaded, 16 * 8)
            pe.transpose(ps[:, 7, 0:P], rows[:, :], ident[:, :]).then_inc(vecs_turned, 1)
            pe.wait_ge(c_ready, 1)
            for n in range(8):
                pe.wait_ge(ada_loaded[n % 2], 16 * (n // 2 + 1))
                for m in range(2):
                    for k in range(KT):
                        last = pe.matmul(ps[:, 6, 2 * n + m:2 * n + m + 1], ada_w[:, n % 2, k, P * m:P * m + P],
                                         c_act[:, k:k + 1], start=(k == 0), stop=(k == KT - 1))
                last.then_inc(ada_used, 1)
            for g in range(4):
                pe.wait_ge(xn_ready, g + 1)
                for k in range(KT):
                    n = KT * g + k
                    if n >= 4:
                        pe.wait_ge(full_ready, n - 3)
                    for t in range(4):
                        last = pe.transpose(ps[:, n % 4, P * t:P * t + P], xin[:, g % 2, t, P * k:P * k + P], ident[:, :])
                    last.then_inc(x_turned, 1)
            barrier(pe, 1)

            def tile_product(s):
                for k in range(KT):
                    last = split_product(pe, banks(s), w_hi[s][:, k], w_lo[s][:, k], h_hi, h_lo, k, k == 0, k == KT - 1)
                last.then_inc(product_done, 1)

            pe.wait_ge(w_ready, START + 1)
            tile_product(0)
            with pe.Fori(0, HEADS) as h:
                for e in range(2):
                    s = 1 - e
                    pe.wait_ge(w_ready, START + 2 * h + e + 2)
                    pe.wait_ge(ps_free[s], h + e + 1)
                    tile_product(s)
            with pe.Fori(0, 2 * HEADS) as j:
                for p, name in enumerate(CLASSES):
                    s = slot(p)
                    pe.wait_ge(ps_free[s], in_slot(p, j, USES) + 1)
                    if name in TILES:
                        t = TILES.index(name)
                        pe.wait_ge(w_ready, START + QK_USES + WTILES * j + t + 1)
                        for k in range(KT):
                            last = split_product(pe, banks(s), w_hi[slot(t)][:, k], w_lo[slot(t)][:, k],
                                                 h_hi, h_lo, k, k == 0, k == KT - 1)
                    else:
                        d = int(name == "decay_bwd")
                        if d == 0:
                            pe.wait_ge(lr_loaded, 16 * j + 16)
                            pe.wait_ge(gk_loaded, 32 * j + 32)
                        for b in range(2):
                            last = pe.matmul(banks(s)[:, b], gk_up[:, d, :], lr_half[:, 512 * b:512 * b + 512],
                                             start=True, stop=True)
                    last.then_inc(product_done, 1)
            barrier(pe, 2)

            def kv_turn(n, g, q, s):
                pe.wait_ge(kv_copied, START + n - 1)
                pe.transpose(ps[:, s, 0:P], kb_in[g][:, q, :], ident[:, :])
                for half in range(2):
                    last = pe.transpose(ps[:, s, P + P * half:2 * P + P * half],
                                        vt_in[g][:, half, UNIT * q:UNIT * q + UNIT], ident[:, :])
                last.then_inc(kv_turned, 1)

            def kv_multiply(n, s):
                wait_apart(pe, (kv_copied, START + n + 1), (zb_ready, START + n - 1))
                pe.matmul(ps[:, 2 + s, 0:HEAD_V], kb_tok[s][:, :], v_all[:, UNITS - 1 - n, :],
                          start=True, stop=True).then_inc(kv_product, 1)

            with pe.Fori(0, 2 * HEADS) as b:
                for e in range(8):
                    if e in (0, 4):
                        pe.wait_ge(kb_loaded[e // 4], 32 * b + 32)
                    kv_turn(8 * b + e, e // 4, 3 - e % 4, e % 2)
                    if e:
                        kv_multiply(8 * b + e - 1, (e - 1) % 2)
                kv_multiply(8 * b + 7, 1)
            for m in range(KT):
                pe.wait_ge(gate_loaded[m % 2], 16 * (m // 2 + 1))
                for k in range(KT):
                    last = pe.matmul(ps[:, 4, m:m + 1], gate_w[:, m % 2, k, :], c_act[:, k:k + 1],
                                     start=(k == 0), stop=(k == KT - 1))
                last.then_inc(gate_product, 1)
            pe.wait_ge(gate_wide_ready, 1)
            for k in range(KT):
                last = pe.matmul(ps[:, 5 + k // 4, P * (k % 4):P * (k % 4) + P], gate_wide[:, k, :], ident[:, :],
                                 start=True, stop=True)
            last.then_inc(gate_spread, 1)
            sweep_barrier(pe)

            def scores(b, e):
                n, g, q, s = 8 * b + e, e // 4, e % 4, e % 2
                if q == 0:
                    pe.wait_ge(group_loaded[g], 32 * b + 32)
                pe.wait_ge(score_ready, START + n - 1)
                pe.transpose(ps[:, s, 0:P], dec_u[g][:, q, 2, :], ident[:, :])
                for d in range(2):
                    last = pe.matmul(ps[:, s, P + P * d:2 * P + P * d], dec_u[g][:, q, 2 + d, :], dec_u[g][:, q, d, :],
                                     start=True, stop=True)
                last.then_inc(scores_done, 1)

            def attend(b, e):
                n, g, q, s = 8 * b + e, e // 4, e % 4, e % 2
                pe.wait_ge(kf_copied, START + n + 1)
                pe.wait_ge(zf_ready, START + n - 1)
                pe.matmul(ps[:, 2 + s, 0:HEAD_V], kf_tok[s][:, :], v_all[:, n, :], start=True, stop=True).then_inc(states_product, 1)
                pe.wait_ge(normed, START + n - 1)
                o = ps[:, 4 + s, 0:HEAD_V]
                pe.matmul(o, dec_u[g][:, q, 1, :], sb_all[:, n, :], start=True, stop=False)
                pe.wait_ge(score_ready, START + n + 1)
                pe.matmul(o, score[s][:, :], v_all[:, n, :], start=False, stop=False)
                pe.wait_ge(sf_ready, START + n + 1)
                pe.matmul(o, dec_u[g][:, q, 0, :], sf[s][:, :], start=False, stop=True).then_inc(attn_done, 1)

            def turn(b, e):
                n, s = 8 * b + e, e % 2
                pe.wait_ge(normed, START + n + 1)
                pe.wait_ge(og_ready, START + n - 1)
                for half in range(2):
                    last = pe.transpose(ps[:, 6 + s, P * half:P * half + P], o_n[s][:, P * half:P * half + P], ident[:, :])
                last.then_inc(o_turned, 1)

            def units(b, first=False, last=False):
                for e in range(8):
                    if e < 7:
                        scores(b, e + 1)
                    elif not last:
                        scores(b + 1, 0)
                    attend(b, e)
                    if e:
                        turn(b, e - 1)
                    elif not first:
                        turn(b - 1, 7)

            scores(0, 0)
            units(0, first=True)
            with pe.Fori(1, UNITS // 8 - 1) as b:
                units(b)
            units(UNITS // 8 - 1, last=True)
            turn(UNITS // 8 - 1, 7)
            barrier(pe, 4)

            pe.wait_ge(credits_given, 1)
            with pe.Fori(0, GROUPS) as g:
                pe.wait_ge(pw_ready, g + 2)
                for b in range(NB):
                    s = b % 2
                    pe.wait_ge(pooled_ready, START + NB * g + b + 1)
                    pe.wait_ge(pa_ready, START + NB * g + b - 1)
                    for dh in range(2):
                        cols = slice(P * dh, P * dh + P)
                        bank = ps[:, 2 * s + dh]
                        for a in range(2):
                            pe.matmul(bank, pw_hi[:, a, cols], pooled_hi[s][:, a, :], start=(a == 0), stop=False)
                            pe.matmul(bank, pw_hi[:, a, cols], pooled_lo[s][:, a, :], start=False, stop=False)
                            last = pe.matmul(bank, pw_lo[:, a, cols], pooled_hi[s][:, a, :], start=False, stop=(a == 1))
                    last.then_inc(pool_product, 1)
            barrier(pe, 5)

            for r in range(2):
                with pe.Fori(0, KT // 2) as i:
                    for e in range(2):
                        m = 2 * i + e
                        pe.wait_ge(pj_ready, KT * r + m + 1)
                        pe.wait_ge(gated, START + KT * r + m - 1)
                        for k in range(KT):
                            if r == 1:
                                pe.wait_ge(src_ready, k + 1)
                            last = split_product(pe, banks(e), w_hi[e][:, k], w_lo[e][:, k], h_hi, h_lo, k, k == 0, k == KT - 1)
                        last.then_inc(pj_product, 1)
            barrier(pe, 6)

            with pe.Fori(0, T // P // 2) as i:
                for e in range(2):
                    n = 2 * i + e
                    pe.wait_ge(m_ready, START + n + 1)
                    pe.wait_ge(normed7, START + n - 1)
                    for k in range(KT):
                        pe.wait_ge(wo_ready, k + 1)
                        for lhs, rhs in ((m_hi, wo_hi), (m_hi, wo_lo), (m_lo, wo_hi)):
                            for b in range(2):
                                last = pe.matmul(ps[:, 2 * e + b], lhs[e][:, k, :], rhs[:, k, 512 * b:512 * b + 512],
                                                 start=(k == 0 and lhs is m_hi and rhs is wo_hi),
                                                 stop=(k == KT - 1 and lhs is m_lo))
                    last.then_inc(out_product, 1)
            barrier(pe, 7)

        @block.scalar
        def _(act):
            act.wait_ge(vecs_ready, 1)
            act.activation(c_act[:, :], vecs[:, V_C:V_C + KT], ACT.Silu).then_inc(c_ready, 1)
            for g in range(4):
                act.wait_ge(x_loaded[g % 2], 16 * (g // 2 + 1))
                for t in range(4):
                    if g or t:
                        act.wait_ge(sumsq_ready, 4 * g + t)
                    act.activation(flat(ps[:, 4:6]), xin[:, g % 2, t], ACT.Square,
                                   accum_out=sumsq[:, 4 * g + t:4 * g + t + 1]).then_inc(sumsq_ready, 1)
                act.wait_ge(var_ready, g + 1)
                act.activation(rstd[:, 4 * g:4 * g + 4], rstd[:, 4 * g:4 * g + 4], ACT.Sqrt).then_inc(std_ready, 1)
                for k in range(KT):
                    n = KT * g + k
                    act.wait_ge(full_ready, n + 1)
                    act.activation(h_hi[:, k, 512 * g:512 * g + 512], h_full[:, n % 2], ACT.Copy).then_inc(hi_ready, 1)
            barrier(act, 1)

            def evacuate(n_use, ps_slot, out_slot, stored, func, scale=1.0):
                act.wait_ge(product_done, START + n_use + 1)
                act.wait_ge(tile_free[out_slot], stored)
                act.activation(tile_out[:, out_slot], flat(banks(ps_slot)), func, scale=scale).then_inc(tile_ready, 1)

            evacuate(0, 0, 0, 1, ACT.Copy)
            act.wait_ge(tile_ready, 1)
            act.sem_inc(ps_free[0], 1)
            with act.Fori(0, HEADS) as h:
                for e in range(2):
                    evacuate(2 * h + e + 1, 1 - e, 1 - e, h + e + 1, ACT.Copy,
                             scale=float(P) ** -0.5 if e == 0 else 1.0)
                    act.wait_ge(tile_ready, 2 * h + e + 2)
                    act.sem_inc(ps_free[1 - e], 1)
            with act.Fori(0, HEADS) as h:
                with act.Fori(0, 2) as s2:
                    j = 2 * h + s2
                    for p, name in enumerate(CLASSES):
                        use = QK_USES + USES * j + p
                        if name in TILES:
                            t = TILES.index(name)
                            evacuate(use, slot(p), slot(t), in_slot(t, j, WTILES) + 1, FUNC[name])
                            act.wait_ge(tile_ready, QK_USES + WTILES * j + t + 1)
                            act.sem_inc(ps_free[slot(p)], 1)
                        else:
                            d = int(name == "decay_bwd")
                            z = flat(banks(slot(p))[:, 0:2])
                            act.wait_ge(product_done, START + use + 1)
                            act.activation(dec_a[:, :], z, ACT.Abs, bias=vecs[:, ds(V_GKB + HEADS * d + h, 1)]).then_inc(abs_done, 1)
                            act.wait_ge(abs_done, 2 * j + d + 1)
                            act.activation(dec_a[:, :], dec_a[:, :], ACT.Exp, scale=-1.0).then_inc(expneg_done, 1)
                            act.wait_ge(expneg_done, 2 * j + d + 1)
                            act.activation(dec_a[:, :], dec_a[:, :], ACT.Ln, bias=one_col[:, :]).then_inc(logsig_ready, 1)
                            act.wait_ge(centred, 2 * j + d + 1)
                            sign = (1.0 if d == 0 else -1.0) / NORMALIZER
                            act.wait_ge(decay_free, 2 * j + d + 1)
                            act.activation(q_dec[:, :], dec_a[:, :], ACT.Exp, scale=sign)
                            act.activation(k_dec[:, :], dec_a[:, :], ACT.Exp, scale=-sign).then_inc(exps_ready, 1)
            barrier(act, 2)

            for d in range(2):
                act.wait_ge(into_sum, 2 * d + 2)
                act.activation(into[:, d], into_tmp[:, d], ACT.Exp, scale=1.0 / NORMALIZER).then_inc(into_ready, 1)
            with act.Fori(0, UNITS // 2) as i:
                for e in range(2):
                    n = 2 * i + e
                    act.wait_ge(kv_turned, n + 1)
                    act.wait_ge(kv_product, START + n - 1)
                    act.activation(kb_tok[e][:, :], ps[:, e, 0:P], ACT.Copy)
                    act.activation(v_all[:, UNITS - 1 - n, :], ps[:, e, P:3 * P], ACT.Copy).then_inc(kv_copied, 1)
            sweep_barrier(act)

            def copies(b, e):
                n, s = 8 * b + e, e % 2
                act.wait_ge(scores_done, n + 1)
                act.wait_ge(states_product, START + n - 1)
                act.activation(kf_tok[s][:, :], ps[:, s, 0:P], ACT.Copy).then_inc(kf_copied, 1)
                act.wait_ge(attn_done, START + n - 1)
                act.activation(score[s][:, :], ps[:, s, P:2 * P], ACT.Copy).then_inc(score_copied, 1)
                act.wait_ge(zf_ready, START + n)
                act.activation(sf[s][:, :], zf[1 - s][:, :], ACT.Copy, scale=into[:, 0, ds(n, 1)]).then_inc(sf_ready, 1)

            def head_norm(b, e):
                n, s = 8 * b + e, e % 2
                act.wait_ge(attn_done, START + n + 1)
                act.wait_ge(rs_ready, START + n - 1)
                act.activation(o_sq[s][:, :], ps[:, 4 + s, 0:HEAD_V], ACT.Square, accum_out=o_ss[s][:, 0:1]).then_inc(ss_ready, 1)
                act.wait_ge(ss_ready, n + 1)
                act.activation(o_ss[s][:, 1:2], o_ss[s][:, 0:1], ACT.Sqrt, scale=1.0 / HEAD_V,
                               bias=eps_col[:, :]).then_inc(sd_ready, 1)

            def units(b, last=False):
                for e in range(8):
                    if e < 7:
                        copies(b, e + 1)
                    elif not last:
                        copies(b + 1, 0)
                    head_norm(b, e)

            act.wait_ge(zf_cleared, 1)
            copies(0, 0)
            with act.Fori(0, UNITS // 8 - 1) as b:
                units(b)
            units(UNITS // 8 - 1, last=True)
            barrier(act, 4)

            act.wait_ge(credits_given, 1)
            with act.Fori(0, GROUPS) as g:
                act.wait_ge(pw_loaded, 16 * g + 16)
                act.wait_ge(pool_product, START + NB * g)
                act.activation(pw_hi[:, :, :], pw_in[:, :, :], ACT.Copy).then_inc(pw_hi_ready, 1)

                def split_pooled(b):
                    s = b % 2
                    act.wait_ge(pooled_loaded[s], 32 * g + 16 * (b // 2) + 16)
                    act.wait_ge(pool_product, START + NB * g + b - 1)
                    act.activation(pooled_hi[s][:, :, :], pooled_in[s][:, :, :], ACT.Copy).then_inc(pooled_hi_ready, 1)

                def split_result(b):
                    act.wait_ge(pa_ready, START + NB * g + b + 1)
                    act.activation(h_hi[:, ds(2 * g, 2), 512 * b:512 * b + 512], pa[b % 2][:, :, :], ACT.Copy).then_inc(pa_hi_ready, 1)

                split_pooled(0)
                for b in range(1, NB):
                    split_pooled(b)
                    split_result(b - 1)
                split_result(NB - 1)
            def load_source(k):
                u = k // 2 * NB
                act.dma_start(src_in[:, k % 2].rearrange("p (u t) -> p u t", t=512),
                              gla_out[u:u + NB, k % 2].rearrange("u p t -> p u t")).then_inc(src_loaded[k % 2], 16)

            barrier(act, 5)

            for k in range(2):
                load_source(k)
            act.wait_ge(pj_product, KT)
            for k in range(KT):
                act.wait_ge(src_loaded[k % 2], 16 * (k // 2 + 1))
                act.activation(h_hi[:, k, :], src_in[:, k % 2], ACT.Copy).then_inc(src_hi, 1)
                if k + 2 < KT:
                    act.wait_ge(src_ready, k + 1)
                    load_source(k + 2)
            barrier(act, 6)

            for k in range(KT):
                act.wait_ge(wo_loaded[k % 2], 16 * (k // 2 + 1))
                act.activation(wo_hi[:, k, :], wo_in[:, k % 2], ACT.Copy).then_inc(wo_hi_ready, 1)
            with act.Fori(0, T // P // 2) as i:
                for e in range(2):
                    n = 2 * i + e
                    act.wait_ge(m_loaded[e], 16 * i + 16)
                    act.wait_ge(out_product, START + n - 1)
                    act.activation(m_hi[e][:, :, :], m_in[e][:, :, :], ACT.Copy).then_inc(m_hi_ready, 1)
                    act.wait_ge(out_product, START + n + 1)
                    act.activation(fin_sq[e][:, :], flat(ps[:, 2 * e:2 * e + 2]), ACT.Square,
                                   accum_out=fin_s[e][:, 0:1]).then_inc(ss7_ready, 1)
                    act.wait_ge(ss7_ready, n + 1)
                    act.activation(fin_s[e][:, 1:2], fin_s[e][:, 0:1], ACT.Sqrt, scale=1.0 / D,
                                   bias=eps_col[:, :]).then_inc(sd7_ready, 1)
            barrier(act, 7)

        @block.vector
        def _(dve):
            for s in (w_ready, decayed_ready, zb_ready, kv_copied, score_ready, kf_copied, zf_ready, normed,
                      o_turned, sd_ready, rs_ready, sf_ready, og_ready, attn_done, states_product, kv_product):
                dve.sem_inc(s, START)
            for s in (*ps_free, *tile_free, decay_free):
                dve.sem_inc(s, 1)
            for s in og_stored:
                dve.sem_inc(s, 16)
            dve.wait_ge(vecs_turned, 1)
            dve.tensor_copy(vecs[:, :], ps[:, 7, 0:P]).then_inc(vecs_ready, 1)
            dve.wait_ge(vecs_ready, 1)
            for r in range(KT // 2):
                dve.tensor_copy(gnorm8[:, 2 * r:2 * r + 2], vecs[:, V_GNORM:V_GNORM + 2])

            def inverse_rms(g):
                dve.wait_ge(sumsq_ready, 4 * g + 4)
                cols = slice(4 * g, 4 * g + 4)
                dve.tensor_scalar(rstd[:, cols], sumsq[:, cols], 1.0 / D, EPS, ALU.mult, ALU.add).then_inc(var_ready, 1)
                dve.wait_ge(std_ready, g + 1)
                dve.reciprocal(rstd[:, cols], rstd[:, cols]).then_inc(rstd_ready, 1)
                dve.wait_ge(rstd_ready, g + 1)
                for t in range(4):
                    last = dve.tensor_scalar(xin[:, g % 2, t], xin[:, g % 2, t], rstd[:, 4 * g + t:4 * g + t + 1], None, ALU.mult)
                last.then_inc(xn_ready, 1)

            inverse_rms(0)
            dve.wait_ge(ada_used, 8)
            dve.tensor_tensor(h_shift[:, :], ps[:, 6, 0:KT], vecs[:, V_BADA:V_BADA + KT], ALU.add).then_inc(mod_ready, 1)
            dve.scalar_tensor_tensor(h_scale[:, :], ps[:, 6, KT:2 * KT], 1.0, vecs[:, V_BADA + KT:V_BADA + 2 * KT],
                                     ALU.add, ALU.add).then_inc(mod_part, 1)
            dve.wait_ge(mod_part, 1)
            dve.tensor_tensor(h_scale[:, :], h_scale[:, :], vecs[:, V_GPRE:V_GPRE + KT], ALU.mult).then_inc(mod_ready, 1)
            dve.wait_ge(mod_ready, 2)
            for g in range(4):
                if g:
                    inverse_rms(g)
                for k in range(KT):
                    n = KT * g + k
                    dve.wait_ge(x_turned, n + 1)
                    if n >= 2:
                        dve.wait_ge(lo_ready, n - 1)
                    dve.tensor_scalar(h_full[:, n % 2], ps[:, n % 4], h_scale[:, k:k + 1], h_shift[:, k:k + 1],
                                      ALU.mult, ALU.add).then_inc(full_ready, 1)
            barrier(dve, 1)

            def split_weights(s, hi_sem, ready_sem, count):
                dve.tensor_copy(w_hi[s][:, :, :], stage[:, s]).then_inc(hi_sem, 1)
                dve.wait_ge(hi_sem, count + 1)
                dve.tensor_tensor(w_lo[s][:, :, :], stage[:, s], w_hi[s][:, :, :].bitcast(F32), ALU.subtract).then_inc(ready_sem, 1)

            dve.wait_ge(pool_consts, 3)
            dve.wait_ge(w_loaded[0], 16)
            split_weights(0, w_hi_ready, w_ready, 0)
            with dve.Fori(0, HEADS) as h:
                for e in range(2):
                    s = 1 - e
                    dve.wait_ge(product_done, START + 2 * h + e)
                    dve.wait_ge(w_loaded[s], 16 * h + 16 * e + 16)
                    split_weights(s, w_hi_ready, w_ready, 2 * h + e + 1)
            with dve.Fori(0, HEADS) as h:
                with dve.Fori(0, 2) as s2:
                    j = 2 * h + s2

                    def split_tile(t):
                        back = use_of(t - 2) + USES if t >= 2 else use_of(t + WTILES - 2)
                        dve.wait_ge(product_done, START + QK_USES + USES * j - USES + back + 1)
                        dve.wait_ge(w_loaded[slot(t)], 16 * in_slot(t, j, WTILES) + 16)
                        split_weights(slot(t), w_hi_ready, w_ready, QK_USES + WTILES * j + t)

                    def scale_tile(t, col):
                        dve.wait_ge(tile_ready, QK_USES + WTILES * j + t + 1)
                        dve.tensor_scalar(tile_out[:, slot(t)], tile_out[:, slot(t)], col, None, ALU.mult).then_inc(tile_scaled, 1)

                    def decay(d):
                        p = CLASSES.index(("decay_fwd", "decay_bwd")[d])
                        n = 2 * j + d
                        z = flat(banks(slot(p))[:, 0:2]).rearrange("p (u t) -> p u t", t=UNIT)
                        a = dec_a[:, :].rearrange("p (u t) -> p u t", t=UNIT)
                        dve.wait_ge(abs_done, n + 1)
                        dve.tensor_scalar(dec_in[:, :, 1:UNIT + 1], z, vecs[:, ds(V_GKB + HEADS * d + h, 1)], 0.0,
                                          ALU.add, ALU.min).then_inc(min_done, 1)
                        dve.wait_ge(min_done, n + 1)
                        dve.wait_ge(logsig_ready, n + 1)
                        dve.sem_inc(ps_free[slot(p)], 1)
                        dve.tensor_tensor(dec_in[:, :, 1:UNIT + 1], dec_in[:, :, 1:UNIT + 1], a, ALU.subtract).then_inc(la_done, 1)
                        dve.wait_ge(la_done, n + 1)
                        dve.tensor_tensor_scan(flat(dec_sum[:, :, :]), flat(run_on[:, :, :]), flat(dec_in[:, :, :]), 0.0,
                                               ALU.mult, ALU.add).then_inc(scan_done, 1)
                        dve.wait_ge(scan_done, n + 1)
                        dve.tensor_copy(mid[:, d, ds(HU * j + 1, HU)], dec_sum[:, :, UNIT // 2])
                        dve.tensor_copy(tot[:, d, ds(HU * j + 1, HU)], dec_sum[:, :, UNIT])
                        own = dec_sum[:, :, 1 - d:1 - d + UNIT]
                        dve.tensor_tensor(a, own, dec_sum[:, :, UNIT // 2:UNIT // 2 + 1].to_broadcast([P, HU, UNIT]),
                                          ALU.subtract).then_inc(centred, 1)

                    split_tile(0)
                    split_tile(1)
                    split_tile(2)
                    split_tile(3)
                    scale_tile(1, vecs[:, ds(V_PSCALE + j, 1)])
                    decay(0)
                    split_tile(4)
                    split_tile(5)
                    scale_tile(3, gnorm8[:, ds(j, 1)])
                    decay(1)
            barrier(dve, 2)

            for d in range(2):
                dve.tensor_tensor(into_tmp[:, d], tot[:, d, d:d + UNITS], mid[:, d, d:d + UNITS], ALU.subtract).then_inc(into_sum, 1)
                dve.wait_ge(into_sum, 2 * d + 1)
                dve.tensor_tensor(into_tmp[:, d], into_tmp[:, d], mid[:, d, d + 1:d + 1 + UNITS], ALU.add).then_inc(into_sum, 1)
            dve.wait_ge(into_ready, 2)
            dve.memset(into[:, 0, 0:UNITS:UPH], 0.0)
            with dve.Fori(0, HEADS) as hh:
                dve.wait_ge(zb_ready, START + UPH * hh)
                dve.memset(zb[1][:, :], 0.0).then_inc(zb_cleared, 1)
                wait_apart(dve, (zb_cleared, hh + 1))
                with dve.Fori(0, UPH // 2) as i:
                    for e in range(2):
                        n = UPH * hh + 2 * i + e
                        factor = into[:, 1, ds(UNITS - 1 - n, 1)]
                        wait_apart(dve, (zb_ready, START + n))
                        dve.tensor_scalar(sb_all[:, UNITS - 1 - n, :], zb[1 - e][:, :], factor, None, ALU.mult)
                        dve.wait_ge(kv_product, START + n + 1)
                        dve.scalar_tensor_tensor(zb[e][:, :], zb[1 - e][:, :], factor,
                                                 ps[:, 2 + e, 0:HEAD_V], ALU.mult, ALU.add).then_inc(zb_ready, 1)
            dve.wait_ge(gate_product, KT)
            dve.tensor_tensor(gate_col[:, :], ps[:, 4, 0:KT], vecs[:, V_BADA + 2 * KT:V_BADA + 3 * KT], ALU.add).then_inc(gate_sum, 1)
            dve.wait_ge(gate_sum, 1)
            dve.tensor_tensor(gate_col[:, :], gate_col[:, :], vecs[:, V_GPOST:V_GPOST + KT], ALU.mult).then_inc(gate_sum, 1)
            dve.wait_ge(gate_sum, 2)
            dve.tensor_copy(gate_wide, gate_col[:, :].unsqueeze(2).to_broadcast([P, KT, P])).then_inc(gate_wide_ready, 1)
            dve.wait_ge(gate_spread, 1)
            dve.tensor_copy(gate_row[:, :], flat(ps[:, 5:7]))
            sweep_barrier(dve)

            def choose(b, e):
                n, s = 8 * b + e, e % 2
                wait_apart(dve, (scores_done, n + 1), (score_copied, n + 1))
                dve.copy_predicated(score[s][:, :], later[:, :], ps[:, s, 2 * P:3 * P]).then_inc(score_ready, 1)

            def add_state(b, e):
                n, s = 8 * b + e, e % 2
                dve.wait_ge(states_product, START + n + 1)
                dve.wait_ge(sf_ready, START + n)
                dve.wait_ge(zf_ready, START + n)
                dve.scalar_tensor_tensor(zf[s][:, :], zf[1 - s][:, :], into[:, 0, ds(n, 1)],
                                         ps[:, 2 + s, 0:HEAD_V], ALU.mult, ALU.add).then_inc(zf_ready, 1)

            def normalize(b, e):
                n, s = 8 * b + e, e % 2
                dve.wait_ge(sd_ready, START + n + 1)
                dve.reciprocal(o_ss[s][:, 2:3], o_ss[s][:, 1:2]).then_inc(rs_ready, 1)
                dve.wait_ge(rs_ready, START + n + 1)
                dve.wait_ge(o_turned, START + n - 1)
                dve.tensor_scalar(o_n[s][:, :], ps[:, 4 + s, 0:HEAD_V], o_ss[s][:, 2:3], None, ALU.mult).then_inc(normed, 1)

            def gate(b, e):
                n, g, s = 8 * b + e, e // 4, e % 2
                cols = slice(UNIT * (e % 4), UNIT * (e % 4) + UNIT)
                if e % 4 == 0:
                    dve.wait_ge(group_loaded[g], 32 * b + 32)
                    dve.wait_ge(og_stored[g], 16 * b + 16)
                dve.wait_ge(o_turned, START + n + 1)
                dve.tensor_tensor(o_g[g][:, :, cols], ps[:, 6 + s, 0:HEAD_V].rearrange("p (a t) -> p a t", a=2),
                                  gate_u[g][:, :, cols], ALU.mult).then_inc(og_ready, 1)

            def units(b, first=False, last=False):
                for e in range(8):
                    if e < 7:
                        choose(b, e + 1)
                    elif not last:
                        choose(b + 1, 0)
                    add_state(b, e)
                    normalize(b, e)
                    if e:
                        gate(b, e - 1)
                    elif not first:
                        gate(b - 1, 7)

            dve.memset(zf[1][:, :], 0.0).then_inc(zf_cleared, 1)
            dve.wait_ge(zf_cleared, 1)
            choose(0, 0)
            units(0, first=True)
            with dve.Fori(1, UNITS // 8 - 1) as b:
                units(b)
            units(UNITS // 8 - 1, last=True)
            gate(UNITS // 8 - 1, 7)
            barrier(dve, 4)

            for s in (gated, summed, m_ready, fin_ready, out_product, normed7, pooled_ready, pa_ready, pool_product, pa_split):
                dve.sem_inc(s, START)
            for s in (*y_free, *fin_free, pw_ready):
                dve.sem_inc(s, 1)
            dve.sem_inc(credits_given, 1)

            with dve.Fori(0, GROUPS) as g:
                dve.wait_ge(pw_hi_ready, g + 1)
                dve.tensor_tensor(pw_lo[:, :, :], pw_in[:, :, :], pw_hi[:, :, :].bitcast(F32), ALU.subtract).then_inc(pw_ready, 1)

                def split_pooled(b):
                    s = b % 2
                    dve.wait_ge(pooled_hi_ready, NB * g + b + 1)
                    dve.tensor_tensor(pooled_lo[s][:, :, :], pooled_in[s][:, :, :], pooled_hi[s][:, :, :].bitcast(F32),
                                      ALU.subtract).then_inc(pooled_ready, 1)

                def gate_result(b):
                    s = b % 2
                    dve.wait_ge(pool_product, START + NB * g + b + 1)
                    dve.wait_ge(pg_loaded[s], 32 * g + 16 * (b // 2) + 16)
                    dve.wait_ge(pa_split, START + NB * g + b - 1)
                    dve.tensor_tensor(pa[s][:, :, :], ps[:, 2 * s:2 * s + 2], pg_in[s][:, :, :], ALU.mult).then_inc(pa_ready, 1)

                split_pooled(0)
                for b in range(1, NB):
                    split_pooled(b)
                    gate_result(b - 1)
                gate_result(NB - 1)

            def split_next(r, m, e, i):
                dve.wait_ge(pj_loaded[e], 16 * (KT // 2) * r + 16 * i + 16)
                split_weights(e, pj_hi_ready, pj_ready, KT * r + m)

            split_next(0, 0, 0, 0)
            split_next(0, 1, 1, 0)
            barrier(dve, 5)

            def gate_tile(r, m, e, i):
                dve.wait_ge(pj_product, KT * r + m + 1)
                dve.wait_ge(sig_loaded[e], 16 * (KT // 2) * r + 16 * i + 16)
                dve.wait_ge(y_free[e], KT // 2 * r + i + 1)
                dve.tensor_tensor(y_out[:, e], flat(banks(e)), sig_in[:, e], ALU.mult).then_inc(gated, 1)

            for r in range(2):
                if r == 1:
                    for k in range(KT):
                        dve.wait_ge(src_hi, k + 1)
                        dve.tensor_tensor(h_lo[:, k, :], src_in[:, k % 2], h_hi[:, k, :].bitcast(F32), ALU.subtract).then_inc(src_ready, 1)
                with dve.Fori(0, KT // 2 - 1) as i:
                    for e in range(2):
                        gate_tile(r, 2 * i + e, e, i)
                        split_next(r, 2 * i + e + 2, e, i + 1)
                for e in range(2):
                    gate_tile(r, KT - 2 + e, e, KT // 2 - 1)
                    if r == 0:
                        split_next(1, e, e, 0)
            barrier(dve, 6)

            for k in range(KT):
                dve.wait_ge(wo_hi_ready, k + 1)
                dve.tensor_tensor(wo_lo[:, k, :], wo_in[:, k % 2], wo_hi[:, k, :].bitcast(F32), ALU.subtract).then_inc(wo_ready, 1)

            def split_tokens(n, e):
                dve.wait_ge(m_hi_ready, n + 1)
                dve.tensor_tensor(m_lo[e][:, :, :], m_in[e][:, :, :], m_hi[e][:, :, :].bitcast(F32), ALU.subtract).then_inc(m_ready, 1)

            with dve.Fori(0, T // P // 2) as i:
                for e in range(2):
                    n = 2 * i + e
                    split_tokens(n, e)
                    dve.wait_ge(sd7_ready, n + 1)
                    dve.reciprocal(fin_s[e][:, 2:3], fin_s[e][:, 1:2]).then_inc(rs7_ready, 1)
                    dve.wait_ge(rs7_ready, n + 1)
                    dve.wait_ge(fin_free[e], i + 1)
                    dve.scalar_tensor_tensor(fin[e][:, :], flat(ps[:, 2 * e:2 * e + 2]), fin_s[e][:, 2:3], gate_row[:, :],
                                             ALU.mult, ALU.mult).then_inc(normed7, 1)
            barrier(dve, 7)

        @block.gpsimd
        def _(pool):
            pool.memset(rows[:, :], 0.0).then_inc(rows_cleared, 1)
            pool.memset(ones[:, :], 1.0)
            pool.memset(eps_col[:, :], EPS)
            pool.memset(one_col[:, :], 1.0)
            pool.memset(mid[:, :, :], 0.0)
            pool.memset(tot[:, :, :], 0.0)
            pool.memset(edge[:, :, :], 1.0).then_inc(pool_consts, 1)
            pool.wait_ge(pool_consts, 1)
            pool.affine_select(out=ident[:, :], in_=ones[:, :], compare_op=ALU.is_equal, fill=0.0, base=0,
                               pattern=[[-1, P]], channel_multiplier=1).then_inc(consts_ready, 1)
            pool.affine_select(out=later[:, :], in_=ones[:, :], compare_op=ALU.is_gt, fill=0.0, base=0,
                               pattern=[[-1, P]], channel_multiplier=1)
            for g, w in enumerate(WINDOWS):
                for t in range(w // 2):
                    pool.memset(edge[:, g, t:t + 1], w / (t + w // 2))
                for r in range(1, w // 2):
                    pool.memset(edge[:, g, 2 * PAD - r:2 * PAD - r + 1], w / (r + w // 2))
            for g in range(4):
                for k in range(KT):
                    n = KT * g + k
                    pool.wait_ge(hi_ready, n + 1)
                    pool.wait_ge(full_ready, n + 1)
                    cols = slice(512 * g, 512 * g + 512)
                    pool.tensor_tensor(h_lo[:, k, cols], h_full[:, n % 2], h_hi[:, k, cols].bitcast(F32),
                                       ALU.subtract).then_inc(lo_ready, 1)
            barrier(pool, 1)

            pool.memset(gk_up[:, :, :], 0.0).then_inc(gk_cleared, 1)
            pool.memset(dec_in[:, :, 0:1], 0.0)
            pool.memset(run_on[:, :, :], 1.0).then_inc(pool_consts, 1)
            pool.wait_ge(pool_consts, 2)
            pool.memset(run_on[:, :, 0:1], 0.0).then_inc(pool_consts, 1)
            def store(dst, t_slot, count):
                pool.dma_start(dst, tile_out[:, t_slot]).then_inc(tile_stored[t_slot], 16)
                pool.wait_ge(tile_stored[t_slot], 16 * count)
                pool.sem_inc(tile_free[t_slot], 1)

            pool.wait_ge(tile_ready, 1)
            store(proj[M_LR], 0, 1)
            with pool.Fori(0, HEADS) as h:
                for e in range(2):
                    pool.wait_ge(tile_ready, 2 * h + e + 2)
                    store(proj[(M_Q, M_K)[e] + h], 1 - e, h + e + 1)
            with pool.Fori(0, HEADS) as h:
                with pool.Fori(0, 2) as s2:
                    j = 2 * h + s2

                    def store_tile(t):
                        name = TILES[t]
                        if name in ("p_gate", "gla_gate"):
                            wait_apart(pool, (tile_scaled, 2 * j + t // 2 + 1))
                        else:
                            pool.wait_ge(tile_ready, QK_USES + WTILES * j + t + 1)
                        a = tile_out[:, slot(t)]
                        if name in ("v", "gla_gate"):
                            dst = (v_ch if name == "v" else gate_ch)[ds(NB * h, NB), s2].rearrange("b p t -> p b t")
                            a = a.rearrange("p (b t) -> p b t", t=512)
                        else:
                            dst = proj[TILE_AT[name] + j]
                        pool.dma_start(dst, a).then_inc(tile_stored[slot(t)], 16)
                        pool.wait_ge(tile_stored[slot(t)], 16 * in_slot(t, j, WTILES) + 16)
                        pool.sem_inc(tile_free[slot(t)], 1)

                    def apply_decay(d):
                        n = 2 * j + d
                        pool.wait_ge(exps_ready, n + 1)
                        pool.wait_ge(q_loaded, 16 * j + 16)
                        pool.wait_ge(k_loaded, 16 * j + 16)
                        pool.tensor_tensor(q_dec[:, :], q_dec[:, :], q_half[:, :], ALU.mult)
                        pool.tensor_tensor(k_dec[:, :], k_dec[:, :], k_half[:, :], ALU.mult).then_inc(decayed_ready, 1)
                        pool.wait_ge(decayed_ready, START + n + 1)
                        for a, src, stored in ((d, q_dec, qd_stored), (2 + d, k_dec, kd_stored)):
                            pool.dma_start(decayed[ds(HU * j, HU), :, a, :].rearrange("u p t -> p u t"),
                                           src[:, :].rearrange("p (u t) -> p u t", t=UNIT)).then_inc(stored, 16)
                        pool.wait_ge(qd_stored, 16 * n + 16)
                        pool.wait_ge(kd_stored, 16 * n + 16)
                        pool.sem_inc(decay_free, 1)

                    store_tile(0)
                    store_tile(1)
                    apply_decay(0)
                    store_tile(2)
                    store_tile(3)
                    apply_decay(1)
                    store_tile(4)
                    store_tile(5)
            barrier(pool, 2)

            JOBS = [(m, s) for m in range(KT) for s in range(2)]

            def load_half(n):
                m, s = JOBS[n]
                first = PAD if s == 0 else 0
                lo = HALF * s - PAD + first
                hi = min(HALF * s + HALF + PAD, T)
                pool.dma_start(pu[n % 3][:, first:first + hi - lo], proj[M_PIN + m, :, lo:hi]).then_inc(pu_loaded[n % 3], 16)
                zeros = slice(0, PAD) if s == 0 else slice(HALF + PAD, WIDE)
                pool.memset(pu[n % 3][:, zeros], 0.0).then_inc(pool_step, 1)

            steps_done = 2
            for n in range(2):
                load_half(n)
            for n, (m, s) in enumerate(JOBS):
                w, g, u = WINDOWS[m // 2], m // 2, pu[n % 3]
                levels = len(bin(w)) - 3
                pool.wait_ge(pu_loaded[n % 3], 16 * (n // 3 + 1))
                lo, hi = 1, WIDE
                pool.wait_ge(pool_step, steps_done)
                pool.tensor_tensor(psum2[0][:, 1:WIDE], u[:, 0:WIDE - 1], u[:, 1:WIDE], ALU.add).then_inc(pool_step, 1)
                steps_done += 1
                for k in range(1, levels):
                    r = 2 ** (k - 1)
                    lo, hi = lo + r, hi - r
                    a, b = psum2[(k - 1) % 2], psum2[k % 2]
                    pool.wait_ge(pool_step, steps_done)
                    pool.tensor_tensor(b[:, lo:hi], a[:, lo - r:hi - r], a[:, lo + r:hi + r], ALU.add).then_inc(pool_step, 1)
                    steps_done += 1
                total = psum2[(levels - 1) % 2]
                at = PAD if s == 0 else HALF
                pool.wait_ge(pool_step, steps_done)
                pool.tensor_tensor(total[:, at:at + PAD], total[:, at:at + PAD], edge[:, g, PAD * s:PAD * s + PAD],
                                   ALU.mult).then_inc(pool_step, 1)
                steps_done += 1
                pool.wait_ge(pool_step, steps_done)
                inner = slice(PAD, PAD + HALF)
                pool.tensor_scalar(total[:, inner], total[:, inner], 1.0 / w, None, ALU.mult).then_inc(pool_step, 1)
                steps_done += 1
                pool.wait_ge(pool_step, steps_done)
                pool.tensor_tensor(u[:, inner], total[:, inner], u[:, inner], ALU.subtract).then_inc(pool_step, 1)
                steps_done += 1
                pool.wait_ge(pool_step, steps_done)
                pool.dma_start(pooled_ch[m, :, HALF * s:HALF * s + HALF], u[:, inner]).then_inc(pu_stored[n % 3], 16)
                if n + 2 < len(JOBS):
                    if n >= 1:
                        pool.wait_ge(pu_stored[(n + 2) % 3], 16 * ((n - 1) // 3 + 1))
                    load_half(n + 2)
                    steps_done += 1
            for s in range(3):
                pool.wait_ge(pu_stored[s], 16 * len(range(s, len(JOBS), 3)))
            barrier(pool, 4)

            pool.wait_ge(credits_given, 1)
            with pool.Fori(0, GROUPS) as g:
                for b in range(NB):
                    pool.wait_ge(pa_hi_ready, NB * g + b + 1)
                    tiles, cols = ds(2 * g, 2), slice(512 * b, 512 * b + 512)
                    pool.tensor_tensor(h_lo[:, tiles, cols], pa[b % 2][:, :, :], h_hi[:, tiles, cols].bitcast(F32),
                                       ALU.subtract).then_inc(pa_split, 1)
            barrier(pool, 5)

            for r, dst in enumerate((y_pool, merged)):
                with pool.Fori(0, KT // 2) as i:
                    for e in range(2):
                        m = 2 * i + e
                        pool.wait_ge(gated, START + KT * r + m + 1)
                        if r == 1:
                            pool.wait_ge(y_loaded[e], 16 * i + 16)
                            pool.tensor_tensor(y_out[:, e], y_out[:, e], src_in[:, e], ALU.add).then_inc(summed, 1)
                            pool.wait_ge(summed, START + m + 1)
                        pool.dma_start(dst[m], y_out[:, e]).then_inc(y_stored[e], 16)
                        pool.wait_ge(y_stored[e], 16 * (KT // 2) * r + 16 * i + 16)
                        pool.sem_inc(y_free[e], 1)
            barrier(pool, 6)

            with pool.Fori(0, T // P // 2) as i:
                for e in range(2):
                    n = 2 * i + e
                    pool.wait_ge(normed7, START + n + 1)
                    pool.wait_ge(x7_loaded[e], 16 * i + 16)
                    pool.tensor_tensor(fin[e][:, :], fin[e][:, :], x_in[e][:, :], ALU.add).then_inc(fin_ready, 1)
                    pool.wait_ge(fin_ready, START + n + 1)
                    pool.dma_start(out[0, ds(P * n, P), :], fin[e][:, :]).then_inc(out_stored[e], 16)
                    pool.wait_ge(out_stored[e], 16 * i + 16)
                    pool.sem_inc(fin_free[e], 1)
            barrier(pool, 7)

_INS = ["x", "c", "w_ada", "b_ada", "g_pre", "g_post", "w_in", "pool_w", "pool_scale", "gk_up_fwd", "gk_bias_fwd",
        "gk_up_bwd", "gk_bias_bwd", "gla_norm_g", "w_proj_pool", "w_proj_gla", "w_out"]


def kernel(**inputs):
    import numpy as _np
    import concourse.bacc as _bacc
    from concourse import mybir as _mybir
    from concourse.bass_utils import run_bass_kernel_spmd as _run

    nc = _bacc.Bacc("TRN2", target_bir_lowering=False, num_devices=1)
    arrays, args = {}, []
    for name in _INS:
        a = _np.ascontiguousarray(inputs[name])
        arrays[f"in_{name}"] = a
        args.append(nc.dram_tensor(f"in_{name}", a.shape, _mybir.dt.from_np(a.dtype), kind="ExternalInput").ap())
    out = nc.dram_tensor("out_0", (1, T, D), F32, kind="ExternalOutput").ap()
    build(nc, *args, out)
    r = _run(nc, [arrays], core_ids=[0])
    return r.results[0]["out_0"]
```

```python
import numpy as np

import concourse.bass as bass
from concourse import mybir

F32 = mybir.dt.float32
F32R = mybir.dt.float32r
BF16 = mybir.dt.bfloat16
I32 = mybir.dt.int32
ALU = mybir.AluOpType
ACT = mybir.ActivationFunctionType
ds = bass.ds

P = 128
T = 2048
D = 1024
KT = D // P
NB = T // 512
HEADS = 4
RANK = 16
NORMALIZER = 16.0
UNIT = 128
UPH = T // UNIT
UNITS = HEADS * UPH
HALF = T // 2
HU = HALF // UNIT
EPS = 1e-6
GROUPS = 4
WINDOWS = (2, 4, 8, 16)
PAD = max(WINDOWS) // 2
HEAD_V = 256

C_PIN, C_PGATE, C_Q, C_K, C_V, C_GGATE = 0, 1024, 2048, 2560, 3072, 4096
C_LR, C_BGP, C_BGG = 5120, 5152, 6176
M_PIN, M_PGATE, M_BGP, M_BGG, M_Q, M_K, M_LR = 0, 8, 16, 24, 32, 36, 40
M_ALL = 41
V_C, V_BADA, V_GPRE, V_PSCALE, V_GKB, V_GNORM = 0, 8, 32, 40, 48, 56
START = 2
ENGINES = 5


def build(nc, x, c, w_ada, b_ada, g_pre, g_post, w_in, pool_w, pool_scale, gk_up_fwd, gk_bias_fwd,
          gk_up_bwd, gk_bias_bwd, gla_norm_g, w_proj_pool, w_proj_gla, w_out, out):
    base = (nc.sbuf_base + 63) // 64 * 64
    limit = nc.sbuf_usable_end

    class Region:

        def __init__(self, at):
            self.at = at

        def __call__(self, name, shape, dtype=F32):
            size = 2 if dtype == BF16 else 4
            n = size * int(np.prod(shape[1:]))
            t = nc.alloc_sbuf_tensor_at(name, shape, dtype, offset=self.at)
            self.at += (n + 31) // 32 * 32
            assert self.at <= limit, (name, self.at, limit)
            return t.ap()

    def sem(name):
        return nc.alloc_semaphore(name)

    proj = nc.dram_tensor("proj", (M_ALL, P, T), F32).ap()
    decayed = nc.dram_tensor("decayed", (UNITS, P, 4, UNIT), F32).ap()
    v_ch = nc.dram_tensor("v_ch", (HEADS * NB, 2, P, 512), F32).ap()
    gate_ch = nc.dram_tensor("gate_ch", (HEADS * NB, 2, P, 512), F32).ap()
    gla_out = nc.dram_tensor("gla_out", (HEADS * NB, 2, P, 512), F32).ap()
    pooled_ch = nc.dram_tensor("pooled_ch", (KT, P, T), F32).ap()
    y_pool = nc.dram_tensor("y_pool", (KT, P, T), F32).ap()
    merged = nc.dram_tensor("merged", (KT, P, T), F32).ap()

    keep = Region(base)
    ident = keep("ident", [P, P])
    ones = keep("ones", [P, P])
    later = keep("later", [P, P], I32)
    vecs = keep("vecs", [P, P])
    gnorm8 = keep("gnorm8", [P, KT])
    c_act = keep("c_act", [P, KT])
    h_scale = keep("h_scale", [P, KT])
    h_shift = keep("h_shift", [P, KT])
    eps_col = keep("eps_col", [P, 1])
    one_col = keep("one_col", [P, 1])
    mid = keep("mid", [P, 2, UNITS + 2])
    tot = keep("tot", [P, 2, UNITS + 2])
    edge = keep("edge", [P, GROUPS, 2 * PAD])
    weights_at = keep.at
    stage = keep("stage", [P, 2, KT, P])
    w_hi = [keep(f"w_hi{s}", [P, KT, P], F32R) for s in range(2)]
    w_lo = [keep(f"w_lo{s}", [P, KT, P], F32R) for s in range(2)]
    low = keep.at

    big = Region(low)
    h_hi = big("h_hi", [P, KT, T], F32R)
    h_lo = big("h_lo", [P, KT, T], F32R)
    above = big.at

    r0 = Region(above)
    xin = r0("xin", [P, 3, 4, D])
    sumsq = r0("sumsq", [P, T // P])
    rstd = r0("rstd", [P, T // P])
    h_full = [Region(weights_at + 4 * D * (3 + 2 * (s // 2)) + 2048 * (s % 2))(f"h_full{s}", [P, 512]) for s in range(4)]
    early_h = Region(low)
    ada_w = early_h("ada_w", [P, 8, KT, 256])
    rows = early_h("rows", [P, P])
    ada_acc = early_h("ada_acc", [P, 8, 256])

    r1 = Region(above)
    tile_out = r1("tile_out", [P, 2, T])
    lr_split = r1("lr_split", [P, HALF], F32R)
    gk_in = r1("gk_in", [P, 2, P])
    gk_split = r1("gk_split", [P, 2, P], F32R)
    q_half = r1("q_half", [P, HALF])
    k_half = r1("k_half", [P, HALF])
    dec_a = r1("dec_a", [P, HALF])
    lr_in = dec_a
    dec_in = r1("dec_in", [P, HU, UNIT + 1])
    dec_sum = r1("dec_sum", [P, HU, UNIT + 1])
    run_on = r1("run_on", [P, HU, UNIT + 1], BF16)
    q_dec = r1("q_dec", [P, HALF])
    k_dec = r1("k_dec", [P, HALF])

    into = Region(limit // 64 * 64 - 4 * D - 512)("into", [P, 2, UNITS])

    h_size = 2 * 4 * KT * T
    held = Region(low)
    v_all = held("v_all", [P, UNITS, HEAD_V])
    sb_all = held("sb_all", [P, UNITS, HEAD_V])
    assert held.at == low + h_size
    inputs3 = Region(held.at)
    dec_u = [inputs3(f"dec_u{s}", [P, 4, 4, UNIT]) for s in range(2)]
    gate_u = [inputs3(f"gate_u{s}", [P, 2, 512]) for s in range(2)]

    r2 = Region(inputs3.at)
    kb_in = [r2(f"kb_in{s}", [P, 4, UNIT]) for s in range(2)]
    vt_in = [r2(f"vt_in{s}", [P, 2, 512]) for s in range(2)]
    over3 = Region(held.at + 4 * 16 * UNIT)
    kb_in += [over3(f"kb_in{s}", [P, 4, UNIT]) for s in range(2, 4)]
    vt_in += [over3(f"vt_in{s}", [P, 2, 512]) for s in range(2, 4)]
    assert over3.at <= inputs3.at
    zb = [r2(f"zb{s}", [P, HEAD_V]) for s in range(2)]

    r3 = Region(inputs3.at)
    o_g = [r3(f"o_g{s}", [P, 2, 512]) for s in range(2)]
    kf_tok = [r3(f"kf_tok{s}", [P, P]) for s in range(2)]
    score = [r3(f"score{s}", [P, UNIT]) for s in range(2)]
    sf = [r3(f"sf{s}", [P, HEAD_V]) for s in range(2)]
    zf = [r3(f"zf{s}", [P, HEAD_V]) for s in range(2)]
    o_sq = [r3(f"o_sq{s}", [P, HEAD_V]) for s in range(2)]
    o_n = [r3(f"o_n{s}", [P, HEAD_V]) for s in range(2)]
    o_ss = [r3(f"o_ss{s}", [P, 8]) for s in range(2)]
    assert max(r2.at, r3.at) <= limit // 64 * 64 - 4 * D - 512

    WIDE = HALF + 2 * PAD
    rp = Region(weights_at)
    pu = [rp(f"pu{s}", [P, WIDE]) for s in range(3)]
    window = [rp(f"window{s}", [P, WIDE]) for s in range(2)]
    kb_tok = [rp(f"kb_tok{s}", [P, P]) for s in range(2)]
    into_tmp = rp("into_tmp", [P, 2, UNITS])
    zb += [rp(f"zb{s}", [P, HEAD_V]) for s in range(2, 4)]
    assert rp.at <= low

    gate_row = Region(limit // 64 * 64 - 4 * D)("gate_row", [P, D])

    r4 = Region(above)
    pooled_in = [r4(f"pooled_in{s}", [P, 2, 512]) for s in range(2)]
    pooled_hi = [r4(f"pooled_hi{s}", [P, 2, 512], F32R) for s in range(2)]
    pooled_lo = [r4(f"pooled_lo{s}", [P, 2, 512], F32R) for s in range(2)]
    pg_in = [r4(f"pg_in{s}", [P, 2, 512]) for s in range(2)]
    pa = [r4(f"pa{s}", [P, 2, 512]) for s in range(2)]
    gate_w = [r4(f"gate_w{s}", [P, D]) for s in range(2)]
    rw = Region(weights_at)
    pw_in = rw("pw_in", [P, GROUPS, 2, 256])
    pw_hi = rw("pw_hi", [P, GROUPS, 2, 256], F32R)
    pw_lo = rw("pw_lo", [P, GROUPS, 2, 256], F32R)
    assert r4.at <= limit // 64 * 64 - 4 * D

    r5 = Region(above)
    src_in = r5("src_in", [P, 2, T])
    y_out = r5("y_out", [P, 2, T])
    sig_place = r5.at
    sig_in = r5("sig_in", [P, 2, T])

    r7 = Region(low)
    wo_hi = r7("wo_hi", [P, KT, D], F32R)
    wo_lo = r7("wo_lo", [P, KT, D], F32R)
    m_in = [r7(f"m_in{s}", [P, KT, P]) for s in range(2)]
    m_hi = [r7(f"m_hi{s}", [P, KT, P], F32R) for s in range(2)]
    m_lo = [r7(f"m_lo{s}", [P, KT, P], F32R) for s in range(2)]
    x_in = [r7(f"x_in{s}", [P, D]) for s in range(2)]
    fin = [r7(f"fin{s}", [P, D]) for s in range(2)]
    fin_sq = [r7(f"fin_sq{s}", [P, D]) for s in range(2)]
    fin_s = [r7(f"fin_s{s}", [P, 4]) for s in range(2)]
    assert r7.at <= above
    wo_at = [weights_at + 4 * D * i for i in (0, 1, 2, 4)] + [sig_place, sig_place + 4 * D, above, above + 4 * D]
    wo_in = [Region(at)(f"wo_in{k}", [P, D]) for k, at in enumerate(wo_at)]

    ps = nc.alloc_psum_tensor("ps", [P, 8, 512], F32).ap()

    step_done, cleared, passed = sem("step_done"), sem("cleared"), sem("passed")
    swept, credits_given = sem("swept"), sem("credits_given")
    early = []

    def sem01(name):
        early.append(nc.alloc_semaphore(name))
        return early[-1]

    unused = iter(early)

    def again(name):
        return next(unused)

    consts_ready = sem01("consts_ready")
    rows_loaded = sem01("rows_loaded")
    rows_cleared = sem01("rows_cleared")
    vecs_turned, vecs_ready, c_ready = sem01("vecs_turned"), sem01("vecs_ready"), sem01("c_ready")
    ada_loaded = [sem01(f"ada_loaded{s}") for s in range(4)]
    ada_used, ada_step, mod_part, mod_ready = sem01("ada_used"), sem01("ada_step"), sem01("mod_part"), sem01("mod_ready")
    x_loaded = [sem01(f"x_loaded{s}") for s in range(3)]
    sumsq_ready, var_ready, std_ready, rstd_ready = sem01("sumsq_ready"), sem01("var_ready"), sem01("std_ready"), sem01("rstd_ready")
    xn_ready, x_turned = sem01("xn_ready"), sem01("x_turned")
    hi_ready, full_ready, lo_ready = sem01("hi_ready"), sem01("full_ready"), sem01("lo_ready")
    lo_ready_dve = sem01("lo_ready_dve")

    w_loaded = [sem01(f"w_loaded{s}") for s in range(2)]
    w_hi_ready = sem01("w_hi_ready")
    w_ready = sem01("w_ready")
    product_done, z_done, z_free = sem01("product_done"), sem01("z_done"), sem01("z_free")
    ps_free = [sem01(f"ps_free{s}") for s in range(2)]
    tile_ready, tile_scaled = sem01("tile_ready"), sem01("tile_scaled")
    tile_stored = [sem(f"tile_stored{s}") for s in range(2)]
    tile_free = [sem01(f"tile_free{s}") for s in range(2)]
    decay_free = sem01("decay_free")
    lr_loaded, gk_loaded, q_loaded, k_loaded = sem01("lr_loaded"), sem01("gk_loaded"), sem01("q_loaded"), sem01("k_loaded")
    gk_cleared = sem01("gk_cleared")
    lr_hi_ready, lr_ready = sem01("lr_hi_ready"), sem01("lr_ready")
    abs_done, expneg_done, logsig_ready = sem01("abs_done"), sem01("expneg_done"), sem01("logsig_ready")
    min_done, la_done, scan_done, centred = sem01("min_done"), sem01("la_done"), sem01("scan_done"), sem01("centred")
    exps_ready, decayed_ready = sem01("exps_ready"), sem01("decayed_ready")
    qd_stored, kd_stored = sem("qd_stored"), sem("kd_stored")

    def barrier(eng, step, storing=False, waits=True):
        if storing:
            eng.sem_inc(step_done, 1)
        else:
            eng.drain().then_inc(step_done, 1)
        if waits:
            eng.wait_ge(step_done, ENGINES * (step if step < 3 else step - 1))
        if step == 4:
            eng.wait_ge(cleared, len(early))
            eng.sem_inc(passed, 1)

    def sweep_barrier(eng):
        eng.drain().then_inc(swept, 1)
        eng.wait_ge(swept, ENGINES - 1)

    def wait_apart(eng, *waits):
        for s, v in waits:
            eng.wait_ge(s, v)
        eng.sem_inc(passed, 1)

    def split_product(pe, banks, lhs_hi, lhs_lo, rhs_hi, rhs_lo, k, first_k, last_k):
        for b in range(NB):
            pe.matmul(banks[:, b], lhs_hi, rhs_hi[:, k, ds(512 * b, 512)], start=first_k, stop=False)
        for b in range(NB):
            pe.matmul(banks[:, b], lhs_hi, rhs_lo[:, k, ds(512 * b, 512)], start=False, stop=False)
        for b in range(NB):
            last = pe.matmul(banks[:, b], lhs_lo, rhs_hi[:, k, ds(512 * b, 512)], start=False, stop=last_k)
        return last

    kb_loaded = [sem01(f"kb_loaded{s}") for s in range(4)]
    into_sum, into_ready = sem01("into_sum"), sem01("into_ready")
    kv_turned, kv_copied, kv_product = sem01("kv_turned"), sem01("kv_copied"), sem01("kv_product")
    zb_ready, sb_ready = sem01("zb_ready"), sem01("sb_ready")
    zb_cleared, zf_cleared, pool_consts = sem01("zb_cleared"), sem("zf_cleared"), sem01("pool_consts")
    pu_loaded = [sem(f"pu_loaded{s}") for s in range(3)]
    pu_stored = [sem(f"pu_stored{s}") for s in range(3)]
    pool_step = sem("pool_step")
    dec_loaded = [sem(f"dec_loaded{s}") for s in range(2)]
    gla_gate_loaded = [sem(f"gla_gate_loaded{s}") for s in range(2)]
    scores_done, attn_done = sem("scores_done"), sem("attn_done")
    states_product = sem("states_product")
    kf_copied, score_copied, score_ready = sem("kf_copied"), sem("score_copied"), sem("score_ready")
    sf_ready, zf_ready = sem("sf_ready"), sem("zf_ready")
    ss_ready, sd_ready, rs_ready, normed, o_turned, og_ready = (sem(n) for n in (
        "ss_ready", "sd_ready", "rs_ready", "normed", "o_turned", "og_ready"))
    og_stored = [sem(f"og_stored{s}") for s in range(2)]
    gate_loaded = [again(f"gate_loaded{s}") for s in range(2)]
    gate_cleared, gate_rows_loaded, gate_step, gate_spread, gate_sum, gate_ready = (again(n) for n in (
        "gate_cleared", "gate_rows_loaded", "gate_step", "gate_spread", "gate_sum", "gate_ready"))
    pooled_loaded = [again(f"pooled_loaded{s}") for s in range(2)]
    pg_loaded = [again(f"pg_loaded{s}") for s in range(2)]
    pw_loaded, pw_hi_ready, pw_ready = again("pw_loaded"), again("pw_hi_ready"), again("pw_ready")
    pooled_hi_ready, pooled_ready, pool_product = again("pooled_hi_ready"), again("pooled_ready"), again("pool_product")
    pa_ready, pa_hi_ready, pa_split = again("pa_ready"), again("pa_hi_ready"), again("pa_split")

    h_tile_used = again("h_tile_used")
    src_loaded = [again(f"src_loaded{e}") for e in range(2)]
    src_hi, src_ready = again("src_hi"), again("src_ready")
    pj_loaded = [again(f"pj_loaded{e}") for e in range(2)]
    pj_hi_ready, pj_ready, pj_product = again("pj_hi_ready"), again("pj_ready"), again("pj_product")
    sig_loaded = [again(f"sig_loaded{e}") for e in range(2)]
    y_loaded = [again(f"y_loaded{e}") for e in range(2)]
    gated, summed = again("gated"), again("summed")
    y_stored = [sem(f"y_stored{e}") for e in range(2)]
    y_free = [again(f"y_free{e}") for e in range(2)]
    wo_loaded = [again(f"wo_loaded{k}") for k in range(KT)]
    tail_ready, m_head_loaded = again("tail_ready"), again("m_head_loaded")
    tail_stored = [again(f"tail_stored{b}") for b in range(NB)]
    wo_hi_ready, wo_ready = again("wo_hi_ready"), again("wo_ready")
    m_loaded = [again(f"m_loaded{s}") for s in range(2)]
    x7_loaded = [again(f"x7_loaded{s}") for s in range(2)]
    m_hi_ready, m_ready, out_product = again("m_hi_ready"), again("m_ready"), again("out_product")
    ss7_ready, sd7_ready, rs7_ready, normed7, fin_ready = (again(n) for n in (
        "ss7_ready", "sd7_ready", "rs7_ready", "normed7", "fin_ready"))
    out_stored = [sem(f"out_stored{s}") for s in range(2)]

    FIRST_TILES = 1 + 2 * HEADS
    TILES = ("p_in", "p_gate", "v", "gla_gate", "bg_pool", "bg_gla")
    DECAY_IN = (2, 4)
    COLUMN = {"p_in": C_PIN, "p_gate": C_PGATE, "v": C_V, "gla_gate": C_GGATE, "bg_pool": C_BGP, "bg_gla": C_BGG}
    TILE_AT = {"p_in": M_PIN, "p_gate": M_PGATE, "bg_pool": M_BGP, "bg_gla": M_BGG}
    FUNC = {"p_in": ACT.Copy, "p_gate": ACT.Silu, "v": ACT.Copy, "gla_gate": ACT.Silu,
            "bg_pool": ACT.Sigmoid, "bg_gla": ACT.Sigmoid}
    TURN = len(TILES)
    IN_SLOT = [(FIRST_TILES + 1) // 2, FIRST_TILES // 2]
    w_in_v = w_in[0].rearrange("(k p) n -> p k n", p=P)

    def slot(t):
        return (FIRST_TILES + t) % 2

    def in_slot(s, j, t):
        return IN_SLOT[s] + TURN // 2 * j + sum(slot(q) == s for q in range(t))

    def banks(s):
        return ps[:, 4 * s:4 * s + 4]

    def flat(a):
        return a.rearrange("p b n -> p (b n)")

    def wait_h_tile(eng, r, k):
        if k < KT - 1:
            eng.wait_ge(h_tile_used, (KT - 1) * (KT * r + KT - 1) + k + 1)
        else:
            eng.wait_ge(pj_product, KT * r + KT)

    def load_rows(eng, small):
        for at, n, src in small:
            eng.dma_start(rows[at:at + n, :], src.rearrange("o (r p) -> (o r) p", p=P)).then_inc(rows_loaded, 16)

    block = nc.Block()
    with block:

        @block.sync
        def _(sp):
            sp.wait_ge(rows_cleared, 1)
            load_rows(sp, ((V_C, 8, c), (V_BADA, 24, b_ada), (V_GPRE, 8, g_pre)))
            ada_v = w_ada[0].rearrange("(k p) n -> p k n", p=P)
            x_v = x[0].rearrange("(g t p) n -> g p t n", t=4, p=P)
            for n in range(8):
                if n in (2, 6):
                    g = n // 4
                    sp.dma_start(xin[:, g], x_v[g]).then_inc(x_loaded[g], 16)
                sp.dma_start(ada_w[:, n], ada_v[:, :, 256 * n:256 * n + 256]).then_inc(ada_loaded[n // 2], 16)
            sp.dma_start(xin[:, 2], x_v[2]).then_inc(x_loaded[2], 16)
            sp.dma_start(stage[:, 0], w_in_v[:, :, C_LR:C_LR + P]).then_inc(w_loaded[0], 16)
            sp.wait_ge(x_turned, KT)
            sp.dma_start(xin[:, 0], x_v[3]).then_inc(x_loaded[0], 16)
            barrier(sp, 1)

            with sp.Fori(0, HEADS) as h:
                sp.wait_ge(w_ready, START + 2 * h)
                sp.dma_start(stage[:, 1], w_in_v[:, :, ds(C_Q + P * h, P)]).then_inc(w_loaded[1], 16)
                sp.wait_ge(w_ready, START + 2 * h + 1)
                sp.dma_start(stage[:, 0], w_in_v[:, :, ds(C_K + P * h, P)]).then_inc(w_loaded[0], 16)
            def load_tile(t, j):
                sp.wait_ge(w_ready, START + FIRST_TILES + TURN * j + t - 1)
                sp.dma_start(stage[:, slot(t)], w_in_v[:, :, ds(COLUMN[TILES[t]] + P * j, P)]).then_inc(w_loaded[slot(t)], 16)

            with sp.Fori(0, HEADS) as h:
                with sp.Fori(0, 2) as s:
                    j = 2 * h + s
                    load_tile(0, j)
                    load_tile(1, j)
                    sp.wait_ge(tile_stored[0], 16 * IN_SLOT[0])
                    sp.wait_ge(tile_stored[1], 16 * IN_SLOT[1])
                    sp.wait_ge(decayed_ready, START + 2 * j)
                    sp.wait_ge(gk_cleared, 1)
                    for r in range(4):
                        at = 2 * RANK * r
                        sp.dma_start(lr_in[at:at + 2 * RANK, :], proj[M_LR, 0:2 * RANK, ds(HALF * s, HALF)]).then_inc(lr_loaded, 16)
                        sp.dma_start(gk_in[at:at + RANK, 0, :], gk_up_fwd[0, :, ds(P * h, P)]).then_inc(gk_loaded, 16)
                        sp.dma_start(gk_in[at + RANK:at + 2 * RANK, 1, :], gk_up_bwd[0, :, ds(P * h, P)]).then_inc(gk_loaded, 16)
                    sp.dma_start(q_half[:, :], proj[M_Q + h, :, ds(HALF * s, HALF)]).then_inc(q_loaded, 16)
                    sp.dma_start(k_half[:, :], proj[M_K + h, :, ds(HALF * s, HALF)]).then_inc(k_loaded, 16)
                    for t in range(2, TURN):
                        load_tile(t, j)
            barrier(sp, 2)

            def load_group(b, g, back):
                if back is not None:
                    wait_apart(sp, (kv_turned, back))
                n = UNITS // 4 - 1 - g - 4 * b
                sp.dma_start(kb_in[g][:, :, :], decayed[ds(4 * n, 4), :, 3, :].rearrange("n p t -> p n t")).then_inc(kb_loaded[g], 16)
                sp.dma_start(vt_in[g][:, :, :], v_ch[n].rearrange("a p t -> p a t")).then_inc(kb_loaded[g], 16)

            for g in range(4):
                load_group(0, g, None)
            with sp.Fori(0, HEADS - 1) as b:
                for g in range(4):
                    load_group(b + 1, g, UPH * b + 4 * g + 4)

            def load_decayed(n, g):
                sp.dma_start(dec_u[g][:, :, :, :], decayed[ds(4 * n, 4)].rearrange("n p a t -> p n a t")).then_inc(dec_loaded[g], 16)

            def load_gates(n, g):
                sp.dma_start(gate_u[g][:, :, :], gate_ch[n].rearrange("a p t -> p a t")).then_inc(gla_gate_loaded[g], 16)

            def store_units(n, g):
                wait_apart(sp, (og_ready, START + 4 * n + 4))
                sp.dma_start(gla_out[n].rearrange("a p t -> p a t"), o_g[g][:, :, :]).then_inc(og_stored[g], 16)

            for s in range(2):
                sp.wait_ge(tile_stored[s], 16 * (IN_SLOT[s] + TURN // 2 * 2 * HEADS))
            load_decayed(0, 0)
            load_gates(1, 1)
            sp.wait_ge(kv_turned, UNITS)
            load_gates(0, 0)
            load_decayed(1, 1)
            sweep_barrier(sp)
            for s in early:
                sp.sem_clear(s).then_inc(cleared, 1)

            with sp.Fori(0, UNITS // 8 - 1) as b:
                for g in range(2):
                    n = 2 * b + g
                    wait_apart(sp, (attn_done, START + 4 * n + 4))
                    load_decayed(n + 2, g)
                    store_units(n, g)
                    load_gates(n + 2, g)
            for g in range(2):
                store_units(UNITS // 4 - 2 + g, g)
            barrier(sp, 4)

            def load_weights(r, m, e):
                wt_v = (w_proj_pool, w_proj_gla)[r][0].rearrange("(k p) n -> p k n", p=P)
                sp.dma_start(stage[:, e], wt_v[:, :, ds(P * m, P)]).then_inc(pj_loaded[e], 16)

            def load_pooled(b, g):
                s = g % 2
                sp.wait_ge(pooled_ready, START + GROUPS * b + g - 1)
                sp.dma_start(pooled_in[s][:, :, :], pooled_ch[2 * g:2 * g + 2, :, ds(512 * b, 512)]
                             .rearrange("a p t -> p a t")).then_inc(pooled_loaded[s], 16)

            def load_pool_gate(b, g):
                s = g % 2
                sp.wait_ge(pa_ready, START + GROUPS * b + g - 1)
                sp.dma_start(pg_in[s][:, :, :], proj[M_PGATE + 2 * g:M_PGATE + 2 * g + 2, :, ds(512 * b, 512)]
                             .rearrange("a p t -> p a t")).then_inc(pg_loaded[s], 16)

            sp.wait_ge(credits_given, 1)
            sp.dma_start(pw_in[:, :, :, :], pool_w[0].rearrange("g (a p) n -> p g a n", p=P)).then_inc(pw_loaded, 16)
            for g in range(2):
                sp.wait_ge(og_stored[g], 16 * (1 + UNITS // 8))
            sp.wait_ge(gate_cleared, 1)
            sp.dma_start(gate_row[0:1, :], b_ada[:, 2 * D:3 * D]).then_inc(gate_rows_loaded, 16)

            def load_blocks(b, last=False):
                for g in range(GROUPS):
                    if g + 1 < GROUPS:
                        load_pooled(b, g + 1)
                    elif not last:
                        load_pooled(b + 1, 0)
                    load_pool_gate(b, g)
                    if g % 2 == 0:
                        e = g // 2
                        sp.wait_ge(gate_step, START + 2 * b + e - 1)
                        sp.dma_start(gate_w[e][:, :], w_ada[0, ds(P * (2 * b + e), P), 2 * D:3 * D]).then_inc(gate_loaded[e], 16)

            load_pooled(0, 0)
            with sp.Fori(0, NB - 1) as b:
                load_blocks(b)
            load_blocks(NB - 1, last=True)
            sp.wait_ge(gate_step, START + KT)
            sp.dma_start(gate_w[0][0:1, :], g_post[:, :]).then_inc(gate_rows_loaded, 16)
            sp.wait_ge(pw_ready, GROUPS)
            for e in range(2):
                load_weights(0, e, e)
            barrier(sp, 5)

            def load_gate(r, m, e):
                sp.wait_ge(gated, START + KT * r + m - 1)
                sp.dma_start(sig_in[:, e], proj[(M_BGP, M_BGG)[r] + m]).then_inc(sig_loaded[e], 16)
                if r == 1:
                    sp.wait_ge(summed, START + m - 1)
                    sp.dma_start(src_in[:, e], y_pool[m]).then_inc(y_loaded[e], 16)

            for r in range(2):
                if r == 1:
                    sp.wait_ge(src_ready, KT)
                    for e in range(2):
                        sp.wait_ge(y_stored[e], 16 * (KT // 2))
                for e in range(2):
                    load_gate(r, e, e)
                with sp.Fori(1, KT // 2) as i:
                    for e in range(2):
                        m = 2 * i + e
                        sp.wait_ge(pj_ready, KT * r + m - 1)
                        load_weights(r, m, e)
                        load_gate(r, m, e)
                if r == 0:
                    for e in range(2):
                        sp.wait_ge(pj_ready, KT + e - 1)
                        load_weights(1, e, e)
            wo_v = w_out[0].rearrange("(k p) n -> k p n", p=P)

            def load_wo(k):
                sp.dma_start(wo_in[k][:, :], wo_v[k]).then_inc(wo_loaded[k], 16)

            sp.wait_ge(pj_ready, 2 * KT - 1)
            load_wo(0)
            sp.wait_ge(pj_ready, 2 * KT)
            load_wo(1)
            sp.wait_ge(pj_product, 2 * KT - 1)
            load_wo(2)
            load_wo(3)
            sp.wait_ge(gated, START + 2 * KT - 1)
            load_wo(4)
            load_wo(5)
            sp.wait_ge(summed, START + KT - 1)
            load_wo(6)
            load_wo(7)

            def load_merged(n, e):
                sp.dma_start(m_in[e][:, :, :], merged[:, :, ds(P * n, P)].rearrange("k p t -> p k t")).then_inc(m_loaded[e], 16)

            def load_x(n, e):
                sp.dma_start(x_in[e][:, :], x[0, ds(P * n, P), :]).then_inc(x7_loaded[e], 16)

            sp.wait_ge(y_stored[0], 16 * KT)
            sp.wait_ge(y_stored[1], 16 * (KT - 1))
            wait_h_tile(sp, 1, 0)
            sp.dma_start(m_in[0][:, 0:KT - 1, :], merged[0:KT - 1, :, 0:P].rearrange("k p t -> p k t")).then_inc(m_head_loaded, 16)
            for b in range(NB):
                sp.wait_ge(tail_ready, b + 1)
                sp.dma_start(merged[KT - 1, :, 512 * b:512 * b + 512], y_out[:, 1, 512 * b:512 * b + 512]).then_inc(tail_stored[b], 16)
                if b == 0:
                    sp.wait_ge(tail_stored[0], 16)
                    sp.dma_start(m_in[0][:, KT - 1, :], merged[KT - 1, :, 0:P]).then_inc(m_loaded[0], 16)
                    load_merged(1, 1)
                    for e in range(2):
                        load_x(e, e)
            for b in range(1, NB):
                sp.wait_ge(tail_stored[b], 16)
            with sp.Fori(0, T // P // 2 - 1) as i:
                for e in range(2):
                    n = 2 * i + e
                    wait_apart(sp, (m_ready, n + 2))
                    load_merged(n + 2, e)
                    wait_apart(sp, (fin_ready, n + 1))
                    sp.dma_start(out[0, ds(P * n, P), :], fin[e][:, :]).then_inc(out_stored[e], 16)
                    load_x(n + 2, e)
            for e in range(2):
                n = T // P - 2 + e
                sp.wait_ge(fin_ready, n + 1)
                sp.dma_start(out[0, P * n:P * n + P, :], fin[e][:, :]).then_inc(out_stored[e], 16)
            for e in range(2):
                sp.wait_ge(out_stored[e], 16 * (1 + T // P // 2))
            barrier(sp, 6)

        @block.tensor
        def _(pe):
            pe.sem_inc(product_done, START)
            pe.wait_ge(consts_ready, 1)
            pe.wait_ge(rows_loaded, 16 * 7)
            pe.transpose(ps[:, 7, 0:P], rows[:, :], ident[:, :]).then_inc(vecs_turned, 1)
            for n in range(8):
                pe.wait_ge(ada_step, 2 * KT * (n // 2 + 1))
                for m in range(2):
                    last = pe.matmul(ps[:, 6, 2 * n + m:2 * n + m + 1], ada_acc[:, n, P * m:P * m + P],
                                     ones[:, 0:1], start=True, stop=True)
                last.then_inc(ada_used, 1)
            for g in range(4):
                pe.wait_ge(xn_ready, g + 1)
                for k in range(KT):
                    n = KT * g + k
                    if n >= 4:
                        pe.wait_ge(full_ready, n - 3)
                    for t in range(4):
                        last = pe.transpose(ps[:, n % 4, P * t:P * t + P], xin[:, g % 3, t, P * k:P * k + P], ident[:, :])
                    last.then_inc(x_turned, 1)
            barrier(pe, 1)

            def tile_product(s):
                for k in range(KT):
                    last = split_product(pe, banks(s), w_hi[s][:, k], w_lo[s][:, k], h_hi, h_lo, k, k == 0, k == KT - 1)
                last.then_inc(product_done, 1)

            pe.wait_ge(w_ready, START + 1)
            tile_product(0)
            with pe.Fori(0, HEADS) as h:
                for e in range(2):
                    s = 1 - e
                    pe.wait_ge(w_ready, START + 2 * h + e + 2)
                    pe.wait_ge(ps_free[s], h + e + 1)
                    tile_product(s)
            with pe.Fori(0, 2 * HEADS) as j:
                for t in range(TURN):
                    s = slot(t)
                    pe.wait_ge(ps_free[s], in_slot(s, j, t) + 1)
                    pe.wait_ge(w_ready, START + FIRST_TILES + TURN * j + t + 1)
                    if t - 1 in DECAY_IN:
                        pe.wait_ge(z_free, 2 * j + DECAY_IN.index(t - 1) + 1)
                    for k in range(KT):
                        if t in DECAY_IN and k == KT // 2:
                            d, other = DECAY_IN.index(t), 1 - s
                            pe.wait_ge(ps_free[other], in_slot(other, j, t) + 1)
                            if d == 0:
                                pe.wait_ge(lr_ready, j + 1)
                            for b in range(2):
                                last = pe.matmul(banks(other)[:, b], gk_split[:, d, :], lr_split[:, 512 * b:512 * b + 512],
                                                 start=True, stop=True)
                            last.then_inc(z_done, 1)
                        last = split_product(pe, banks(s), w_hi[s][:, k], w_lo[s][:, k], h_hi, h_lo, k, k == 0, k == KT - 1)
                    last.then_inc(product_done, 1)
            barrier(pe, 2)

            def kv_turn(n, g, q, s):
                pe.wait_ge(kv_copied, START + n - 1)
                pe.transpose(ps[:, s, 0:P], kb_in[g][:, q, :], ident[:, :])
                for half in range(2):
                    last = pe.transpose(ps[:, s, P + P * half:2 * P + P * half],
                                        vt_in[g][:, half, UNIT * q:UNIT * q + UNIT], ident[:, :])
                last.then_inc(kv_turned, 1)

            def kv_multiply(n, s):
                wait_apart(pe, (kv_copied, START + n + 1), (zb_ready, START + n - 1))
                pe.matmul(ps[:, 2 + s, 0:HEAD_V], kb_tok[s][:, :], v_all[:, UNITS - 1 - n, :],
                          start=True, stop=True).then_inc(kv_product, 1)

            with pe.Fori(0, HEADS) as b:
                for e in range(UPH):
                    n = UPH * b + e
                    if e % 4 == 0:
                        pe.wait_ge(kb_loaded[e // 4], 32 * b + 32)
                    kv_turn(n, e // 4, 3 - e % 4, e % 2)
                    if e:
                        kv_multiply(n - 1, (e - 1) % 2)
                kv_multiply(UPH * b + UPH - 1, 1)
            sweep_barrier(pe)

            def scores(b, e):
                n, g, q, s = 8 * b + e, e // 4, e % 4, e % 2
                if q == 0:
                    pe.wait_ge(dec_loaded[g], 16 * b + 16)
                pe.wait_ge(score_ready, START + n - 1)
                pe.transpose(ps[:, s, 0:P], dec_u[g][:, q, 2, :], ident[:, :])
                for d in range(2):
                    last = pe.matmul(ps[:, s, P + P * d:2 * P + P * d], dec_u[g][:, q, 2 + d, :], dec_u[g][:, q, d, :],
                                     start=True, stop=True)
                last.then_inc(scores_done, 1)

            def attend(b, e):
                n, g, q, s = 8 * b + e, e // 4, e % 4, e % 2
                pe.wait_ge(kf_copied, START + n + 1)
                pe.wait_ge(zf_ready, START + n - 1)
                pe.matmul(ps[:, 2 + s, 0:HEAD_V], kf_tok[s][:, :], v_all[:, n, :], start=True, stop=True).then_inc(states_product, 1)
                pe.wait_ge(normed, START + n - 1)
                o = ps[:, 4 + s, 0:HEAD_V]
                pe.matmul(o, dec_u[g][:, q, 1, :], sb_all[:, n, :], start=True, stop=False)
                pe.wait_ge(score_ready, START + n + 1)
                pe.matmul(o, score[s][:, :], v_all[:, n, :], start=False, stop=False)
                pe.wait_ge(sf_ready, START + n + 1)
                pe.matmul(o, dec_u[g][:, q, 0, :], sf[s][:, :], start=False, stop=True).then_inc(attn_done, 1)

            def turn(b, e):
                n, s = 8 * b + e, e % 2
                pe.wait_ge(normed, START + n + 1)
                pe.wait_ge(og_ready, START + n - 1)
                for half in range(2):
                    last = pe.transpose(ps[:, 6 + s, P * half:P * half + P], o_n[s][:, P * half:P * half + P], ident[:, :])
                last.then_inc(o_turned, 1)

            def units(b, first=False, last=False):
                for e in range(8):
                    if e < 7:
                        scores(b, e + 1)
                    elif not last:
                        scores(b + 1, 0)
                    attend(b, e)
                    if e:
                        turn(b, e - 1)
                    elif not first:
                        turn(b - 1, 7)

            scores(0, 0)
            units(0, first=True)
            with pe.Fori(1, UNITS // 8 - 1) as b:
                units(b)
            units(UNITS // 8 - 1, last=True)
            turn(UNITS // 8 - 1, 7)
            barrier(pe, 4)

            pe.wait_ge(credits_given, 1)
            pe.wait_ge(pw_ready, GROUPS)
            with pe.Fori(0, NB) as b:
                for g in range(GROUPS):
                    s = g % 2
                    pe.wait_ge(pooled_ready, START + GROUPS * b + g + 1)
                    pe.wait_ge(pa_ready, START + GROUPS * b + g - 1)
                    for dh in range(2):
                        cols = slice(P * dh, P * dh + P)
                        bank = ps[:, 2 * s + dh]
                        for a in range(2):
                            pe.matmul(bank, pw_hi[:, g, a, cols], pooled_hi[s][:, a, :], start=(a == 0), stop=False)
                            pe.matmul(bank, pw_hi[:, g, a, cols], pooled_lo[s][:, a, :], start=False, stop=False)
                            last = pe.matmul(bank, pw_lo[:, g, a, cols], pooled_hi[s][:, a, :], start=False, stop=(a == 1))
                    last.then_inc(pool_product, 1)
            pe.wait_ge(gate_step, START + KT)
            for b in range(2):
                pe.matmul(ps[:, 4 + b], ones[:, :], gate_row[:, 512 * b:512 * b + 512], start=True, stop=True)
            pe.wait_ge(gate_rows_loaded, 32)
            for b in range(2):
                last = pe.matmul(ps[:, 6 + b], ones[0:1, :], gate_w[0][0:1, 512 * b:512 * b + 512], start=True, stop=True)
            last.then_inc(gate_spread, 1)
            barrier(pe, 5, waits=False)

            pe.wait_ge(pa_ready, START + GROUPS * NB)
            for r in range(2):
                with pe.Fori(0, KT // 2) as i:
                    for e in range(2):
                        m = 2 * i + e
                        pe.wait_ge(pj_ready, KT * r + m + 1)
                        pe.wait_ge(gated, START + KT * r + m - 1)
                        if r == 0 and e == 1:
                            pe.wait_ge(gate_ready, 1)
                        for k in range(KT):
                            if r == 0:
                                pe.wait_ge(pa_split, START + GROUPS * (NB - 1) + k // 2 + 1)
                            else:
                                pe.wait_ge(src_ready, k + 1)
                            last = split_product(pe, banks(e), w_hi[e][:, k], w_lo[e][:, k], h_hi, h_lo, k, k == 0, k == KT - 1)
                            if k < KT - 1:
                                last.then_inc(h_tile_used, 1)
                        last.then_inc(pj_product, 1)
            def token_product(n, e, ready, first=False):
                pe.wait_ge(m_ready, ready)
                pe.wait_ge(normed7, START + n - 1)
                for k in range(KT):
                    if first:
                        pe.wait_ge(wo_ready, k + 1)
                        if k == KT - 1:
                            pe.wait_ge(m_ready, 2)
                    for lhs, rhs in ((m_hi, wo_hi), (m_hi, wo_lo), (m_lo, wo_hi)):
                        for b in range(2):
                            last = pe.matmul(ps[:, 2 * e + b], lhs[e][:, k, :], rhs[:, k, 512 * b:512 * b + 512],
                                             start=(k == 0 and lhs is m_hi and rhs is wo_hi),
                                             stop=(k == KT - 1 and lhs is m_lo))
                last.then_inc(out_product, 1)

            token_product(0, 0, 1, first=True)
            with pe.Fori(0, T // P // 2 - 1) as i:
                token_product(2 * i + 1, 1, 2 * i + 3)
                token_product(2 * i + 2, 0, 2 * i + 4)
            token_product(T // P - 1, 1, T // P + 1)
            barrier(pe, 6)

        @block.scalar
        def _(act):
            act.wait_ge(rows_cleared, 1)
            load_rows(act, ((V_PSCALE, 8, pool_scale), (V_GKB, 4, gk_bias_fwd), (V_GKB + 4, 4, gk_bias_bwd),
                            (V_GNORM, 2, gla_norm_g)))
            act.wait_ge(vecs_ready, 1)
            act.activation(c_act[:, :], vecs[:, V_C:V_C + KT], ACT.Silu).then_inc(c_ready, 1)

            def square(g, t):
                if g or t:
                    act.wait_ge(sumsq_ready, 4 * g + t)
                act.activation(flat(ps[:, 4:6]), xin[:, g % 3, t], ACT.Square,
                               accum_out=sumsq[:, 4 * g + t:4 * g + t + 1]).then_inc(sumsq_ready, 1)
                if t == 3:
                    act.wait_ge(var_ready, g + 1)
                    act.activation(rstd[:, 4 * g:4 * g + 4], rstd[:, 4 * g:4 * g + 4], ACT.Sqrt).then_inc(std_ready, 1)

            def row_squares(g):
                act.wait_ge(x_loaded[g], 16)
                for t in range(4):
                    square(g, t)

            row_squares(0)
            row_squares(1)
            for g in range(4):
                for k in range(KT):
                    n = KT * g + k
                    if g < 2 and k == 0:
                        act.wait_ge(x_loaded[(g + 2) % 3], 16 * ((g + 2) // 3 + 1))
                    if g < 2 and k % 2:
                        square(g + 2, k // 2)
                    act.wait_ge(full_ready, n + 1)
                    act.activation(h_hi[:, k, 512 * g:512 * g + 512], h_full[n % 4][:, :], ACT.Copy).then_inc(hi_ready, 1)
            act.wait_ge(w_loaded[0], 16)
            act.activation(w_hi[0][:, :, :], stage[:, 0], ACT.Copy).then_inc(w_hi_ready, 1)
            barrier(act, 1)

            def evacuate(n_use, ps_slot, out_slot, stored, func, scale=1.0):
                act.wait_ge(product_done, START + n_use + 1)
                act.wait_ge(tile_free[out_slot], stored)
                act.activation(tile_out[:, out_slot], flat(banks(ps_slot)), func, scale=scale).then_inc(tile_ready, 1)

            evacuate(0, 0, 0, 1, ACT.Copy)
            act.wait_ge(tile_ready, 1)
            act.sem_inc(ps_free[0], 1)
            with act.Fori(0, HEADS) as h:
                for e in range(2):
                    evacuate(2 * h + e + 1, 1 - e, 1 - e, h + e + 1, ACT.Copy,
                             scale=float(P) ** -0.5 if e == 0 else 1.0)
                    act.wait_ge(tile_ready, 2 * h + e + 2)
                    act.sem_inc(ps_free[1 - e], 1)
            with act.Fori(0, HEADS) as h:
                with act.Fori(0, 2) as s2:
                    j = 2 * h + s2
                    for t, name in enumerate(TILES):
                        if t in DECAY_IN:
                            d = DECAY_IN.index(t)
                            z = flat(banks(1 - slot(t))[:, 0:2])
                            act.wait_ge(z_done, 2 * j + d + 1)
                            act.activation(dec_a[:, :], z, ACT.Abs, bias=vecs[:, ds(V_GKB + HEADS * d + h, 1)]).then_inc(abs_done, 1)
                            act.wait_ge(abs_done, 2 * j + d + 1)
                            act.activation(dec_a[:, :], dec_a[:, :], ACT.Exp, scale=-1.0).then_inc(expneg_done, 1)
                            act.wait_ge(expneg_done, 2 * j + d + 1)
                            act.activation(dec_a[:, :], dec_a[:, :], ACT.Ln, bias=one_col[:, :]).then_inc(logsig_ready, 1)
                            act.wait_ge(centred, 2 * j + d + 1)
                            sign = (1.0 if d == 0 else -1.0) / NORMALIZER
                            act.wait_ge(decay_free, 2 * j + d + 1)
                            act.activation(q_dec[:, :], dec_a[:, :], ACT.Exp, scale=sign)
                            act.activation(k_dec[:, :], dec_a[:, :], ACT.Exp, scale=-sign).then_inc(exps_ready, 1)
                        s = slot(t)
                        evacuate(FIRST_TILES + TURN * j + t, s, s, in_slot(s, j, t) + 1, FUNC[name])
                        act.wait_ge(tile_ready, FIRST_TILES + TURN * j + t + 1)
                        act.sem_inc(ps_free[s], 1)
            barrier(act, 2)

            for d in range(2):
                act.wait_ge(into_sum, 2 * d + 2)
                act.activation(into[:, d], into_tmp[:, d], ACT.Exp, scale=1.0 / NORMALIZER).then_inc(into_ready, 1)
            with act.Fori(0, UNITS // 2) as i:
                for e in range(2):
                    n = 2 * i + e
                    act.wait_ge(kv_turned, n + 1)
                    act.wait_ge(kv_product, START + n - 1)
                    act.activation(kb_tok[e][:, :], ps[:, e, 0:P], ACT.Copy)
                    act.activation(v_all[:, UNITS - 1 - n, :], ps[:, e, P:3 * P], ACT.Copy).then_inc(kv_copied, 1)
            sweep_barrier(act)

            def copies(b, e):
                n, s = 8 * b + e, e % 2
                act.wait_ge(scores_done, n + 1)
                act.wait_ge(states_product, START + n - 1)
                act.activation(kf_tok[s][:, :], ps[:, s, 0:P], ACT.Copy).then_inc(kf_copied, 1)
                act.wait_ge(attn_done, START + n - 1)
                act.activation(score[s][:, :], ps[:, s, P:2 * P], ACT.Copy).then_inc(score_copied, 1)
                act.wait_ge(zf_ready, START + n)
                act.activation(sf[s][:, :], zf[1 - s][:, :], ACT.Copy, scale=into[:, 0, ds(n, 1)]).then_inc(sf_ready, 1)

            def head_norm(b, e):
                n, s = 8 * b + e, e % 2
                act.wait_ge(attn_done, START + n + 1)
                act.wait_ge(rs_ready, START + n - 1)
                act.activation(o_sq[s][:, :], ps[:, 4 + s, 0:HEAD_V], ACT.Square, accum_out=o_ss[s][:, 0:1]).then_inc(ss_ready, 1)
                act.wait_ge(ss_ready, n + 1)
                act.activation(o_ss[s][:, 1:2], o_ss[s][:, 0:1], ACT.Sqrt, scale=1.0 / HEAD_V,
                               bias=eps_col[:, :]).then_inc(sd_ready, 1)

            def units(b, last=False):
                for e in range(8):
                    if e < 7:
                        copies(b, e + 1)
                    elif not last:
                        copies(b + 1, 0)
                    head_norm(b, e)

            act.activation(o_ss[0][:, 3:4], eps_col[:, :], ACT.Sqrt)
            act.wait_ge(zf_cleared, 1)
            copies(0, 0)
            with act.Fori(0, UNITS // 8 - 1) as b:
                units(b)
            units(UNITS // 8 - 1, last=True)
            barrier(act, 4)

            act.wait_ge(credits_given, 1)
            act.wait_ge(pw_loaded, 16)
            for g in range(GROUPS):
                act.activation(pw_hi[:, g], pw_in[:, g], ACT.Copy).then_inc(pw_hi_ready, 1)

            def split_pooled(b, g):
                s = g % 2
                act.wait_ge(pooled_loaded[s], 32 * b + 16 * (g // 2) + 16)
                act.wait_ge(pool_product, START + GROUPS * b + g - 1)
                act.activation(pooled_hi[s][:, :, :], pooled_in[s][:, :, :], ACT.Copy).then_inc(pooled_hi_ready, 1)

            def split_result(b, g):
                act.wait_ge(pa_ready, START + GROUPS * b + g + 1)
                act.activation(h_hi[:, 2 * g:2 * g + 2, ds(512 * b, 512)], pa[g % 2][:, :, :], ACT.Copy).then_inc(pa_hi_ready, 1)

            split_pooled(0, 0)
            with act.Fori(0, NB - 1) as b:
                for g in range(GROUPS):
                    split_pooled(*((b, g + 1) if g + 1 < GROUPS else (b + 1, 0)))
                    split_result(b, g)
            for g in range(GROUPS):
                if g + 1 < GROUPS:
                    split_pooled(NB - 1, g + 1)
                split_result(NB - 1, g)

            def load_source(k):
                u = k // 2 * NB
                act.dma_start(src_in[:, k % 2].rearrange("p (u t) -> p u t", t=512),
                              gla_out[u:u + NB, k % 2].rearrange("u p t -> p u t")).then_inc(src_loaded[k % 2], 16)

            barrier(act, 5)

            for g in range(2):
                act.wait_ge(og_stored[g], 16 * (1 + UNITS // 8))
            for k in range(2):
                load_source(k)
            for k in range(KT):
                wait_h_tile(act, 0, k)
                act.wait_ge(src_loaded[k % 2], 16 * (k // 2 + 1))
                act.activation(h_hi[:, k, :], src_in[:, k % 2], ACT.Copy).then_inc(src_hi, 1)
                if k + 2 < KT:
                    act.wait_ge(src_ready, k + 1)
                    load_source(k + 2)
            for k in range(KT):
                act.wait_ge(wo_loaded[k], 16)
                wait_h_tile(act, 1, k // 2)
                act.activation(wo_hi[:, k, :], wo_in[k][:, :], ACT.Copy).then_inc(wo_hi_ready, 1)
            wait_h_tile(act, 1, 1)
            act.wait_ge(m_head_loaded, 16)
            act.activation(m_hi[0][:, 0:KT - 1, :], m_in[0][:, 0:KT - 1, :], ACT.Copy).then_inc(m_hi_ready, 1)
            act.wait_ge(m_loaded[0], 16)
            act.activation(m_hi[0][:, KT - 1, :], m_in[0][:, KT - 1, :], ACT.Copy).then_inc(m_hi_ready, 1)

            def split_tokens(n, e, i):
                act.wait_ge(m_loaded[e], 16 * i + 16)
                act.wait_ge(out_product, START + n - 1)
                act.activation(m_hi[e][:, :, :], m_in[e][:, :, :], ACT.Copy).then_inc(m_hi_ready, 1)

            def row_root(n, e):
                act.wait_ge(out_product, START + n + 1)
                act.activation(fin_sq[e][:, :], flat(ps[:, 2 * e:2 * e + 2]), ACT.Square,
                               accum_out=fin_s[e][:, 0:1]).then_inc(ss7_ready, 1)
                act.wait_ge(ss7_ready, n + 1)
                act.activation(fin_s[e][:, 1:2], fin_s[e][:, 0:1], ACT.Sqrt, scale=1.0 / D,
                               bias=eps_col[:, :]).then_inc(sd7_ready, 1)

            LAST = T // P - 2
            with act.Fori(0, T // P // 2 - 1) as i:
                split_tokens(2 * i + 1, 1, i)
                row_root(2 * i, 0)
                split_tokens(2 * i + 2, 0, i + 1)
                row_root(2 * i + 1, 1)
            split_tokens(LAST + 1, 1, LAST // 2)
            row_root(LAST, 0)
            row_root(LAST + 1, 1)
            barrier(act, 6)

        @block.vector
        def _(dve):
            for s in (w_ready, decayed_ready, zb_ready, sb_ready, kv_copied, score_ready, kf_copied, zf_ready, normed,
                      o_turned, sd_ready, rs_ready, sf_ready, og_ready, attn_done, states_product, kv_product):
                dve.sem_inc(s, START)
            for s in (*ps_free, *tile_free, decay_free):
                dve.sem_inc(s, 1)
            for s in (*og_stored, *out_stored):
                dve.sem_inc(s, 16)
            dve.wait_ge(vecs_turned, 1)
            dve.tensor_copy(vecs[:, :], ps[:, 7, 0:P]).then_inc(vecs_ready, 1)
            dve.wait_ge(vecs_ready, 1)
            for r in range(KT // 2):
                dve.tensor_copy(gnorm8[:, 2 * r:2 * r + 2], vecs[:, V_GNORM:V_GNORM + 2])

            def inverse_rms(g):
                dve.wait_ge(sumsq_ready, 4 * g + 4)
                cols = slice(4 * g, 4 * g + 4)
                dve.tensor_scalar(rstd[:, cols], sumsq[:, cols], 1.0 / D, EPS, ALU.mult, ALU.add).then_inc(var_ready, 1)
                dve.wait_ge(std_ready, g + 1)
                dve.reciprocal(rstd[:, cols], rstd[:, cols]).then_inc(rstd_ready, 1)
                dve.wait_ge(rstd_ready, g + 1)
                for t in range(4):
                    last = dve.tensor_scalar(xin[:, g % 3, t], xin[:, g % 3, t], rstd[:, 4 * g + t:4 * g + t + 1], None, ALU.mult)
                last.then_inc(xn_ready, 1)

            def ada_sums(p):
                dve.wait_ge(ada_loaded[p], 32)
                for k in range(KT):
                    for u in range(2):
                        n, done = 2 * p + u, 2 * KT * p + 2 * k + u
                        if k == 0:
                            dve.tensor_scalar(ada_acc[:, n], ada_w[:, n, k], c_act[:, k:k + 1], None, ALU.mult).then_inc(ada_step, 1)
                        else:
                            dve.wait_ge(ada_step, done - 1)
                            dve.scalar_tensor_tensor(ada_acc[:, n], ada_w[:, n, k], c_act[:, k:k + 1], ada_acc[:, n],
                                                     ALU.mult, ALU.add).then_inc(ada_step, 1)

            dve.wait_ge(c_ready, 1)
            ada_sums(0)
            inverse_rms(0)
            ada_sums(1)
            ada_sums(2)
            ada_sums(3)
            dve.wait_ge(ada_used, 8)
            dve.tensor_tensor(h_shift[:, :], ps[:, 6, 0:KT], vecs[:, V_BADA:V_BADA + KT], ALU.add).then_inc(mod_ready, 1)
            dve.scalar_tensor_tensor(h_scale[:, :], ps[:, 6, KT:2 * KT], 1.0, vecs[:, V_BADA + KT:V_BADA + 2 * KT],
                                     ALU.add, ALU.add).then_inc(mod_part, 1)
            dve.wait_ge(mod_part, 1)
            dve.tensor_tensor(h_scale[:, :], h_scale[:, :], vecs[:, V_GPRE:V_GPRE + KT], ALU.mult).then_inc(mod_ready, 1)
            dve.wait_ge(mod_ready, 2)

            def odd_lo(n):
                g, k = n // KT, n % KT
                cols = slice(512 * g, 512 * g + 512)
                dve.wait_ge(hi_ready, n + 1)
                dve.tensor_tensor(h_lo[:, k, cols], h_full[n % 4][:, :], h_hi[:, k, cols].bitcast(F32), ALU.subtract).then_inc(lo_ready_dve, 1)

            inverse_rms(1)
            for g in range(4):
                if g in (1, 2):
                    inverse_rms(g + 1)
                for k in range(KT):
                    n = KT * g + k
                    dve.wait_ge(x_turned, n + 1)
                    if n >= 4:
                        dve.wait_ge(*((lo_ready_dve, n // 2 - 1) if n % 2 else (lo_ready, n // 2 - 1)))
                    dve.tensor_scalar(h_full[n % 4][:, :], ps[:, n % 4], h_scale[:, k:k + 1], h_shift[:, k:k + 1],
                                      ALU.mult, ALU.add).then_inc(full_ready, 1)
                    if n % 2 == 0 and n:
                        odd_lo(n - 1)
            odd_lo(4 * KT - 1)
            dve.wait_ge(w_hi_ready, 1)
            dve.tensor_tensor(w_lo[0][:, :, :], stage[:, 0], w_hi[0][:, :, :].bitcast(F32), ALU.subtract).then_inc(w_ready, 1)
            barrier(dve, 1)

            def split_weights(s, hi_sem, ready_sem, count):
                dve.tensor_copy(w_hi[s][:, :, :], stage[:, s]).then_inc(hi_sem, 1)
                dve.wait_ge(hi_sem, count + 1)
                dve.tensor_tensor(w_lo[s][:, :, :], stage[:, s], w_hi[s][:, :, :].bitcast(F32), ALU.subtract).then_inc(ready_sem, 1)

            dve.wait_ge(pool_consts, 3)
            with dve.Fori(0, HEADS) as h:
                for e in range(2):
                    s = 1 - e
                    dve.wait_ge(product_done, START + 2 * h + e)
                    dve.wait_ge(w_loaded[s], 16 * h + 16 * e + 16)
                    split_weights(s, w_hi_ready, w_ready, 2 * h + e + 1)
            with dve.Fori(0, HEADS) as h:
                with dve.Fori(0, 2) as s2:
                    j = 2 * h + s2

                    def split_tile(t):
                        dve.wait_ge(product_done, START + FIRST_TILES + TURN * j + t - 1)
                        dve.wait_ge(w_loaded[slot(t)], 16 * in_slot(slot(t), j, t) + 16)
                        split_weights(slot(t), w_hi_ready, w_ready, FIRST_TILES + TURN * j + t)

                    def scale_tile(t, col):
                        dve.wait_ge(tile_ready, FIRST_TILES + TURN * j + t + 1)
                        dve.tensor_scalar(tile_out[:, slot(t)], tile_out[:, slot(t)], col, None, ALU.mult).then_inc(tile_scaled, 1)

                    def decay(d):
                        n = 2 * j + d
                        z = flat(banks(1 - slot(DECAY_IN[d]))[:, 0:2]).rearrange("p (u t) -> p u t", t=UNIT)
                        a = dec_a[:, :].rearrange("p (u t) -> p u t", t=UNIT)
                        dve.wait_ge(abs_done, n + 1)
                        dve.tensor_scalar(dec_in[:, :, 1:UNIT + 1], z, vecs[:, ds(V_GKB + HEADS * d + h, 1)], 0.0,
                                          ALU.add, ALU.min).then_inc(min_done, 1)
                        dve.wait_ge(min_done, n + 1)
                        dve.wait_ge(logsig_ready, n + 1)
                        dve.sem_inc(z_free, 1)
                        dve.tensor_tensor(dec_in[:, :, 1:UNIT + 1], dec_in[:, :, 1:UNIT + 1], a, ALU.subtract).then_inc(la_done, 1)
                        dve.wait_ge(la_done, n + 1)
                        dve.tensor_tensor_scan(flat(dec_sum[:, :, :]), flat(run_on[:, :, :]), flat(dec_in[:, :, :]), 0.0,
                                               ALU.mult, ALU.add).then_inc(scan_done, 1)
                        dve.wait_ge(scan_done, n + 1)
                        dve.tensor_copy(mid[:, d, ds(HU * j + 1, HU)], dec_sum[:, :, UNIT // 2])
                        dve.tensor_copy(tot[:, d, ds(HU * j + 1, HU)], dec_sum[:, :, UNIT])
                        own = dec_sum[:, :, 1 - d:1 - d + UNIT]
                        dve.tensor_tensor(a, own, dec_sum[:, :, UNIT // 2:UNIT // 2 + 1].to_broadcast([P, HU, UNIT]),
                                          ALU.subtract).then_inc(centred, 1)

                    def split_low_rank():
                        dve.wait_ge(lr_loaded, 64 * j + 64)
                        dve.wait_ge(gk_loaded, 128 * j + 128)
                        dve.tensor_copy(gk_split[:, :, :], gk_in[:, :, :])
                        dve.tensor_copy(lr_split[:, :], lr_in[:, :]).then_inc(lr_hi_ready, 1)
                        dve.wait_ge(lr_hi_ready, j + 1)
                        low = slice(4 * RANK, 8 * RANK)
                        dve.tensor_tensor(gk_split[low, :, :], gk_in[low, :, :], gk_split[low, :, :].bitcast(F32), ALU.subtract)
                        for at in (2 * RANK, 6 * RANK):
                            low = slice(at, at + 2 * RANK)
                            last = dve.tensor_tensor(lr_split[low, :], lr_in[low, :], lr_split[low, :].bitcast(F32), ALU.subtract)
                        last.then_inc(lr_ready, 1)

                    split_tile(0)
                    split_tile(1)
                    split_low_rank()
                    split_tile(2)
                    split_tile(3)
                    scale_tile(1, vecs[:, ds(V_PSCALE + j, 1)])
                    decay(0)
                    split_tile(4)
                    split_tile(5)
                    scale_tile(3, gnorm8[:, ds(j, 1)])
                    decay(1)
            barrier(dve, 2)

            for d in range(2):
                dve.tensor_tensor(into_tmp[:, d], tot[:, d, d:d + UNITS], mid[:, d, d:d + UNITS], ALU.subtract).then_inc(into_sum, 1)
                dve.wait_ge(into_sum, 2 * d + 1)
                dve.tensor_tensor(into_tmp[:, d], into_tmp[:, d], mid[:, d, d + 1:d + 1 + UNITS], ALU.add).then_inc(into_sum, 1)
            dve.wait_ge(into_ready, 2)
            dve.memset(into[:, 0, 0:UNITS:UPH], 0.0)
            with dve.Fori(0, HEADS) as hh:
                dve.wait_ge(zb_ready, START + UPH * hh)
                dve.memset(zb[3][:, :], 0.0).then_inc(zb_cleared, 1)
                wait_apart(dve, (zb_cleared, hh + 1))
                with dve.Fori(0, UPH // 4) as i:
                    for e in range(4):
                        n = UPH * hh + 4 * i + e
                        factor = into[:, 1, ds(UNITS - 1 - n, 1)]
                        before, after = zb[(e - 1) % 4], zb[e]
                        wait_apart(dve, (kv_product, START + n + 1), (sb_ready, START + n - 1), (zb_ready, START + n))
                        dve.scalar_tensor_tensor(after[:, :], before[:, :], factor, ps[:, 2 + e % 2, 0:HEAD_V],
                                                 ALU.mult, ALU.add).then_inc(zb_ready, 1)
                        dve.tensor_scalar(sb_all[:, UNITS - 1 - n, :], before[:, :], factor, None, ALU.mult).then_inc(sb_ready, 1)
            sweep_barrier(dve)

            def choose(b, e):
                n, s = 8 * b + e, e % 2
                wait_apart(dve, (scores_done, n + 1), (score_copied, n + 1))
                dve.copy_predicated(score[s][:, :], later[:, :], ps[:, s, 2 * P:3 * P]).then_inc(score_ready, 1)

            def add_state(b, e):
                n, s = 8 * b + e, e % 2
                dve.wait_ge(states_product, START + n + 1)
                dve.wait_ge(sf_ready, START + n)
                dve.wait_ge(zf_ready, START + n)
                dve.scalar_tensor_tensor(zf[s][:, :], zf[1 - s][:, :], into[:, 0, ds(n, 1)],
                                         ps[:, 2 + s, 0:HEAD_V], ALU.mult, ALU.add).then_inc(zf_ready, 1)

            def normalize(b, e):
                n, s = 8 * b + e, e % 2
                dve.wait_ge(sd_ready, START + n + 1)
                dve.reciprocal(o_ss[s][:, 2:3], o_ss[s][:, 1:2]).then_inc(rs_ready, 1)
                dve.wait_ge(rs_ready, START + n + 1)
                dve.wait_ge(o_turned, START + n - 1)
                dve.tensor_scalar(o_n[s][:, :], ps[:, 4 + s, 0:HEAD_V], o_ss[s][:, 2:3], None, ALU.mult).then_inc(normed, 1)

            def gate(b, e):
                n, g, s = 8 * b + e, e // 4, e % 2
                cols = slice(UNIT * (e % 4), UNIT * (e % 4) + UNIT)
                if e % 4 == 0:
                    dve.wait_ge(gla_gate_loaded[g], 16 * b + 16)
                    dve.wait_ge(og_stored[g], 16 * b + 16)
                dve.wait_ge(o_turned, START + n + 1)
                dve.tensor_tensor(o_g[g][:, :, cols], ps[:, 6 + s, 0:HEAD_V].rearrange("p (a t) -> p a t", a=2),
                                  gate_u[g][:, :, cols], ALU.mult).then_inc(og_ready, 1)

            def units(b, first=False, last=False):
                for e in range(8):
                    if e < 7:
                        choose(b, e + 1)
                    elif not last:
                        choose(b + 1, 0)
                    add_state(b, e)
                    normalize(b, e)
                    if e:
                        gate(b, e - 1)
                    elif not first:
                        gate(b - 1, 7)

            dve.memset(zf[1][:, :], 0.0).then_inc(zf_cleared, 1)
            dve.wait_ge(zf_cleared, 1)
            choose(0, 0)
            units(0, first=True)
            with dve.Fori(1, UNITS // 8 - 1) as b:
                units(b)
            units(UNITS // 8 - 1, last=True)
            gate(UNITS // 8 - 1, 7)
            barrier(dve, 4)

            for s in (gate_step, gated, summed, out_product, normed7, pooled_ready, pa_ready, pool_product, pa_split):
                dve.sem_inc(s, START)
            for s in y_free:
                dve.sem_inc(s, 1)
            dve.sem_inc(credits_given, 1)
            dve.memset(gate_row[:, :], 0.0).then_inc(gate_cleared, 1)

            for g in range(GROUPS):
                dve.wait_ge(pw_hi_ready, g + 1)
                dve.tensor_tensor(pw_lo[:, g], pw_in[:, g], pw_hi[:, g].bitcast(F32), ALU.subtract).then_inc(pw_ready, 1)

            def split_pooled(b, g):
                s = g % 2
                dve.wait_ge(pooled_hi_ready, GROUPS * b + g + 1)
                dve.tensor_tensor(pooled_lo[s][:, :, :], pooled_in[s][:, :, :], pooled_hi[s][:, :, :].bitcast(F32),
                                  ALU.subtract).then_inc(pooled_ready, 1)

            def gate_result(b, g):
                s = g % 2
                dve.wait_ge(pool_product, START + GROUPS * b + g + 1)
                dve.wait_ge(pg_loaded[s], 32 * b + 16 * (g // 2) + 16)
                dve.wait_ge(pa_split, START + GROUPS * b + g - 1)
                dve.tensor_tensor(pa[s][:, :, :], ps[:, 2 * s:2 * s + 2], pg_in[s][:, :, :], ALU.mult).then_inc(pa_ready, 1)

            def split_next(r, m, e, i):
                dve.wait_ge(pj_loaded[e], 16 * (KT // 2) * r + 16 * i + 16)
                split_weights(e, pj_hi_ready, pj_ready, KT * r + m)

            def add_gate_tile(b, e):
                dve.wait_ge(gate_loaded[e], 16 * b + 16)
                dve.wait_ge(gate_step, START + 2 * b + e)
                dve.scalar_tensor_tensor(gate_row[:, :], gate_w[e][:, :], c_act[:, ds(2 * b + e, 1)], gate_row[:, :],
                                         ALU.mult, ALU.add).then_inc(gate_step, 1)

            split_pooled(0, 0)
            dve.wait_ge(gate_rows_loaded, 16)
            with dve.Fori(0, NB - 1) as b:
                for g in range(GROUPS):
                    split_pooled(*((b, g + 1) if g + 1 < GROUPS else (b + 1, 0)))
                    gate_result(b, g)
                    if g % 2:
                        add_gate_tile(b, g // 2)
            for g in range(GROUPS):
                if g + 1 < GROUPS:
                    split_pooled(NB - 1, g + 1)
                gate_result(NB - 1, g)
                if g in (1, 2):
                    add_gate_tile(NB - 1, g - 1)
                if g == 2:
                    split_next(0, 0, 0, 0)
            barrier(dve, 5)
            split_next(0, 1, 1, 0)
            dve.wait_ge(gate_spread, 1)
            dve.tensor_copy(gate_row[:, :], flat(ps[:, 4:6])).then_inc(gate_sum, 1)
            dve.wait_ge(gate_sum, 1)
            dve.tensor_tensor(gate_row[:, :], gate_row[:, :], flat(ps[:, 6:8]), ALU.mult).then_inc(gate_ready, 1)

            def gate_tile(r, m, e, i):
                dve.wait_ge(pj_product, KT * r + m + 1)
                dve.wait_ge(sig_loaded[e], 16 * (KT // 2) * r + 16 * i + 16)
                dve.wait_ge(y_free[e], KT // 2 * r + i + 1)
                dve.tensor_tensor(y_out[:, e], flat(banks(e)), sig_in[:, e], ALU.mult).then_inc(gated, 1)
                if r == 1:
                    dve.wait_ge(gated, START + KT + m + 1)
                    dve.wait_ge(y_loaded[e], 16 * i + 16)
                    dve.tensor_tensor(y_out[:, e], y_out[:, e], src_in[:, e], ALU.add).then_inc(summed, 1)

            def split_source(k):
                dve.wait_ge(src_hi, k + 1)
                dve.tensor_tensor(h_lo[:, k, :], src_in[:, k % 2], h_hi[:, k, :].bitcast(F32), ALU.subtract).then_inc(src_ready, 1)

            for r in range(2):
                with dve.Fori(0, KT // 2 - 1) as i:
                    for e in range(2):
                        gate_tile(r, 2 * i + e, e, i)
                        split_next(r, 2 * i + e + 2, e, i + 1)
                gate_tile(r, KT - 2, 0, KT // 2 - 1)
                if r == 0:
                    split_next(1, 0, 0, 0)
                    for k in range(KT - 1):
                        split_source(k)
                    gate_tile(0, KT - 1, 1, KT // 2 - 1)
                    split_source(KT - 1)
                    split_next(1, 1, 1, 0)

            def split_wo(k):
                dve.wait_ge(wo_hi_ready, k + 1)
                wait_h_tile(dve, 1, KT // 2 + k // 2)
                dve.tensor_tensor(wo_lo[:, k, :], wo_in[k][:, :], wo_hi[:, k, :].bitcast(F32), ALU.subtract).then_inc(wo_ready, 1)

            for k in range(KT - 2):
                split_wo(k)
            dve.wait_ge(m_hi_ready, 1)
            dve.tensor_tensor(m_lo[0][:, 0:KT - 1, :], m_in[0][:, 0:KT - 1, :], m_hi[0][:, 0:KT - 1, :].bitcast(F32),
                              ALU.subtract).then_inc(m_ready, 1)
            dve.wait_ge(pj_product, 2 * KT)
            dve.wait_ge(sig_loaded[1], 16 * KT)
            dve.wait_ge(y_loaded[1], 16 * (KT // 2))
            dve.wait_ge(y_free[1], KT)
            for b in range(NB):
                cols = slice(512 * b, 512 * b + 512)
                dve.tensor_tensor(y_out[:, 1, cols], ps[:, 4 + b], sig_in[:, 1, cols], ALU.mult).then_inc(gated, 1)
                dve.wait_ge(gated, START + 2 * KT + b)
                dve.tensor_tensor(y_out[:, 1, cols], y_out[:, 1, cols], src_in[:, 1, cols], ALU.add).then_inc(tail_ready, 1)

            for k in range(KT - 2, KT):
                split_wo(k)
            dve.wait_ge(m_hi_ready, 2)
            dve.tensor_tensor(m_lo[0][:, KT - 1, :], m_in[0][:, KT - 1, :], m_hi[0][:, KT - 1, :].bitcast(F32),
                              ALU.subtract).then_inc(m_ready, 1)

            def split_tokens(n, e):
                dve.wait_ge(m_hi_ready, n + 2)
                dve.tensor_tensor(m_lo[e][:, :, :], m_in[e][:, :, :], m_hi[e][:, :, :].bitcast(F32), ALU.subtract).then_inc(m_ready, 1)

            def finish(n, e, i):
                dve.wait_ge(sd7_ready, n + 1)
                dve.reciprocal(fin_s[e][:, 2:3], fin_s[e][:, 1:2]).then_inc(rs7_ready, 1)
                dve.wait_ge(rs7_ready, n + 1)
                dve.wait_ge(out_stored[e], 16 * i + 16)
                dve.scalar_tensor_tensor(fin[e][:, :], flat(ps[:, 2 * e:2 * e + 2]), fin_s[e][:, 2:3], gate_row[:, :],
                                         ALU.mult, ALU.mult).then_inc(normed7, 1)
                dve.wait_ge(normed7, START + n + 1)
                dve.wait_ge(x7_loaded[e], 16 * i + 16)
                dve.tensor_tensor(fin[e][:, :], fin[e][:, :], x_in[e][:, :], ALU.add).then_inc(fin_ready, 1)

            LAST = T // P - 2
            with dve.Fori(0, T // P // 2 - 1) as i:
                split_tokens(2 * i + 1, 1)
                finish(2 * i, 0, i)
                split_tokens(2 * i + 2, 0)
                finish(2 * i + 1, 1, i)
            split_tokens(LAST + 1, 1)
            finish(LAST, 0, LAST // 2)
            finish(LAST + 1, 1, LAST // 2)
            barrier(dve, 6)

        @block.gpsimd
        def _(pool):
            pool.memset(rows[:, :], 0.0).then_inc(rows_cleared, 1)
            pool.memset(ones[:, :], 1.0)
            pool.memset(eps_col[:, :], EPS)
            pool.memset(one_col[:, :], 1.0)
            pool.memset(mid[:, :, :], 0.0)
            pool.memset(tot[:, :, :], 0.0)
            pool.memset(edge[:, :, :], 1.0).then_inc(pool_consts, 1)
            pool.wait_ge(pool_consts, 1)
            pool.affine_select(out=ident[:, :], in_=ones[:, :], compare_op=ALU.is_equal, fill=0.0, base=0,
                               pattern=[[-1, P]], channel_multiplier=1).then_inc(consts_ready, 1)
            pool.affine_select(out=later[:, :], in_=ones[:, :], compare_op=ALU.is_gt, fill=0.0, base=0,
                               pattern=[[-1, P]], channel_multiplier=1)
            for g, w in enumerate(WINDOWS):
                for t in range(w // 2):
                    pool.memset(edge[:, g, t:t + 1], w / (t + w // 2))
                for r in range(1, w // 2):
                    pool.memset(edge[:, g, 2 * PAD - r:2 * PAD - r + 1], w / (r + w // 2))
            for n in range(0, 4 * KT, 2):
                g, k = n // KT, n % KT
                pool.wait_ge(hi_ready, n + 1)
                pool.wait_ge(full_ready, n + 1)
                cols = slice(512 * g, 512 * g + 512)
                pool.tensor_tensor(h_lo[:, k, cols], h_full[n % 4][:, :], h_hi[:, k, cols].bitcast(F32),
                                   ALU.subtract).then_inc(lo_ready, 1)
            barrier(pool, 1)

            pool.memset(gk_in[:, :, :], 0.0).then_inc(gk_cleared, 1)
            pool.memset(dec_in[:, :, 0:1], 0.0)
            pool.memset(run_on[:, :, :], 1.0).then_inc(pool_consts, 1)
            pool.wait_ge(pool_consts, 2)
            pool.memset(run_on[:, :, 0:1], 0.0).then_inc(pool_consts, 1)
            def free_slot(t_slot, count):
                pool.wait_ge(tile_stored[t_slot], 16 * count)
                pool.sem_inc(tile_free[t_slot], 1)

            pool.wait_ge(tile_ready, 1)
            pool.dma_start(proj[M_LR], tile_out[:, 0]).then_inc(tile_stored[0], 16)
            with pool.Fori(0, HEADS) as h:
                for e in range(2):
                    pool.wait_ge(tile_ready, 2 * h + e + 2)
                    pool.dma_start(proj[(M_Q, M_K)[e] + h], tile_out[:, 1 - e]).then_inc(tile_stored[1 - e], 16)
                    free_slot(e, h + 1)
            with pool.Fori(0, HEADS) as h:
                with pool.Fori(0, 2) as s2:
                    j = 2 * h + s2

                    def store_tile(t):
                        name = TILES[t]
                        if name in ("p_gate", "gla_gate"):
                            wait_apart(pool, (tile_scaled, 2 * j + t // 2 + 1))
                        else:
                            pool.wait_ge(tile_ready, FIRST_TILES + TURN * j + t + 1)
                        a = tile_out[:, slot(t)]
                        if name in ("v", "gla_gate"):
                            dst = (v_ch if name == "v" else gate_ch)[ds(NB * h, NB), s2].rearrange("b p t -> p b t")
                            a = a.rearrange("p (b t) -> p b t", t=512)
                        else:
                            dst = proj[TILE_AT[name] + j]
                        pool.dma_start(dst, a).then_inc(tile_stored[slot(t)], 16)
                        other = 1 - slot(t)
                        free_slot(other, in_slot(other, j, t))

                    def apply_decay(d):
                        n = 2 * j + d
                        pool.wait_ge(exps_ready, n + 1)
                        pool.wait_ge(q_loaded, 16 * j + 16)
                        pool.wait_ge(k_loaded, 16 * j + 16)
                        pool.tensor_tensor(q_dec[:, :], q_dec[:, :], q_half[:, :], ALU.mult)
                        pool.tensor_tensor(k_dec[:, :], k_dec[:, :], k_half[:, :], ALU.mult).then_inc(decayed_ready, 1)
                        pool.wait_ge(decayed_ready, START + n + 1)
                        for a, src, stored in ((d, q_dec, qd_stored), (2 + d, k_dec, kd_stored)):
                            pool.dma_start(decayed[ds(HU * j, HU), :, a, :].rearrange("u p t -> p u t"),
                                           src[:, :].rearrange("p (u t) -> p u t", t=UNIT)).then_inc(stored, 16)
                        pool.wait_ge(qd_stored, 16 * n + 16)
                        pool.wait_ge(kd_stored, 16 * n + 16)
                        pool.sem_inc(decay_free, 1)

                    store_tile(0)
                    store_tile(1)
                    apply_decay(0)
                    store_tile(2)
                    store_tile(3)
                    apply_decay(1)
                    store_tile(4)
                    store_tile(5)
            barrier(pool, 2, storing=True)

            JOBS = [(m, s) for m in range(KT) for s in range(2)]

            def load_half(n):
                m, s = JOBS[n]
                first = PAD if s == 0 else 0
                lo = HALF * s - PAD + first
                hi = min(HALF * s + HALF + PAD, T)
                pool.dma_start(pu[n % 3][:, first:first + hi - lo], proj[M_PIN + m, :, lo:hi]).then_inc(pu_loaded[n % 3], 16)
                zeros = slice(0, PAD) if s == 0 else slice(HALF + PAD, WIDE)
                pool.memset(pu[n % 3][:, zeros], 0.0).then_inc(pool_step, 1)

            steps_done = 2
            for n in range(2):
                load_half(n)
            for n, (m, s) in enumerate(JOBS):
                w, g, u = WINDOWS[m // 2], m // 2, pu[n % 3]
                levels = len(bin(w)) - 3
                pool.wait_ge(pu_loaded[n % 3], 16 * (n // 3 + 1))
                lo, hi = 1, WIDE
                pool.wait_ge(pool_step, steps_done)
                pool.tensor_tensor(window[0][:, 1:WIDE], u[:, 0:WIDE - 1], u[:, 1:WIDE], ALU.add).then_inc(pool_step, 1)
                steps_done += 1
                for k in range(1, levels):
                    r = 2 ** (k - 1)
                    lo, hi = lo + r, hi - r
                    a, b = window[(k - 1) % 2], window[k % 2]
                    pool.wait_ge(pool_step, steps_done)
                    pool.tensor_tensor(b[:, lo:hi], a[:, lo - r:hi - r], a[:, lo + r:hi + r], ALU.add).then_inc(pool_step, 1)
                    steps_done += 1
                total = window[(levels - 1) % 2]
                at = PAD if s == 0 else HALF
                pool.wait_ge(pool_step, steps_done)
                pool.tensor_tensor(total[:, at:at + PAD], total[:, at:at + PAD], edge[:, g, PAD * s:PAD * s + PAD],
                                   ALU.mult).then_inc(pool_step, 1)
                steps_done += 1
                pool.wait_ge(pool_step, steps_done)
                inner = slice(PAD, PAD + HALF)
                pool.tensor_scalar(total[:, inner], total[:, inner], 1.0 / w, None, ALU.mult).then_inc(pool_step, 1)
                steps_done += 1
                pool.wait_ge(pool_step, steps_done)
                pool.tensor_tensor(u[:, inner], total[:, inner], u[:, inner], ALU.subtract).then_inc(pool_step, 1)
                steps_done += 1
                pool.wait_ge(pool_step, steps_done)
                pool.dma_start(pooled_ch[m, :, HALF * s:HALF * s + HALF], u[:, inner]).then_inc(pu_stored[n % 3], 16)
                if n + 2 < len(JOBS):
                    if n >= 1:
                        pool.wait_ge(pu_stored[(n + 2) % 3], 16 * ((n - 1) // 3 + 1))
                    load_half(n + 2)
                    steps_done += 1
            for s in range(3):
                pool.wait_ge(pu_stored[s], 16 * len(range(s, len(JOBS), 3)))
            barrier(pool, 4)

            pool.wait_ge(credits_given, 1)
            with pool.Fori(0, NB) as b:
                for g in range(GROUPS):
                    pool.wait_ge(pa_hi_ready, GROUPS * b + g + 1)
                    tiles, cols = slice(2 * g, 2 * g + 2), ds(512 * b, 512)
                    pool.tensor_tensor(h_lo[:, tiles, cols], pa[g % 2][:, :, :], h_hi[:, tiles, cols].bitcast(F32),
                                       ALU.subtract).then_inc(pa_split, 1)
            barrier(pool, 5)

            def store_y(dst, r, m, e, i):
                pool.wait_ge(*((summed, START + m + 1) if r else (gated, START + m + 1)))
                pool.dma_start(dst[m], y_out[:, e]).then_inc(y_stored[e], 16)
                pool.wait_ge(y_stored[e], 16 * (KT // 2) * r + 16 * i + 16)
                pool.sem_inc(y_free[e], 1)

            for r, dst in enumerate((y_pool, merged)):
                with pool.Fori(0, KT // 2 - 1) as i:
                    for e in range(2):
                        store_y(dst, r, 2 * i + e, e, i)
                for e in range(2 - r):
                    store_y(dst, r, KT - 2 + e, e, KT // 2 - 1)
            barrier(pool, 6)

_INS = ["x", "c", "w_ada", "b_ada", "g_pre", "g_post", "w_in", "pool_w", "pool_scale", "gk_up_fwd", "gk_bias_fwd",
        "gk_up_bwd", "gk_bias_bwd", "gla_norm_g", "w_proj_pool", "w_proj_gla", "w_out"]


def kernel(**inputs):
    import numpy as _np
    import concourse.bacc as _bacc
    from concourse import mybir as _mybir
    from concourse.bass_utils import run_bass_kernel_spmd as _run

    nc = _bacc.Bacc("TRN2", target_bir_lowering=False, num_devices=1)
    arrays, args = {}, []
    for name in _INS:
        a = _np.ascontiguousarray(inputs[name])
        arrays[f"in_{name}"] = a
        args.append(nc.dram_tensor(f"in_{name}", a.shape, _mybir.dt.from_np(a.dtype), kind="ExternalInput").ap())
    out = nc.dram_tensor("out_0", (1, T, D), F32, kind="ExternalOutput").ap()
    build(nc, *args, out)
    r = _run(nc, [arrays], core_ids=[0])
    return r.results[0]["out_0"]
```
